# Optimizing a Trainium2 kernel written in Bass

```python
import jax, jax.numpy as jnp
from jax import lax
import numpy as np

D_MODEL = 1024
BATCH = 1
SEQ = 2048
DEPTH = 1
DEC_BATCH = 8
DEC_SEQ = 8
PAST_LEN = 2048
PAGE_SIZE = 128

HEAD_DIM = 64
N_HEADS = D_MODEL // HEAD_DIM
N_HEADS_A = N_HEADS // 2
N_HEADS_B = N_HEADS - N_HEADS_A
D_A = N_HEADS_A * HEAD_DIM
D_B = N_HEADS_B * HEAD_DIM
N_IN = 3 * D_A + 3 * D_B + N_HEADS_A
_SPLITS = (D_A, 2 * D_A, 3 * D_A, 3 * D_A + D_B, 3 * D_A + 2 * D_B, 3 * D_A + 3 * D_B)
ROPE_DIM = HEAD_DIM // 4
ROPE_THETA = 500000.0
D_FF = 4 * D_MODEL
DILATED_PAIRS = ((128, 1), (512, 4), (2048, 16))
WIN_MAX = 2048
MAX_DIL = 16
Q_BLOCK = 128
RMS_EPS = 1e-6
NEG_INF = -1e30
FORGET_BIAS = 8.0

kernel_name = 'hybrid_fox_dilated_decoder_step'

def _rmsnorm(x, g):
    xf = x.astype(jnp.float32)
    y = xf * lax.rsqrt(jnp.mean(xf * xf, axis=-1, keepdims=True) + RMS_EPS)
    return (y * g.astype(jnp.float32)).astype(x.dtype)

def _rope_partial(x, pos):
    half = ROPE_DIM // 2
    inv = ROPE_THETA ** (-jnp.arange(half, dtype=jnp.float32) / half)
    ang = pos.astype(jnp.float32)[:, None] * inv[None, :]
    cos = jnp.cos(ang)[:, None, :]
    sin = jnp.sin(ang)[:, None, :]
    xr = x[..., :ROPE_DIM].astype(jnp.float32)
    x1, x2 = xr[..., :half], xr[..., half:]
    rot = jnp.concatenate([x1 * cos - x2 * sin, x2 * cos + x1 * sin], axis=-1)
    return jnp.concatenate([rot.astype(x.dtype), x[..., ROPE_DIM:]], axis=-1)

def _project(h, pos, w_in, b_f, g_qa, g_ka, g_qb, g_kb):
    bn, t, _ = h.shape
    z = h @ w_in
    qa, ka, va, qb, kb, vb, fa = jnp.split(z, _SPLITS, axis=-1)
    qa = _rmsnorm(qa.reshape(bn, t, N_HEADS_A, HEAD_DIM), g_qa)
    ka = _rmsnorm(ka.reshape(bn, t, N_HEADS_A, HEAD_DIM), g_ka)
    va = va.reshape(bn, t, N_HEADS_A, HEAD_DIM)
    qb = _rope_partial(_rmsnorm(qb.reshape(bn, t, N_HEADS_B, HEAD_DIM), g_qb), pos)
    kb = _rope_partial(_rmsnorm(kb.reshape(bn, t, N_HEADS_B, HEAD_DIM), g_kb), pos)
    vb = vb.reshape(bn, t, N_HEADS_B, HEAD_DIM)
    logf = jax.nn.log_sigmoid(fa.astype(jnp.float32) + b_f.astype(jnp.float32))
    return qa, ka, va, logf, qb, kb, vb

def _fox_prompt(q, k, v, logf):
    bn, s_len = q.shape[:2]
    scale = HEAD_DIM ** -0.5
    c = jnp.cumsum(logf, axis=1)
    c_k = c.transpose(0, 2, 1)
    nb = s_len // Q_BLOCK
    qb = q.reshape(bn, nb, Q_BLOCK, N_HEADS_A, HEAD_DIM).transpose(1, 0, 2, 3, 4)
    cb = c.reshape(bn, nb, Q_BLOCK, N_HEADS_A).transpose(1, 0, 3, 2)
    kpos = jnp.arange(s_len)

    def block(args):
        i, qi, ci = args
        s = jnp.einsum('bqhd,bkhd->bhqk', qi, k, preferred_element_type=jnp.float32) * scale
        s = s + ci[..., :, None] - c_k[..., None, :]
        qpos = i * Q_BLOCK + jnp.arange(Q_BLOCK)
        s = jnp.where(kpos[None, :] <= qpos[:, None], s, NEG_INF)
        p = jax.nn.softmax(s, axis=-1)
        return jnp.einsum('bhqk,bkhd->bqhd', p, v.astype(jnp.float32))

    o = lax.map(block, (jnp.arange(nb), qb, cb))
    return o.transpose(1, 0, 2, 3, 4).reshape(bn, s_len, N_HEADS_A, HEAD_DIM)

def _fox_sample(q, k, v, logf, ck, cv, clogf, page_table):
    db, t = q.shape[:2]
    n_pages = page_table.shape[1]
    scale = HEAD_DIM ** -0.5
    cn = jnp.cumsum(logf, axis=1).transpose(0, 2, 1)
    causal = jnp.tril(jnp.ones((t, t), dtype=bool))
    s = jnp.einsum('bqhd,bkhd->bhqk', q, k, preferred_element_type=jnp.float32) * scale
    s = jnp.where(causal, s + cn[..., :, None] - cn[..., None, :], NEG_INF)
    m = s.max(-1)
    p = jnp.exp(s - m[..., None])
    l = p.sum(-1)
    acc = jnp.einsum('bhqk,bkhd->bhqd', p, v.astype(jnp.float32))
    lf = clogf[page_table].astype(jnp.float32).reshape(db, n_pages * PAGE_SIZE, N_HEADS_A)
    r = lax.cumsum(lf, axis=1, reverse=True) - lf
    r = r.reshape(db, n_pages, PAGE_SIZE, N_HEADS_A).transpose(1, 0, 3, 2)

    def step(carry, xs):
        m, l, acc = carry
        pages, r_pg = xs
        kp = ck[pages]
        vp = cv[pages]
        s = jnp.einsum('bqhd,bkhd->bhqk', q, kp, preferred_element_type=jnp.float32) * scale
        s = s + cn[..., :, None] + r_pg[..., None, :]
        m_new = jnp.maximum(m, s.max(-1))
        a = jnp.exp(m - m_new)
        p = jnp.exp(s - m_new[..., None])
        acc = acc * a[..., None] + jnp.einsum('bhqk,bkhd->bhqd', p, vp.astype(jnp.float32))
        return (m_new, l * a + p.sum(-1), acc), None

    (m, l, acc), _ = lax.scan(step, (m, l, acc), (page_table.T, r))
    return (acc / l[..., None]).transpose(0, 2, 1, 3)

def _combine(outs, lses):
    wts = jax.nn.softmax(jnp.stack(lses), axis=0)
    return jnp.sum(wts[..., None] * jnp.stack(outs), axis=0)

def _dilated_prompt(q, k, v):
    bn, s_len = q.shape[:2]
    scale = HEAD_DIM ** -0.5
    mult = MAX_DIL * Q_BLOCK
    s_pad = -(-s_len // mult) * mult
    padw = ((0, 0), (0, s_pad - s_len), (0, 0), (0, 0))
    qp, kp, vp = jnp.pad(q, padw), jnp.pad(k, padw), jnp.pad(v, padw)
    qi = jnp.arange(Q_BLOCK)[:, None]
    ki = jnp.arange(2 * Q_BLOCK)[None, :]
    dist = Q_BLOCK + qi - ki
    outs, lses = [], []
    for (w, d) in DILATED_PAIRS:
        steps = w // d
        sub = s_pad // d
        nb = sub // Q_BLOCK

        def to_res(x):
            return x.reshape(bn, sub, d, N_HEADS_B, HEAD_DIM).transpose(0, 2, 1, 3, 4).reshape(
                bn, d, nb, Q_BLOCK, N_HEADS_B, HEAD_DIM)

        qr, kr, vr = to_res(qp), to_res(kp), to_res(vp)
        shift = ((0, 0), (0, 0), (1, 0), (0, 0), (0, 0), (0, 0))
        kcat = jnp.concatenate([jnp.pad(kr, shift)[:, :, :-1], kr], axis=3)
        vcat = jnp.concatenate([jnp.pad(vr, shift)[:, :, :-1], vr], axis=3)
        blk = jnp.arange(nb)[:, None, None]
        valid = (dist >= 0)[None] & (dist <= steps)[None] & ((blk * Q_BLOCK + ki[None] - Q_BLOCK) >= 0)
        s = jnp.einsum('brnqhd,brnkhd->brnhqk', qr, kcat, preferred_element_type=jnp.float32) * scale
        s = jnp.where(valid[None, None, :, None], s, NEG_INF)
        m = s.max(-1)
        p = jnp.exp(s - m[..., None])
        l = p.sum(-1)
        o = jnp.einsum('brnhqk,brnkhd->brnqhd', p, vcat.astype(jnp.float32))
        o = o / l.transpose(0, 1, 2, 4, 3)[..., None]
        lse = (m + jnp.log(l)).transpose(0, 1, 2, 4, 3)
        o = o.reshape(bn, d, sub, N_HEADS_B, HEAD_DIM).transpose(0, 2, 1, 3, 4).reshape(
            bn, s_pad, N_HEADS_B, HEAD_DIM)
        lse = lse.reshape(bn, d, sub, N_HEADS_B).transpose(0, 2, 1, 3).reshape(bn, s_pad, N_HEADS_B)
        outs.append(o[:, :s_len])
        lses.append(lse[:, :s_len])
    return _combine(outs, lses)

def _dilated_sample(q, k, v, buf_k, buf_v):
    t = q.shape[1]
    wb = buf_k.shape[1]
    scale = HEAD_DIM ** -0.5
    ext_k = jnp.concatenate([buf_k, k.astype(buf_k.dtype)], axis=1)
    ext_v = jnp.concatenate([buf_v, v.astype(buf_v.dtype)], axis=1)
    outs, lses = [], []
    for (w, d) in DILATED_PAIRS:
        steps = w // d
        idx = wb + jnp.arange(t)[:, None] - d * jnp.arange(steps + 1)[None, :]
        valid = idx >= 0
        idx = jnp.maximum(idx, 0)
        kg = ext_k[:, idx]
        vg = ext_v[:, idx]
        s = jnp.einsum('bqhd,bqjhd->bqhj', q, kg, preferred_element_type=jnp.float32) * scale
        s = jnp.where(valid[None, :, None, :], s, NEG_INF)
        m = s.max(-1)
        p = jnp.exp(s - m[..., None])
        l = p.sum(-1)
        o = jnp.einsum('bqhj,bqjhd->bqhd', p, vg.astype(jnp.float32)) / l[..., None]
        outs.append(o)
        lses.append(m + jnp.log(l))
    return _combine(outs, lses), ext_k[:, -wb:], ext_v[:, -wb:]

def _finish(x, oa, ob, w_o, g_mlp, w_up, w_down):
    bn, t = x.shape[:2]
    o = jnp.concatenate([oa.reshape(bn, t, D_A), ob.reshape(bn, t, D_B)], axis=-1).astype(x.dtype)
    x = x + o @ w_o
    u = jax.nn.relu(_rmsnorm(x, g_mlp) @ w_up)
    return x + (u * u) @ w_down

def setup_inputs(seed: int = 0) -> dict:
    key = jax.random.key(seed)
    ks = jax.random.split(key, 20)
    n_pages = PAST_LEN // PAGE_SIZE
    n_used = DEC_BATCH * n_pages
    n_pool = n_used + n_used // 4
    wb = min(WIN_MAX, PAST_LEN)
    nrm = jax.random.normal
    f32 = jnp.float32
    return {
        'x_prompt': nrm(ks[0], (BATCH, SEQ, D_MODEL), f32),
        'x_sample': nrm(ks[1], (DEC_BATCH, DEC_SEQ, D_MODEL), f32),
        'cache_k': nrm(ks[2], (DEPTH, n_pool, PAGE_SIZE, N_HEADS_A, HEAD_DIM), f32),
        'cache_v': nrm(ks[3], (DEPTH, n_pool, PAGE_SIZE, N_HEADS_A, HEAD_DIM), f32),
        'cache_logf': jax.nn.log_sigmoid(FORGET_BIAS + 0.5 * nrm(ks[4], (DEPTH, n_pool, PAGE_SIZE, N_HEADS_A), f32)),
        'state_win_k': nrm(ks[5], (DEPTH, DEC_BATCH, wb, N_HEADS_B, HEAD_DIM), f32),
        'state_win_v': nrm(ks[6], (DEPTH, DEC_BATCH, wb, N_HEADS_B, HEAD_DIM), f32),
        'page_table': jax.random.permutation(ks[7], n_pool)[:n_used].reshape(DEC_BATCH, n_pages).astype(jnp.int32),
        'g_attn': 1.0 + 0.02 * nrm(ks[8], (DEPTH, D_MODEL), f32),
        'w_in': nrm(ks[9], (DEPTH, D_MODEL, N_IN), f32) * D_MODEL ** -0.5,
        'b_f': FORGET_BIAS + 0.1 * nrm(ks[10], (DEPTH, N_HEADS_A), f32),
        'g_qa': 1.0 + 0.02 * nrm(ks[11], (DEPTH, HEAD_DIM), f32),
        'g_ka': 1.0 + 0.02 * nrm(ks[12], (DEPTH, HEAD_DIM), f32),
        'g_qb': 1.0 + 0.02 * nrm(ks[13], (DEPTH, HEAD_DIM), f32),
        'g_kb': 1.0 + 0.02 * nrm(ks[14], (DEPTH, HEAD_DIM), f32),
        'w_o': nrm(ks[15], (DEPTH, D_MODEL, D_MODEL), f32) * D_MODEL ** -0.5,
        'g_mlp': 1.0 + 0.02 * nrm(ks[16], (DEPTH, D_MODEL), f32),
        'w_up': nrm(ks[17], (DEPTH, D_MODEL, D_FF), f32) * D_MODEL ** -0.5,
        'w_down': nrm(ks[18], (DEPTH, D_FF, D_MODEL), f32) * D_FF ** -0.5,
    }

def reference(x_prompt, x_sample, cache_k, cache_v, cache_logf, state_win_k, state_win_v, page_table,
              g_attn, w_in, b_f, g_qa, g_ka, g_qb, g_kb, w_o, g_mlp, w_up, w_down):
    s_len = x_prompt.shape[1]
    t = x_sample.shape[1]
    past_len = page_table.shape[1] * PAGE_SIZE
    pos_p = jnp.arange(s_len)
    pos_s = past_len + jnp.arange(t)
    wbp = min(WIN_MAX, s_len)
    xp, xs = x_prompt, x_sample
    kp_l, vp_l, fp_l, wkp_l, wvp_l = [], [], [], [], []
    ks_l, vs_l, fs_l, wks_l, wvs_l = [], [], [], [], []
    for layer in range(DEPTH):
        qa, ka, va, lf, qb, kb, vb = _project(_rmsnorm(xp, g_attn[layer]), pos_p, w_in[layer], b_f[layer],
                                              g_qa[layer], g_ka[layer], g_qb[layer], g_kb[layer])
        oa = _fox_prompt(qa, ka, va, lf)
        ob = _dilated_prompt(qb, kb, vb)
        xp = _finish(xp, oa, ob, w_o[layer], g_mlp[layer], w_up[layer], w_down[layer])
        kp_l.append(ka)
        vp_l.append(va)
        fp_l.append(lf)
        wkp_l.append(kb[:, s_len - wbp:])
        wvp_l.append(vb[:, s_len - wbp:])
        qa, ka, va, lf, qb, kb, vb = _project(_rmsnorm(xs, g_attn[layer]), pos_s, w_in[layer], b_f[layer],
                                              g_qa[layer], g_ka[layer], g_qb[layer], g_kb[layer])
        oa = _fox_sample(qa, ka, va, lf, cache_k[layer], cache_v[layer], cache_logf[layer], page_table)
        ob, nwk, nwv = _dilated_sample(qb, kb, vb, state_win_k[layer], state_win_v[layer])
        xs = _finish(xs, oa, ob, w_o[layer], g_mlp[layer], w_up[layer], w_down[layer])
        ks_l.append(ka)
        vs_l.append(va)
        fs_l.append(lf)
        wks_l.append(nwk)
        wvs_l.append(nwv)
    return (xp, xs,
            jnp.stack(kp_l), jnp.stack(vp_l), jnp.stack(fp_l), jnp.stack(wkp_l), jnp.stack(wvp_l),
            jnp.stack(ks_l), jnp.stack(vs_l), jnp.stack(fs_l), jnp.stack(wks_l), jnp.stack(wvs_l))


_drawn_inputs = setup_inputs


def setup_inputs(seed=0):
    import zlib

    import numpy as np

    out = dict(_drawn_inputs(seed))
    spreads = {}
    factors = {'cache_logf': 8.0,
     'g_attn': 2.923,
     'g_qa': 8.0,
     'g_ka': 3.126,
     'g_qb': 8.0,
     'g_kb': 2.927,
     'g_mlp': 3.181}
    for name, (base, spread) in spreads.items():
        noise = np.random.default_rng([zlib.crc32(name.encode()), seed]).standard_normal(out[name].shape)
        drawn = base * np.exp(spread * noise) if base else spread * noise
        out[name] = __import__('jax').numpy.asarray(drawn.astype(out[name].dtype))
    for name, factor in factors.items():
        out[name] = (out[name] * factor).astype(out[name].dtype)
    return out
```

```python
from contextlib import ExitStack

import numpy as np

import concourse.bass as bass
from concourse import mybir

F32 = mybir.dt.float32
F32R = mybir.dt.float32r
I32 = mybir.dt.int32
ALU = mybir.AluOpType
ACT = mybir.ActivationFunctionType
AX_X = mybir.AxisListType.X
ds = bass.ds

P = 128
D_MODEL = 1024
SEQ = 2048
DEC_BATCH = 8
DEC_SEQ = 8
PAST = 2048
PAGE = 128
HD = 64
HEADS = 8
D_G = HEADS * HD
D_FF = 4 * D_MODEL
KC = D_MODEL // P
TILES = SEQ // P
N_TILES = TILES + 1
ROWS = N_TILES * P
N_SAMPLE = DEC_BATCH * DEC_SEQ
N_FA = HEADS
EPS = 1e-6
NEG = -1e30
FBLK = 256


class Phase:

    def __init__(self, nc, name):
        self.nc, self.name, self.ctx, self.held = nc, name, ExitStack(), []

    def __enter__(self):
        return self

    def __exit__(self, *said):
        ended = self.ctx.__exit__(*said)
        if self.held and said[0] is None:
            self.nc.clear_and_free_semaphores(self.held)
            self.nc.all_engine_barrier()
        return ended

    def sb(self, name, shape, dt=F32):
        return self.ctx.enter_context(self.nc.sbuf_tensor(f"{self.name}_{name}", shape, dt))

    def ps(self, name, shape, dt=F32):
        return self.ctx.enter_context(self.nc.psum_tensor(f"{self.name}_{name}", shape, dt))

    def sem(self, name):
        self.held.append(self.nc.alloc_semaphore(f"{self.name}_{name}"))
        return self.held[-1]

    def sems(self, name, n=2):
        return [self.sem(f"{name}{i}") for i in range(n)]

    def block(self):
        return self.ctx.enter_context(self.nc.Block())


def load_constants(nc, c, dram):
    with Phase(nc, "const") as ph:
        loaded = ph.sem("loaded")
        block = ph.block()

        @block.sync
        def _(sp):
            pairs = [(c["ident"][:, :], dram["ident"]), (c["mask"][:, :], dram["mask"])]
            for dst, src in pairs:
                sp.dma_start(dst, src).then_inc(loaded, 16)
            sp.wait_ge(loaded, 16 * len(pairs))


PASS_COLS = 2 * D_G
W_COLS = PASS_COLS + N_FA


def project(nc, c, dram):
    w_in = dram["w_in"]
    pieces = [[(0, 0, PASS_COLS)],
              [(0, 3 * D_G, PASS_COLS)],
              [(0, 2 * D_G, D_G), (D_G, 5 * D_G, D_G + N_FA)]]
    dests = [(dram["q_a"], dram["k_a"]), (dram["q_b"], dram["k_b"]), (dram["v_a"], dram["v_b"])]
    PAIRS = TILES // 2

    with Phase(nc, "proj") as ph:
        w_raw = ph.sb("w_raw", [P, 2, W_COLS])
        w_hi = ph.sb("w_hi", [P, 2, KC * W_COLS], F32R)
        w_lo = ph.sb("w_lo", [P, 2, KC * W_COLS], F32R)
        x_in = ph.sb("x_in", [P, 2, D_MODEL])
        xg = ph.sb("xg", [P, D_MODEL])
        x_hi = ph.sb("x_hi", [P, 2, D_MODEL], F32R)
        x_lo = ph.sb("x_lo", [P, 2, D_MODEL], F32R)
        z = ph.sb("z", [P, 2, PASS_COLS])
        sq = ph.sb("sq", [P, PASS_COLS])
        junk = ph.sb("junk", [P, D_MODEL])
        gains = ph.sb("gains", [P, 2, 2, HD])
        g_attn = ph.sb("g_attn", [P, KC])
        b_f = ph.sb("b_f", [P, N_FA])
        rope = ph.sb("rope", [P, 2, N_TILES, 16])
        turn = ph.sb("turn", [P, 2, 16, 16])
        sums = ph.sb("sums", [P, N_TILES])
        mean = ph.sb("mean", [P, N_TILES])
        rstd = ph.sb("rstd", [P, N_TILES])
        head_sum = ph.sb("head_sum", [P, 16])
        head_mean = ph.sb("head_mean", [P, 16])
        head_rstd = ph.sb("head_rstd", [P, 16])
        minus_half = ph.sb("minus_half", [P, 16])
        fa = ph.sb("fa", [P, N_TILES * N_FA])
        lf_t = ph.sb("lf_t", [P, 5, N_TILES * N_FA])
        t_ps = [ph.ps(f"t{j}", [P, D_MODEL]) for j in range(2)]
        z_ps = [ph.ps(f"z{j}", [P, PASS_COLS]) for j in range(2)]

        consts = ph.sem("consts")
        pool_set = ph.sem("pool_set")
        w_loaded = ph.sems("w_loaded")
        w_hi_done = ph.sem("w_hi_done")
        w_split = ph.sem("w_split")
        x_loaded = ph.sems("x_loaded")
        x_turned = ph.sem("x_turned")
        squared = ph.sem("squared")
        mean_done = ph.sem("mean_done")
        rstd_done = ph.sem("rstd_done")
        xg_done = ph.sem("xg_done")
        hi_done = ph.sem("hi_done")
        lo_done = ph.sem("lo_done")
        product = ph.sem("product")
        z_out = ph.sem("z_out")
        fa_out = ph.sem("fa_out")
        sq_z = ph.sem("sq_z")
        hsum = ph.sem("hsum")
        hmean = ph.sem("hmean")
        hrstd = ph.sem("hrstd")
        z_normed = ph.sem("z_normed")
        z_gained = ph.sem("z_gained")
        turned = ph.sem("turned")
        z_final = ph.sem("z_final")
        z_sent = ph.sems("z_sent")
        lf = ph.sem("lf")
        lf_exp = ph.sem("lf_exp")
        lf_sent = ph.sem("lf_sent")
        block = ph.block()

        def at(p, i, j):
            k = N_TILES * p + j
            return k + 2 * i, k % 2, k // 2 + i

        def w_slot(p, k):
            return k % 2 if p == 0 else 0

        def w_arrived(eng, p, k):
            if p == 0:
                eng.wait_ge(w_loaded[k % 2], 16 * (k // 2 + 1))
            elif p == 1:
                eng.wait_ge(w_loaded[0], 16 * (KC // 2 + 1 + k))
            else:
                eng.wait_ge(w_loaded[0], 16 * (KC // 2 + KC + 2 + 2 * k))

        def w_part(w, p, k):
            return w[:, p % 2, ds(k * W_COLS, W_COLS if p == 2 else PASS_COLS)]

        @block.sync
        def _(sp):
            def load_w(p, k):
                for d0, s0, n in pieces[p]:
                    sp.dma_start(w_raw[:, w_slot(p, k), d0:d0 + n], w_in[ds(k * P, P), s0:s0 + n])\
                        .then_inc(w_loaded[w_slot(p, k)], 16)

            def load_x(t, p, i, j):
                n, slot, _use = at(p, i, j)
                sp.wait_ge(x_turned, n + 1)
                if p == 0:
                    sp.wait_ge(squared, n + 1)
                elif p == 1:
                    sp.wait_ge(squared, N_TILES + 2)
                sp.dma_start(x_in[:, slot, :], dram["x"][ds(t * P, P), :]).then_inc(x_loaded[slot], 16)

            sp.sem_inc(x_turned, 2)
            sp.sem_inc(squared, 2)
            for slot in range(2):
                sp.sem_inc(z_sent[slot], 32)
            load_x(0, 0, 0, 0)
            load_w(0, 0)
            load_w(0, 1)
            sp.dma_start(g_attn[:, :], dram["g_attn"]).then_inc(consts, 16)
            sp.dma_start(b_f[:, :], dram["b_f"].partition_broadcast(P)).then_inc(consts, 16)
            for n, name in enumerate(("g_qa", "g_ka", "g_qb", "g_kb")):
                sp.dma_start(gains[:, n // 2, n % 2, :],
                             dram[name].partition_broadcast(P)).then_inc(consts, 16)
            for n, name in enumerate(("rope_cos", "rope_sin")):
                sp.dma_start(rope[:, n, :, :],
                             dram[name].rearrange("(t p) d -> p t d", p=P)).then_inc(consts, 16)
            for k in range(2, KC):
                sp.wait_ge(w_split, k - 1)
                load_w(0, k)
            load_x(1, 0, 0, 1)
            for p in range(3):
                with sp.Fori(0, PAIRS - 1) as i:
                    if p < 2:
                        sp.wait_ge(w_split, KC * (p + 1) + i)
                        load_w(p + 1, i)
                    for j in range(2):
                        load_x(2 * i + j + 2, p, i, j + 2)
                if p < 2:
                    sp.wait_ge(w_split, KC * (p + 1) + PAIRS - 1)
                    load_w(p + 1, PAIRS - 1)
                load_x(TILES, p, PAIRS, 0)
                if p < 2:
                    load_x(0, p, PAIRS, 1)
                    load_x(1, p, PAIRS, 2)
            sp.wait_ge(lf, 15)
            sp.dma_start(dram["logf"].rearrange("(t p) h -> p t h", p=P),
                         c["logf"][:, :].rearrange("p (t h) -> p t h", h=HEADS)).then_inc(lf_sent, 16)
            sp.wait_ge(lf_sent, 16)

        @block.scalar
        def _(act):
            def hi_w(p, k):
                w_arrived(act, p, k)
                act.activation(w_part(w_hi, p, k), w_raw[:, w_slot(p, k), 0:W_COLS if p == 2 else PASS_COLS],
                               ACT.Copy).then_inc(w_hi_done, 1)

            def hi_x(p, i, j):
                n, slot, use = at(p, i, j)
                if p == 0:
                    act.wait_ge(x_loaded[slot], 16 * (use + 1))
                    act.wait_ge(squared, n + 2)
                    act.activation(junk[:, :], x_in[:, slot, :], ACT.Square,
                                   accum_out=sums[:, ds(2 * i + j, 1)]).then_inc(squared, 1)
                act.wait_ge(xg_done, 2 * (n + 1))
                act.wait_ge(product, n + 1)
                act.activation(x_hi[:, slot, :], xg[:, :], ACT.Copy).then_inc(hi_done, 1)

            def scale(p, i, j):
                n, slot, use = at(p, i, j)
                if p == 0:
                    act.wait_ge(rstd_done, n + 1)
                act.wait_ge(product, n + 3)
                act.wait_ge(z_sent[slot], 32 * (use + 1))
                for q in range(2):
                    act.activation(z[:, slot, q * D_G:(q + 1) * D_G], z_ps[slot][:, q * D_G:(q + 1) * D_G],
                                   ACT.Copy, scale=rstd[:, ds(2 * i + j, 1)]).then_inc(z_out, 1)

            def store(p, i, j):
                n, slot, _use = at(p, i, j)
                act.wait_ge(z_final if p < 2 else z_out, n + 1 if p < 2 else 4 + 2 * (n + 1))
                for q in range(2):
                    act.dma_start(dests[p][q][ds((2 * i + j) * P, P), :],
                                 z[:, slot, q * D_G:(q + 1) * D_G]).then_inc(z_sent[slot], 16)

            act.sem_inc(z_out, 4)
            for k in range(KC):
                hi_w(0, k)
            hi_x(0, 0, 0)
            def step(p, i, j, last=False):
                if not last:
                    hi_x(p, i, j + 1)
                elif p < 2:
                    hi_next(p)
                scale(p, i, j)
                if not (isinstance(i, int) and 2 * i + j == 0):
                    store(p, i, j - 1)
                elif p > 0:
                    store(p - 1, PAIRS, 0)

            def hi_next(p):
                n, slot, _use = at(p, PAIRS, 1)
                act.wait_ge(xg_done, 2 * (n + 1))
                act.wait_ge(product, n + 1)
                act.activation(x_hi[:, slot, :], xg[:, :], ACT.Copy).then_inc(hi_done, 1)

            for p in range(3):
                step(p, 0, 0)
                with act.Fori(0, PAIRS - 1) as i:
                    if p < 2:
                        hi_w(p + 1, i)
                    for j in (1, 2):
                        step(p, i, j)
                if p < 2:
                    hi_w(p + 1, PAIRS - 1)
                step(p, PAIRS - 1, 1)
                step(p, PAIRS, 0, last=True)
            store(2, PAIRS, 0)
            uses = 3 * N_TILES
            act.wait_ge(z_sent[0], 32 + 32 * ((uses + 1) // 2))
            act.wait_ge(z_sent[1], 32 + 32 * (uses // 2))
            act.wait_ge(lf, 2)
            act.activation(lf_t[:, 1, :], lf_t[:, 0, :], ACT.Exp).then_inc(lf_exp, 1)

        @block.gpsimd
        def _(pool):
            pool.sem_inc(lo_done, 1)
            pool.memset(minus_half[:, :], -0.5).then_inc(pool_set, 1)
            pool.wait_ge(consts, 16 * 8)
            for g in range(2):
                pool.tensor_scalar(gains[:, g, 0, :], gains[:, g, 0, :], HD ** -0.5, None,
                                   ALU.mult).then_inc(pool_set, 1)
            pool.wait_ge(pool_set, 3)

            def lo_x(p, i, j):
                n, slot, _use = at(p, i, j)
                if p == 0:
                    pool.wait_ge(mean_done, n + 1)
                    pool.tensor_tensor(rstd[:, ds(2 * i + j, 1)], mean[:, ds(2 * i + j, 1)],
                                       minus_half[:, 0:1], ALU.pow).then_inc(rstd_done, 1)
                pool.wait_ge(hi_done, n + 1)
                pool.tensor_tensor(x_lo[:, slot, :], xg[:, :], x_hi[:, slot, :].bitcast(F32),
                                   ALU.subtract).then_inc(lo_done, 1)

            def norm(p, i, j):
                n, slot, _use = at(p, i, j)
                zs = z[:, slot, :]
                pool.wait_ge(z_out, 4 + 2 * (n + 1))
                pool.tensor_tensor(sq[:, :], zs, zs, ALU.mult).then_inc(sq_z, 1)
                pool.wait_ge(hmean, n + 1)
                pool.tensor_tensor(head_rstd[:, :], head_mean[:, :], minus_half[:, :],
                                   ALU.pow).then_inc(hrstd, 1)
                pool.wait_ge(z_normed, n + 1)
                for q in range(2):
                    part = zs[:, q * D_G:(q + 1) * D_G].rearrange("p (h d) -> p h d", d=HD)
                    last = q == 1 and p == 0
                    op = pool.tensor_tensor(part, part, gains[:, p, q:q + 1, :].to_broadcast([P, HEADS, HD]),
                                            ALU.mult)
                    op.then_inc(z_final if last else z_gained, 1)
                if p == 0:
                    return
                m = n - N_TILES
                pool.wait_ge(z_gained, N_TILES + 2 * (m + 1))
                zh = zs.rearrange("p (h d) -> p h d", d=HD)

                def table(a, d0, d1):
                    return rope[:, a, ds(2 * i + j, 1), d0:d1].to_broadcast([P, 16, d1 - d0])

                pool.tensor_tensor(turn[:, 0, :, :], zh[:, :, 0:16], table(0, 0, 16), ALU.mult).then_inc(turned, 1)
                pool.tensor_tensor(turn[:, 1, :, 0:8], zh[:, :, 8:16], table(1, 0, 8), ALU.mult).then_inc(turned, 1)
                pool.tensor_tensor(turn[:, 1, :, 8:16], zh[:, :, 0:8], table(1, 8, 16), ALU.mult)\
                    .then_inc(turned, 1)
                pool.wait_ge(turned, 3 * (m + 1))
                pool.tensor_tensor(zh[:, :, 0:16], turn[:, 0, :, :], turn[:, 1, :, :], ALU.add)\
                    .then_inc(z_final, 1)

            lo_x(0, 0, 0)
            for p in range(3):
                with pool.Fori(0, PAIRS) as i:
                    for j in range(2):
                        lo_x(p, i, j + 1)
                        if p < 2:
                            norm(p, i, j)
                if p < 2:
                    n, slot, _use = at(p, PAIRS, 1)
                    pool.wait_ge(hi_done, n + 1)
                    pool.tensor_tensor(x_lo[:, slot, :], xg[:, :], x_hi[:, slot, :].bitcast(F32),
                                       ALU.subtract).then_inc(lo_done, 1)
                    norm(p, PAIRS, 0)

        @block.vector
        def _(dve):
            def lo_w(p, k):
                dve.wait_ge(w_hi_done, KC * p + k + 1)
                dve.tensor_tensor(w_part(w_lo, p, k), w_raw[:, w_slot(p, k), 0:W_COLS if p == 2 else PASS_COLS],
                                  w_part(w_hi, p, k).bitcast(F32), ALU.subtract).then_inc(w_split, 1)

            def gain_x(p, i, j):
                n, slot, _use = at(p, i, j)
                dve.wait_ge(x_turned, n + 3)
                dve.wait_ge(lo_done, n + 1)
                for q in range(2):
                    dve.tensor_tensor(xg[:, q * 512:(q + 1) * 512].rearrange("p (k m) -> p k m", m=P),
                                      t_ps[slot][:, q * 512:(q + 1) * 512].rearrange("p (k m) -> p k m", m=P),
                                      g_attn[:, 4 * q:4 * q + 4].unsqueeze(2).to_broadcast([P, 4, P]),
                                      ALU.mult).then_inc(xg_done, 1)

            def mean_x(p, i, j):
                if p > 0:
                    return
                n, _slot, _use = at(p, i, j)
                dve.wait_ge(squared, n + 3)
                dve.tensor_scalar(mean[:, ds(2 * i + j, 1)], sums[:, ds(2 * i + j, 1)], 1.0 / D_MODEL, EPS,
                                  ALU.mult, ALU.add).then_inc(mean_done, 1)

            def heads(p, i, j):
                n, slot, _use = at(p, i, j)
                if p == 2:
                    dve.wait_ge(product, n + 3)
                    dve.scalar_tensor_tensor(fa[:, ds((2 * i + j) * N_FA, N_FA)], t_ps[slot][:, 0:N_FA],
                                             rstd[:, ds(2 * i + j, 1)], b_f[:, :], ALU.mult, ALU.add)\
                        .then_inc(fa_out, 1)
                    return
                dve.wait_ge(sq_z, n + 1)
                dve.tensor_reduce(head_sum[:, :], sq[:, :].rearrange("p (h d) -> p h d", d=HD),
                                  AX_X, ALU.add).then_inc(hsum, 1)
                dve.wait_ge(hsum, n + 1)
                dve.tensor_scalar(head_mean[:, :], head_sum[:, :], 1.0 / HD, EPS, ALU.mult, ALU.add)\
                    .then_inc(hmean, 1)
                dve.wait_ge(hrstd, n + 1)
                zh = z[:, slot, :].rearrange("p (h d) -> p h d", d=HD)
                dve.tensor_tensor(zh, zh, head_rstd[:, :].unsqueeze(2).to_broadcast([P, 16, HD]), ALU.mult)\
                    .then_inc(z_normed, 1)

            dve.sem_inc(fa_out, 2)
            dve.wait_ge(consts, 16 * 8)
            for k in range(KC):
                lo_w(0, k)
            gain_x(0, 0, 0)
            mean_x(0, 0, 0)
            for p in range(3):
                with dve.Fori(0, PAIRS) as i:
                    for j in range(2):
                        gain_x(p, i, j + 1)
                        mean_x(p, i, j + 1)
                        heads(p, i, j)
                    if p < 2:
                        lo_w(p + 1, i)
                if p < 2:
                    gain_x(p, PAIRS, 1)
                heads(p, PAIRS, 0)

            step = [0]

            def chain(op):
                op.then_inc(lf, 1)
                step[0] += 1
                dve.wait_ge(lf, step[0])

            t = [lf_t[:, a, :] for a in range(5)]
            dve.wait_ge(fa_out, 2 + N_TILES)
            chain(dve.tensor_scalar(t[2], fa[:, :], -1.0, None, ALU.mult))
            chain(dve.tensor_tensor(t[0], fa[:, :], t[2], ALU.min))
            dve.wait_ge(lf_exp, 1)
            chain(dve.tensor_scalar(t[2], t[1], 2.0, None, ALU.add))
            chain(dve.reciprocal(t[3], t[2]))
            chain(dve.tensor_tensor(t[2], t[1], t[3], ALU.mult))
            chain(dve.tensor_tensor(t[3], t[2], t[2], ALU.mult))
            chain(dve.tensor_scalar(t[4], t[3], 2.0 / 15, None, ALU.mult))
            for k in (13, 11, 9, 7, 5, 3):
                chain(dve.scalar_tensor_tensor(t[4], t[4], 2.0 / k, t[3], ALU.add, ALU.mult))
            chain(dve.scalar_tensor_tensor(t[4], t[4], 2.0, t[2], ALU.add, ALU.mult))
            chain(dve.scalar_tensor_tensor(c["logf"][:, :], fa[:, :], 0.0, t[4], ALU.min, ALU.subtract))

        @block.tensor
        def _(pe):
            def turn_x(p, i, j):
                n, slot, use = at(p, i, j)
                pe.wait_ge(x_loaded[slot], 16 * (use + 1))
                if isinstance(n, int) and n < 2:
                    pass
                elif p == 2:
                    pe.wait_ge(fa_out, n - 2 * N_TILES + 1)
                for k in range(KC):
                    mm = pe.transpose(t_ps[slot][:, k * P:(k + 1) * P], x_in[:, slot, k * P:(k + 1) * P],
                                      c["ident"][:, :])
                mm.then_inc(x_turned, 1)

            def products(p, i, j):
                n, slot, _use = at(p, i, j)
                pe.wait_ge(hi_done, n + 1)
                pe.wait_ge(lo_done, n + 2)
                pe.wait_ge(z_out, 2 * (n + 1))
                halves = [(z_ps[slot][:, q * D_G:(q + 1) * D_G], q * D_G, D_G) for q in range(2)]
                if p == 2:
                    halves.append((t_ps[slot][:, 0:N_FA], PASS_COLS, N_FA))
                for out, w0, cols in halves:
                    for k in range(KC):
                        xs = slice(k * P, (k + 1) * P)
                        ws = slice(k * W_COLS + w0, k * W_COLS + w0 + cols)
                        pe.matmul(out, x_hi[:, slot, xs], w_hi[:, p % 2, ws], start=(k == 0), stop=False)
                        pe.matmul(out, x_hi[:, slot, xs], w_lo[:, p % 2, ws], start=False, stop=False)
                        mm = pe.matmul(out, x_lo[:, slot, xs], w_hi[:, p % 2, ws], start=False,
                                       stop=(k == KC - 1))
                mm.then_inc(product, 1)

            pe.sem_inc(product, 2)
            turn_x(0, 0, 0)
            for p in range(3):
                pe.wait_ge(w_split, KC * (p + 1))
                with pe.Fori(0, PAIRS) as i:
                    for j in range(2):
                        turn_x(p, i, j + 1)
                        products(p, i, j)
                if p < 2:
                    turn_x(p, PAIRS, 1)
                products(p, PAIRS, 0)


PT_BANKS = 3
PT_SLOTS = 4
O_SLOTS = 2
S_COLS = 2048
HEAD_GROUPS = 2 * TILES // 4


class Count:

    def __init__(self, sem, n):
        self.sem, self.n = sem, n

    def start(self, eng):
        eng.sem_inc(self.sem, 2 * self.n)

    def wait(self, eng, h, k):
        eng.wait_ge(self.sem, self.n * h + 2 * self.n + k + 1)


def last_user(used, k):
    for back in range(1, len(used) + 1):
        if used[(k - back) % len(used)] & used[k]:
            return k - back
    raise ValueError("nothing used it")


def forgetting_steps():
    steps = []
    for i in range(TILES):
        w = (i + 1) * P
        off = (i % 2) * (S_COLS // 2) if w <= S_COLS // 2 else 0
        steps.append([dict(q0=i * P, d=1, k0=0, w=w, s=off, p=(i % 2) * S_COLS, v=list(range(i + 1)), o=i)])
    return steps


def dilated_units():
    units, base = [], 0
    for d in (1, 4, 16):
        nb = SEQ // d // P
        for r in range(d):
            for n in range(nb):
                at = base + r * nb + n
                q0 = n * P * d + r
                if n:
                    units.append(dict(q0=q0, d=d, k0=q0 - P * d, w=2 * P, v=[at - 1, at], o=at))
                else:
                    units.append(dict(q0=q0, d=d, k0=q0, w=P, v=[at], o=at))
        base += TILES
    return units


def dilated_steps():
    units = dilated_units()
    steps = []
    for w in (P, 2 * P):
        kind = [u for u in units if u["w"] == w]
        steps += [kind[k:k + 2] for k in range(0, len(kind), 2)]
    for s, step in enumerate(steps):
        for k, u in enumerate(step):
            u["s"] = (s % 4) * 512 + k * u["w"]
            u["p"] = (s % 4) * 512 + k * u["w"]
    return steps


def attend(nc, c, dram, dilated):
    steps = dilated_steps() if dilated else forgetting_steps()
    branches = 3 if dilated else 1
    NS = len(steps)
    row = HD + 2 if dilated else HD
    names = ("q_b", "k_b", "v_b") if dilated else ("q_a", "k_a", "v_a")

    groups = []
    first_group, last_group = [], []
    for s, step in enumerate(steps):
        blocks = [(u, b) for u in range(len(step)) for b in range(step[u]["w"] // P)]
        first_group.append(len(groups))
        groups += [(s, blocks[k:k + 4]) for k in range(0, len(blocks), 4)]
        last_group.append(len(groups) - 1)
    NG = len(groups)
    copier = [k % 2 for k in range(HEAD_GROUPS)]
    for s in range(NS):
        n = last_group[s] - first_group[s] + 1
        copier += [0 if k < (n + 1) // 2 else 1 for k in range(n)]
    copied_at = [copier[:k].count(copier[k]) for k in range(len(copier))]
    NB = len(copier)

    s_used = [{x // 512 for u in step for x in range(u["s"], u["s"] + u["w"], P)} for step in steps]
    p_used = [{x // P for u in step for x in range(u["p"], u["p"] + u["w"], P)} for step in steps]
    m_used = [{s % 4} for s in range(NS)]
    t_used = [{b % PT_BANKS} for b in range(NB)]
    pT_used = [{g % PT_SLOTS} for g in range(NG)]
    o_used = [{0} for s in range(NS)]

    with Phase(nc, "dil" if dilated else "fox") as ph:
        q_in = ph.sb("q_in", [P, 2, TILES, P])
        k_in = ph.sb("k_in", [P, 2, TILES, P])
        v_in = ph.sb("v_in", [P, 2, branches * TILES, P])
        qT = ph.sb("qT", [P, 2, SEQ])
        kT = ph.sb("kT", [P, 2, SEQ])
        p_sb = ph.sb("p", [P, 2 * S_COLS])
        pT = ph.sb("pT", [P, PT_SLOTS, 4 * P])
        o_sb = ph.sb("o_sb", [P, 2, branches * TILES, row])
        nmax = ph.sb("nmax", [P, 4, 2])
        rden = ph.sb("rden", [P, 4])
        s_ps = ph.ps("s", [P, S_COLS])
        t_ps = [ph.ps(f"t{k}", [P, 4 * P]) for k in range(PT_BANKS)]
        o_ps = ph.ps("o", [P, O_SLOTS, P])

        set_up = ph.sem("set_up")
        qk_loaded = ph.sems("qk_loaded")
        v_loaded = ph.sems("v_loaded")
        sums = ph.sem("sums")
        summed = ph.sem("summed")
        decayed = Count(ph.sem("decayed"), 1)
        turned = Count(ph.sem("turned"), NB)
        copied = [Count(ph.sem("copied_act"), copier.count(0)), Count(ph.sem("copied_dve"), copier.count(1))]
        scored = Count(ph.sem("scored"), NS)
        masked = Count(ph.sem("masked"), NS)
        maxed = Count(ph.sem("maxed"), NS)
        exped = Count(ph.sem("exped"), NS)
        pv = Count(ph.sem("pv"), NG)
        inverted = Count(ph.sem("inverted"), NS)
        posted = Count(ph.sem("posted"), NS)
        o_sent = ph.sems("o_sent")
        if not dilated:
            upto = ph.sb("upto", [P, P])
            ones = ph.sb("ones", [P, P])
            before = ph.sb("before", [P, TILES * HEADS])
            neg_c = ph.sb("neg_c", [P, TILES, HEADS])
            c_loaded = ph.sem("c_loaded")
        n_stores = 6 if dilated else 1
        n_v = n_stores
        block = ph.block()

        def branch_views(tile, hh, cols):
            out = []
            for b, d in enumerate((1, 4, 16) if dilated else (1,)):
                nb = SEQ // d // P
                for r in range(1 if d in (1, 16) else d):
                    t0 = b * TILES + r * nb
                    n = nb if d != 16 else d
                    out.append((tile[:, hh, t0:t0 + n, 0:cols], b, d, r))
            return out

        def tokens(ap, d, r):
            if d == 1:
                return ap.rearrange("(n p) c -> p n c", p=P)
            if d == 16:
                return ap.rearrange("(p r) c -> p r c", r=d)
            return ap.rearrange("(n p r) c -> r p n c", p=P, r=d)[r, :, :, :]

        @block.sync
        def _(sp):
            def load(i, hh):
                h = 2 * i + hh
                cols = ds(h * HD, HD)
                turned.wait(sp, h, -2 * NB + HEAD_GROUPS - 1)
                for name, tile in ((names[0], q_in), (names[1], k_in)):
                    sp.dma_start(tile[:, hh, :, 0:HD], dram[name][0:SEQ, cols].rearrange("(n p) c -> p n c", p=P))\
                        .then_inc(qk_loaded[hh], 16)
                pv.wait(sp, h, -NG - 1)
                for dst, _b, d, r in branch_views(v_in, hh, HD):
                    sp.dma_start(dst, tokens(dram[names[2]][0:SEQ, cols], d, r)).then_inc(v_loaded[hh], 16)

            def store(i, hh):
                h = 2 * i + hh
                posted.wait(sp, h, NS - 1)
                for src, b, d, r in branch_views(o_sb, hh, row):
                    to = dram["dil"][b, :, ds(h * row, row)] if dilated else dram["att"][0:SEQ, ds(h * HD, HD)]
                    sp.dma_start(tokens(to, d, r), src).then_inc(o_sent[hh], 16)

            for hh in range(2):
                sp.sem_inc(o_sent[hh], 16 * n_stores)
            if not dilated:
                sp.dma_start(upto[:, :], dram["upto"]).then_inc(c_loaded, 16)
            load(0, 0)
            load(0, 1)
            with sp.Fori(0, HEADS // 2 - 1) as i:
                for hh in range(2):
                    store(i, hh)
                    load(i + 1, hh)
            for hh in range(2):
                store(HEADS // 2 - 1, hh)
            for hh in range(2):
                sp.wait_ge(o_sent[hh], 16 * n_stores * (HEADS // 2 + 1))

        @block.gpsimd
        def _(pool):
            pool.memset(q_in[:, :, :, HD:P], 0.0).then_inc(set_up, 1)
            pool.memset(k_in[:, :, :, HD:P], 0.0).then_inc(set_up, 1)
            pool.memset(v_in[:, :, :, HD:P], 0.0).then_inc(set_up, 1)
            pool.wait_ge(set_up, 3)
            pool.memset(v_in[:, :, :, HD:HD + 1], 1.0).then_inc(set_up, 1)
            if not dilated:
                pool.memset(q_in[:, :, :, HD:HD + 1], 1.0).then_inc(set_up, 1)
                pool.memset(ones[:, :], 1.0).then_inc(set_up, 1)
        SET_UP = 4 if dilated else 6

        def copy_group(eng, i, hh, b):
            h = 2 * i + hh
            turned.wait(eng, h, b)
            bank = t_ps[b % PT_BANKS]
            if b < HEAD_GROUPS:
                to = (qT if b < HEAD_GROUPS // 2 else kT)[:, hh, b % (HEAD_GROUPS // 2) * 512:][:, 0:512]
                n = 4 * P
                scored.wait(eng, h, -NS - 1)
            else:
                g = b - HEAD_GROUPS
                n = len(groups[g][1]) * P
                pv.wait(eng, h, last_user(pT_used, g))
                to = pT[:, g % PT_SLOTS, 0:n]
            if copier[b] == 0:
                op = nc.scalar.activation(to, bank[:, 0:n], ACT.Copy)
            else:
                op = nc.vector.tensor_copy(to, bank[:, 0:n])
            op.then_inc(copied[copier[b]].sem, 1)

        @block.scalar
        def _(act):
            def exps(i, hh, s):
                h = 2 * i + hh
                maxed.wait(act, h, s)
                turned.wait(act, h, turned_at(last_user(p_used, s)))
                for k, u in enumerate(steps[s]):
                    op = act.activation(p_sb[:, u["p"]:u["p"] + u["w"]], s_ps[:, u["s"]:u["s"] + u["w"]], ACT.Exp,
                                        bias=nmax[:, s % 4, k:k + 1])
                op.then_inc(exped.sem, 1)

            def turned_at(s):
                return HEAD_GROUPS + last_group[s] if s >= 0 else HEAD_GROUPS + last_group[s + NS] - NB

            exped.start(act)
            copied[0].start(act)
            with act.Fori(0, HEADS // 2) as i:
                for hh in range(2):
                    for b in range(HEAD_GROUPS):
                        if copier[b] == 0:
                            copy_group(act, i, hh, b)
                    exps(i, hh, 0)
                    for s in range(NS):
                        for g in range(first_group[s], last_group[s] + 1):
                            if copier[HEAD_GROUPS + g] == 0:
                                copy_group(act, i, hh, HEAD_GROUPS + g)
                        if s + 1 < NS:
                            exps(i, hh, s + 1)

        @block.vector
        def _(dve):
            def maxima(i, hh, s):
                h = 2 * i + hh
                step = steps[s]
                n, w, s0 = len(step), step[0]["w"], step[0]["s"]
                scored.wait(dve, h, s)
                if dilated:
                    part = s_ps[:, s0:s0 + n * w].rearrange("p (n w) -> p n w", w=w)
                    mask = c["mask"][:, 2 * P - w:2 * P].unsqueeze(1).to_broadcast([P, n, w])
                else:
                    part = s_ps[:, s0 + w - P:s0 + w]
                    mask = c["mask"][:, P:2 * P]
                dve.tensor_tensor(part, part, mask, ALU.add).then_inc(masked.sem, 1)
                masked.wait(dve, h, s)
                posted.wait(dve, h, last_user(m_used, s))
                dve.tensor_reduce(nmax[:, s % 4, 0:n], s_ps[:, s0:s0 + n * w].rearrange("p (n w) -> p n w", w=w),
                                  AX_X, ALU.max, negate=True).then_inc(maxed.sem, 1)

            def outputs(i, hh, s):
                h = 2 * i + hh
                step = steps[s]
                pv.wait(dve, h, last_group[s])
                if s == 0:
                    dve.wait_ge(o_sent[hh], 16 * n_stores * (i + 1))
                if dilated:
                    for k, u in enumerate(step):
                        slot = k
                        dve.tensor_scalar(o_sb[:, hh, u["o"], HD + 1:HD + 2], nmax[:, s % 4, k:k + 1], -1.0, None,
                                          ALU.mult)
                        op = dve.tensor_copy(o_sb[:, hh, u["o"], 0:HD + 1], o_ps[:, slot, 0:HD + 1])
                    op.then_inc(posted.sem, 1)
                    return
                slot = 0
                dve.reciprocal(rden[:, slot:slot + 1], o_ps[:, slot, HD:HD + 1]).then_inc(inverted.sem, 1)
                inverted.wait(dve, h, s)
                dve.tensor_scalar(o_sb[:, hh, s, :], o_ps[:, slot, 0:HD], rden[:, slot:slot + 1], None, ALU.mult)\
                    .then_inc(posted.sem, 1)

            for e in (masked, maxed, posted, inverted, decayed, copied[1]):
                e.start(dve)
            if not dilated:
                step = [0]
                lf = c["logf"]
                dve.memset(before[:, 0:HEADS], 0.0).then_inc(sums, 1)
                for t in range(1, TILES):
                    dve.wait_ge(sums, t)
                    dve.tensor_tensor(before[:, t * HEADS:(t + 1) * HEADS], before[:, (t - 1) * HEADS:t * HEADS],
                                      lf[:, (t - 1) * HEADS:t * HEADS], ALU.add).then_inc(sums, 1)
                dve.wait_ge(summed, 1)
                dve.tensor_scalar(neg_c[:, :, :].rearrange("p t h -> p (t h)"), s_ps[:, 0:TILES * HEADS], -1.0, None,
                                  ALU.mult).then_inc(sums, 1)
            dve.wait_ge(set_up, SET_UP)
            with dve.Fori(0, HEADS // 2) as i:
                for hh in range(2):
                    if not dilated:
                        h = 2 * i + hh
                        dve.wait_ge(sums, TILES + 1)
                        turned.wait(dve, h, -2 * NB + HEAD_GROUPS - 1)
                        dve.tensor_copy(k_in[:, hh, :, HD:HD + 1], neg_c[:, :, ds(h, 1)]).then_inc(decayed.sem, 1)
                    for b in range(HEAD_GROUPS):
                        if copier[b] == 1:
                            copy_group(dve, i, hh, b)
                    maxima(i, hh, 0)
                    for s in range(NS):
                        if s + 1 < NS:
                            maxima(i, hh, s + 1)
                        for g in range(first_group[s], last_group[s] + 1):
                            if copier[HEAD_GROUPS + g] == 1:
                                copy_group(dve, i, hh, HEAD_GROUPS + g)
                        outputs(i, hh, s)

        @block.tensor
        def _(pe):
            def bank_free(h, b):
                k = last_user(t_used, b)
                who = copier[k % NB]
                n = copied[who].n
                copied[who].wait(pe, h, copied_at[k % NB] - (n if k < 0 else 0))

            def is_copied(h, b):
                copied[copier[b]].wait(pe, h, copied_at[b])

            def turn_head(i, hh):
                h = 2 * i + hh
                pe.wait_ge(qk_loaded[hh], 32 * (i + 1))
                if not dilated:
                    decayed.wait(pe, h, 0)
                for b in range(HEAD_GROUPS):
                    bank_free(h, b)
                    src = q_in if b < HEAD_GROUPS // 2 else k_in
                    for k in range(4):
                        mm = pe.transpose(t_ps[b % PT_BANKS][:, k * P:(k + 1) * P],
                                          src[:, hh, b % (HEAD_GROUPS // 2) * 4 + k, :], c["ident"][:, :])
                    mm.then_inc(turned.sem, 1)

            def scores(i, hh, s):
                h = 2 * i + hh
                exped.wait(pe, h, last_user(s_used, s))
                for u in steps[s]:
                    q0, d, k0, w = u["q0"], u["d"], u["k0"], u["w"]
                    for x in range(0, w, 512):
                        n = min(512, w - x)
                        a = k0 + x * d
                        mm = pe.matmul(s_ps[:, u["s"] + x:u["s"] + x + n], qT[:, hh, q0:q0 + (P - 1) * d + 1:d],
                                       kT[:, hh, a:a + (n - 1) * d + 1:d], start=True, stop=True)
                mm.then_inc(scored.sem, 1)

            def turn_group(i, hh, g):
                h = 2 * i + hh
                s, blocks = groups[g]
                b = HEAD_GROUPS + g
                exped.wait(pe, h, s)
                bank_free(h, b)
                for k, (u, blk) in enumerate(blocks):
                    p0 = steps[s][u]["p"] + blk * P
                    mm = pe.transpose(t_ps[b % PT_BANKS][:, k * P:(k + 1) * P], p_sb[:, p0:p0 + P], c["ident"][:, :])
                mm.then_inc(turned.sem, 1)

            def products(i, hh, g):
                h = 2 * i + hh
                s, blocks = groups[g]
                is_copied(h, HEAD_GROUPS + g)
                if g == first_group[s]:
                    posted.wait(pe, h, last_user(o_used, s))
                for k, (u, blk) in enumerate(blocks):
                    unit = steps[s][u]
                    mm = pe.matmul(o_ps[:, u, :], pT[:, g % PT_SLOTS, k * P:(k + 1) * P],
                                   v_in[:, hh, unit["v"][blk], :], start=(blk == 0), stop=(blk == unit["w"] // P - 1))
                mm.then_inc(pv.sem, 1)

            for e in (turned, scored, pv):
                e.start(pe)
            if not dilated:
                pe.wait_ge(c_loaded, 16)
                pe.wait_ge(set_up, SET_UP)
                pe.wait_ge(sums, TILES)
                pe.matmul(s_ps[:, 0:TILES * HEADS], upto[:, :], c["logf"][:, 0:TILES * HEADS], start=True, stop=False)
                pe.matmul(s_ps[:, 0:TILES * HEADS], ones[:, :], before[:, :], start=False, stop=True)\
                    .then_inc(summed, 1)
                pe.wait_ge(sums, TILES + 1)
            pe.wait_ge(set_up, SET_UP)
            with pe.Fori(0, HEADS // 2) as i:
                for hh in range(2):
                    turn_head(i, hh)
                    for b in range(HEAD_GROUPS - 3, HEAD_GROUPS):
                        is_copied(2 * i + hh, b)
                    scores(i, hh, 0)
                    pe.wait_ge(v_loaded[hh], 16 * n_v * (i + 1))
                    for s in range(NS):
                        if s + 1 < NS:
                            scores(i, hh, s + 1)
                        turn_group(i, hh, first_group[s])
                        for g in range(first_group[s], last_group[s] + 1):
                            if g < last_group[s]:
                                turn_group(i, hh, g + 1)
                            products(i, hh, g)


GROUPS_KV = 2 * HEADS * DEC_SEQ


def sample_attend(nc, c, dram, dilated):
    NT = 10 if dilated else PAST // PAGE
    sizes = [4, 4, 2] if dilated else [4] * (NT // 4)
    loads = [1, 1, 1] if dilated else [4] * (NT // 4)
    starts = [sum(sizes[:g]) for g in range(len(sizes))]
    NG = len(sizes)
    W = NT * P
    PAIRS = DEC_BATCH // 2
    SEQROWS = HEADS * DEC_SEQ
    names = ("q_b", "k_b", "v_b") if dilated else ("q_a", "k_a", "v_a")
    NX = 2 * NT
    copier = [x % 2 for x in range(NX)]
    p_groups = [list(range(k, min(k + 4, NT))) for k in range(0, NT, 4)]
    PG = len(p_groups)

    with Phase(nc, "sdil" if dilated else "sfox") as ph:
        k_in = ph.sb("k_in", [P, 2, NT, D_G])
        v_in = ph.sb("v_in", [P, 2, NT, D_G])
        kT = ph.sb("kT", [P, 2, 4, 4 * P])
        p_sb = ph.sb("p", [P, W + DEC_SEQ])
        pT = ph.sb("pT", [P, 2, 4 * P])
        pT_new = ph.sb("pT_new", [DEC_SEQ, P])
        new_in = ph.sb("new_in", [2 * DEC_SEQ, 2, D_G])
        v_new = ph.sb("v_new", [DEC_SEQ, 2, D_G])
        q_bd = ph.sb("q_bd", [P, 2, 4, SEQROWS])
        k_new = ph.sb("k_new", [P, 4, 2 * DEC_SEQ])
        own = ph.sb("own", [P, HEADS])
        causal = ph.sb("causal", [P, DEC_SEQ])
        stat = ph.sb("stat", [P, 8])
        o_all = ph.sb("o_all", [P, HEADS, HD])
        o_own = ph.sb("o_own", [P, HD])
        o_sb = ph.sb("o_sb", [P, HD])
        s_ps = ph.ps("s", [P, 2048])
        t_ps = [ph.ps(f"t{k}", [P, 4 * P]) for k in range(2)]
        m_ps = ph.ps("m", [P, 512])
        o_ps = ph.ps("o", [P, D_G])
        if dilated:
            reach = ph.sb("reach", [P, W + DEC_SEQ])
            unreached = ph.sb("unreached", [P, W + DEC_SEQ])
        else:
            table = ph.sb("table", [1, DEC_BATCH * NT], I32)
            lf_in = ph.sb("lf_in", [P, NT, 2, HEADS])
            lf_back = ph.sb("lf_back", [P, NT, 2, HEADS])
            lf_x = ph.sb("lf_x", [P, 2, NT, P])
            lf_new = ph.sb("lf_new", [DEC_SEQ, 2, HEADS])
            lf_newx = ph.sb("lf_newx", [DEC_SEQ, 2, SEQROWS])
            after = ph.sb("after", [P, P])
            upto = ph.sb("upto", [P, P])
            ones = ph.sb("ones", [P, P])
            table_loaded = ph.sem("table_loaded")
            lf_loaded = ph.sem("lf_loaded")
            backed = Count(ph.sem("backed"), NT)
            spread = Count(ph.sem("spread"), 5)

        passed = ph.sem("passed")
        consts = ph.sem("consts")
        zeroed = ph.sem("zeroed")
        new_loaded = ph.sem("new_loaded")
        vn_loaded = ph.sem("vn_loaded")
        k_loaded = [ph.sem(f"k_loaded{g}") for g in range(2 * NG)]
        v_loaded = [ph.sem(f"v_loaded{g}") for g in range(2 * NG)]
        new_turned = Count(ph.sem("new_turned"), 1)
        q_spread = Count(ph.sem("q_spread"), 1)
        turned = Count(ph.sem("turned"), NX)
        copied = [Count(ph.sem("copied_act"), NX // 2), Count(ph.sem("copied_dve"), NX // 2)]
        scored = Count(ph.sem("scored"), 2 * NG + 1)
        masked = Count(ph.sem("masked"), 2)
        maxed = Count(ph.sem("maxed"), 3)
        exped = Count(ph.sem("exped"), 1)
        weighed = Count(ph.sem("weighed"), 1)
        p_turned = Count(ph.sem("p_turned"), PG + 1)
        p_copied = Count(ph.sem("p_copied"), PG + 1)
        pv = Count(ph.sem("pv"), PG + 1)
        out = Count(ph.sem("out"), 4)
        o_sent = ph.sem("o_sent")
        block = ph.block()
        PT_ALL = 2 * NG

        @block.sync
        def _(sp):
            pairs = [(own[:, :], dram["own"]), (causal[:, :], dram["causal_new"])]
            if dilated:
                pairs += [(reach[:, :], dram["reach"]), (unreached[:, :], dram["unreached"])]
            else:
                pairs += [(after[:, :], dram["after"]), (upto[:, :], dram["upto"])]
                sp.dma_start(table[:, :], dram["page_table"]).then_inc(table_loaded, 16)
                sp.wait_ge(table_loaded, 16)
            for dst, src in pairs:
                sp.dma_start(dst, src).then_inc(consts, 16)

            def load_new(i):
                rows = ds(SEQ + i * 2 * DEC_SEQ, 2 * DEC_SEQ)
                new_turned.wait(sp, i, -1)
                for n in range(2):
                    sp.dma_start(new_in[:, n, :], dram[names[n]][rows, :]).then_inc(new_loaded, 16)
                pv.wait(sp, i, -1)
                sp.dma_start(v_new[:, :, :], dram[names[2]][rows, :].rearrange("(s q) d -> q s d", q=DEC_SEQ))\
                    .then_inc(vn_loaded, 16)
                if not dilated:
                    spread.wait(sp, i, -1)
                    sp.dma_start(lf_new[:, :, :], dram["logf"][rows, :].rearrange("(s q) h -> q s h", q=DEC_SEQ))\
                        .then_inc(vn_loaded, 16)

            def load_kv(i, s2, g, kv):
                tile, src = ((k_in, "win_k"), (v_in, "win_v"))[kv] if dilated else \
                            ((k_in, "cache_k"), (v_in, "cache_v"))[kv]
                sem = (k_loaded, v_loaded)[kv][s2 * NG + g]
                if kv == 0:
                    turned.wait(sp, i, s2 * NT + starts[g] + sizes[g] - 1 - NX)
                else:
                    pv.wait(sp, i, g - PG - 1)
                sp.sem_inc(passed, 1)
                if dilated:
                    win = dram[src][ds(2 * i + s2, 1), :, :]
                    if g < 2:
                        view = win.rearrange("a (m r) d -> (a m) r d", r=16)[:, 4 * g:4 * g + 4, :]
                        sp.dma_start(tile[:, s2, 4 * g:4 * g + 4, :], view).then_inc(sem, 16)
                    else:
                        view = win.rearrange("a (m r) d -> (a m) r d", r=16)[96:128, 8:16, :]
                        sp.dma_start(tile[:, s2, 8:10, :], view.rearrange("m (b t) d -> m b (t d)", t=2))\
                            .then_inc(sem, 16)
                    return
                for t in range(starts[g], starts[g] + sizes[g]):
                    page = sp.value_load(table[0:1, ds((2 * i + s2) * NT + t, 1)], min_val=0,
                                         max_val=dram[src].shape[0] - 1)
                    sp.dma_start(tile[:, s2, t, :], dram[src][ds(page, 1), :, :].rearrange("a p d -> (a p) d"))\
                        .then_inc(sem, 16)
                    if kv == 0:
                        if t == 0 and s2 == 0:
                            spread.wait(sp, i, 3 - 5)
                        sp.dma_start(lf_in[:, t, s2, :],
                                     dram["cache_logf"][ds(page, 1), :, :].rearrange("a p d -> (a p) d"))\
                            .then_inc(lf_loaded, 16)

            with sp.Fori(0, PAIRS) as i:
                load_new(i)
                for s2 in range(2):
                    for g in range(NG):
                        load_kv(i, s2, g, 0)
                for g in range(NG):
                    for s2 in range(2):
                        load_kv(i, s2, g, 1)

        @block.gpsimd
        def _(pool):
            pool.memset(q_bd[:, :, :, :], 0.0).then_inc(zeroed, 1)
            if not dilated:
                pool.memset(ones[:, :], 1.0).then_inc(zeroed, 1)
                spread.start(pool)
            if dilated:
                return
            with pool.Fori(0, PAIRS) as i:
                scored.wait(pool, i, -1)
                pool.wait_ge(lf_loaded, 16 * NX * (i + 1))
                pool.wait_ge(vn_loaded, 32 * (i + 1))
                pool.sem_inc(passed, 1)

                def spread_rows(dst, src):
                    pool.tensor_copy(dst.rearrange("p t (h q) -> p t h q", q=DEC_SEQ),
                                     src.unsqueeze(3).to_broadcast([src.shape[0], src.shape[1], HEADS, DEC_SEQ]))\
                        .then_inc(spread.sem, 1)

                for s2 in range(2):
                    spread_rows(lf_x[:, 0, :, s2 * SEQROWS:(s2 + 1) * SEQROWS], lf_in[:, :, s2, :])
                backed.wait(pool, i, NT - 1)
                pool.sem_inc(passed, 1)
                for s2 in range(2):
                    spread_rows(lf_x[:, 1, :, s2 * SEQROWS:(s2 + 1) * SEQROWS], lf_back[:, :, s2, :])
                pool.tensor_scalar(lf_newx[:, :, :].rearrange("p s (h q) -> p s h q", q=DEC_SEQ),
                                   lf_new[:, :, :].unsqueeze(3).to_broadcast([DEC_SEQ, 2, HEADS, DEC_SEQ]),
                                   -1.0, None, ALU.mult).then_inc(spread.sem, 1)

        def copy_tile(eng, i, x):
            turned.wait(eng, i, x)
            s2, t = divmod(x, NT)
            g = t // 4
            scored.wait(eng, i, s2 * NG + g - 2 if s2 * NG + g >= 2 else s2 * NG + g - 3)
            k = t - starts[g]
            to = kT[:, (s2 * NG + g) % 2, :, k * P:(k + 1) * P]
            src = t_ps[x % 2][:, :].rearrange("p (j m) -> p j m", m=P)
            if copier[x] == 0:
                nc.scalar.activation(to, src, ACT.Copy).then_inc(copied[0].sem, 1)
            else:
                nc.vector.tensor_copy(to, src).then_inc(copied[1].sem, 1)

        @block.scalar
        def _(act):
            act.sem_inc(o_sent, 32)
            copied[0].start(act)
            exped.start(act)
            p_copied.start(act)
            with act.Fori(0, PAIRS) as i:
                for x in range(0, NX, 2):
                    copy_tile(act, i, x)
                maxed.wait(act, i, 2)
                p_turned.wait(act, i, -1)
                out.wait(act, i, -1)
                act.activation(p_sb[:, 0:W], s_ps[:, 0:W], ACT.Exp, bias=stat[:, 2:3], accum_out=stat[:, 3:4])
                act.activation(p_sb[:, W:W + DEC_SEQ], m_ps[:, 0:DEC_SEQ], ACT.Exp, bias=stat[:, 2:3],
                               accum_out=stat[:, 4:5]).then_inc(exped.sem, 1)
                for g in range(PG + 1):
                    p_turned.wait(act, i, g)
                    pv.wait(act, i, g - 2 if g >= 2 else g - PG - 1)
                    if g < PG:
                        n = len(p_groups[g]) * P
                        op = act.activation(pT[:, g % 2, 0:n], t_ps[g % 2][:, 0:n], ACT.Copy)
                    else:
                        op = act.activation(pT_new[:, :], t_ps[g % 2][0:DEC_SEQ, 0:P], ACT.Copy)
                    op.then_inc(p_copied.sem, 1)
                out.wait(act, i, 3)
                for s2 in range(2):
                    base = SEQ + s2 * DEC_SEQ
                    for h in range(HEADS):
                        col = (D_G if dilated else 0) + h * HD
                        act.dma_start(dram["att"][ds(i * 2 * DEC_SEQ + base, DEC_SEQ), col:col + HD],
                                       o_sb[s2 * SEQROWS + h * DEC_SEQ:s2 * SEQROWS + (h + 1) * DEC_SEQ, :])\
                            .then_inc(o_sent, 16)
            act.wait_ge(o_sent, 32 + 16 * 2 * HEADS * PAIRS)

        @block.vector
        def _(dve):
            for e in (copied[1], masked, maxed, weighed, q_spread, out) + (() if dilated else (backed,)):
                e.start(dve)
            dve.wait_ge(consts, 64)
            dve.wait_ge(zeroed, 1)
            with dve.Fori(0, PAIRS) as i:
                new_turned.wait(dve, i, 0)
                scored.wait(dve, i, -1)
                turned_new = m_ps[:, 0:2 * 4 * 2 * DEC_SEQ].rearrange("p (n j s q) -> p n j s q", n=2, j=4, s=2)
                for hp in range(2):
                    rows = slice(hp * HD, (hp + 1) * HD)
                    for j in range(4):
                        a = (2 * j + hp) * DEC_SEQ
                        dve.tensor_copy(q_bd[rows, :, j, a:a + DEC_SEQ], turned_new[rows, 0, j, :, :])
                dve.tensor_copy(k_new[:, :, :].rearrange("p j (s q) -> p j s q", s=2), turned_new[:, 1, :, :, :])\
                    .then_inc(q_spread.sem, 1)
                if not dilated:
                    dve.wait_ge(lf_loaded, 16 * NX * (i + 1))
                    spread.wait(dve, i, 3 - 5)
                    dve.memset(lf_back[:, NT - 1, :, :], 0.0).then_inc(backed.sem, 1)
                    for n, t in enumerate(reversed(range(NT - 1))):
                        backed.wait(dve, i, n)
                        dve.tensor_tensor(lf_back[:, t, :, :], lf_back[:, t + 1, :, :], lf_in[:, t + 1, :, :], ALU.add)\
                            .then_inc(backed.sem, 1)
                for x in range(1, NX, 2):
                    copy_tile(dve, i, x)
                scored.wait(dve, i, PT_ALL)
                if dilated:
                    dve.tensor_tensor(s_ps[:, 0:W], s_ps[:, 0:W], unreached[:, 0:W], ALU.add).then_inc(masked.sem, 1)
                    dve.tensor_tensor(m_ps[:, 0:DEC_SEQ], m_ps[:, 0:DEC_SEQ], unreached[:, W:W + DEC_SEQ], ALU.add)\
                        .then_inc(masked.sem, 1)
                else:
                    dve.tensor_tensor(m_ps[:, 0:DEC_SEQ], m_ps[:, 0:DEC_SEQ], causal[:, :], ALU.add)\
                        .then_inc(masked.sem, 2)
                masked.wait(dve, i, 1)
                out.wait(dve, i, -1)
                dve.tensor_reduce(stat[:, 0:1], s_ps[:, 0:W], AX_X, ALU.max, negate=True).then_inc(maxed.sem, 1)
                dve.tensor_reduce(stat[:, 1:2], m_ps[:, 0:DEC_SEQ], AX_X, ALU.max, negate=True).then_inc(maxed.sem, 1)
                maxed.wait(dve, i, 1)
                dve.tensor_tensor(stat[:, 2:3], stat[:, 0:1], stat[:, 1:2], ALU.min).then_inc(maxed.sem, 1)
                exped.wait(dve, i, 0)
                if dilated:
                    dve.scalar_tensor_tensor(p_sb[:, :], p_sb[:, :], 1.0, reach[:, :], ALU.mult, ALU.mult,
                                             accum_out=stat[:, 5:6]).then_inc(weighed.sem, 1)
                else:
                    dve.tensor_tensor(stat[:, 5:6], stat[:, 3:4], stat[:, 4:5], ALU.add).then_inc(weighed.sem, 1)
                weighed.wait(dve, i, 0)
                dve.reciprocal(stat[:, 6:7], stat[:, 5:6]).then_inc(out.sem, 1)
                pv.wait(dve, i, PG)
                dve.tensor_tensor(o_all[:, :, :], o_ps[:, :].rearrange("p (h d) -> p h d", d=HD),
                                  own[:, :].unsqueeze(2).to_broadcast([P, HEADS, HD]), ALU.mult).then_inc(out.sem, 1)
                out.wait(dve, i, 1)
                dve.tensor_reduce(o_own[:, :], o_all[:, :, :].rearrange("p h d -> p d h"), AX_X, ALU.add)\
                    .then_inc(out.sem, 1)
                out.wait(dve, i, 2)
                dve.wait_ge(o_sent, 16 * 2 * HEADS * i + 32)
                dve.tensor_scalar(o_sb[:, :], o_own[:, :], stat[:, 6:7], None, ALU.mult).then_inc(out.sem, 1)

        @block.tensor
        def _(pe):
            for e in (new_turned, turned, scored, p_turned, pv):
                e.start(pe)
            pe.wait_ge(consts, 64)
            pe.wait_ge(zeroed, 1 if dilated else 2)

            def is_copied(i, x):
                copied[copier[x % NX]].wait(pe, i, (x % NX) // 2 - (NX // 2 if x < 0 else 0))

            def turn_tile(i, x):
                s2, t = divmod(x, NT)
                g = t // 4
                if t == starts[g]:
                    pe.wait_ge(k_loaded[s2 * NG + g], 16 * loads[g] * (i + 1))
                if x < 2:
                    p_copied.wait(pe, i, -1)
                else:
                    is_copied(i, x - 2)
                for j in range(4):
                    mm = pe.transpose(t_ps[x % 2][:, j * P:(j + 1) * P], k_in[:, s2, t, j * P:(j + 1) * P],
                                      c["ident"][:, :])
                mm.then_inc(turned.sem, 1)

            def scores(i, gg):
                s2, g = divmod(gg, NG)
                last = s2 * NT + starts[g] + sizes[g] - 1
                is_copied(i, last)
                is_copied(i, last - 1)
                if gg == 0:
                    exped.wait(pe, i, -1)
                n = sizes[g] * P
                rows = slice(s2 * SEQROWS, (s2 + 1) * SEQROWS)
                for j in range(4):
                    mm = pe.matmul(s_ps[rows, starts[g] * P:starts[g] * P + n], q_bd[:, s2, j, :],
                                   kT[:, gg % 2, j, 0:n], start=(j == 0), stop=(j == 3 and dilated))
                mm.then_inc(scored.sem, 1)

            with pe.Fori(0, PAIRS) as i:
                pe.wait_ge(new_loaded, 32 * (i + 1))
                exped.wait(pe, i, -1)
                pe.sem_inc(passed, 1)
                for n in range(2):
                    for j in range(4):
                        a = (n * 4 + j) * 2 * DEC_SEQ
                        mm = pe.transpose(m_ps[:, a:a + 2 * DEC_SEQ], new_in[:, n, j * P:(j + 1) * P],
                                          c["ident"][0:2 * DEC_SEQ, 0:2 * DEC_SEQ])
                mm.then_inc(new_turned.sem, 1)
                q_spread.wait(pe, i, 0)
                done = 0
                for x in range(NX):
                    turn_tile(i, x)
                    while done < 2 * NG and x >= min(NX - 1, (done // NG) * NT + starts[done % NG] + sizes[done % NG] + 1):
                        scores(i, done)
                        done += 1
                while done < 2 * NG:
                    scores(i, done)
                    done += 1
                for s2 in range(2):
                    rows = slice(s2 * SEQROWS, (s2 + 1) * SEQROWS)
                    for j in range(4):
                        mm = pe.matmul(m_ps[rows, 0:DEC_SEQ], q_bd[:, s2, j, :],
                                       k_new[:, j, s2 * DEC_SEQ:(s2 + 1) * DEC_SEQ], start=(j == 0),
                                       stop=(j == 3 and dilated))
                    if not dilated:
                        if s2 == 0:
                            spread.wait(pe, i, 4)
                        mm = pe.matmul(m_ps[rows, 0:DEC_SEQ], lf_newx[:, s2, :], upto[0:DEC_SEQ, 0:DEC_SEQ],
                                       start=False, stop=True)
                if not dilated:
                    for t in range(NT):
                        pe.matmul(s_ps[:, t * P:(t + 1) * P], lf_x[:, 0, t, :], after[:, :], start=False, stop=False)
                        mm = pe.matmul(s_ps[:, t * P:(t + 1) * P], lf_x[:, 1, t, :], ones[:, :], start=False,
                                       stop=(t % 4 == 3))
                mm.then_inc(scored.sem, 1)

                def turn_p(g):
                    if g < 2:
                        is_copied(i, NX - 2 + g)
                        if g == 0:
                            weighed.wait(pe, i, 0)
                    else:
                        p_copied.wait(pe, i, g - 2)
                    if g < PG:
                        for k, t in enumerate(p_groups[g]):
                            mm = pe.transpose(t_ps[g % 2][:, k * P:(k + 1) * P], p_sb[:, t * P:(t + 1) * P],
                                              c["ident"][:, :])
                    else:
                        mm = pe.transpose(t_ps[g % 2][0:DEC_SEQ, 0:P], p_sb[:, W:W + DEC_SEQ], c["ident"][:, :])
                    mm.then_inc(p_turned.sem, 1)

                def products(g):
                    p_copied.wait(pe, i, g)
                    if g == 0:
                        out.wait(pe, i, 1 - 4)
                    if g == PG:
                        pe.wait_ge(vn_loaded, (16 if dilated else 32) * (i + 1))
                    for s2 in range(2):
                        rows = slice(s2 * SEQROWS, (s2 + 1) * SEQROWS)
                        if g < PG:
                            pe.wait_ge(v_loaded[s2 * NG + g], 16 * loads[g] * (i + 1))
                            for k, t in enumerate(p_groups[g]):
                                mm = pe.matmul(o_ps[rows, :], pT[:, g % 2, k * P + s2 * SEQROWS:k * P + (s2 + 1) * SEQROWS],
                                               v_in[:, s2, t, :], start=(t == 0), stop=False)
                        else:
                            mm = pe.matmul(o_ps[rows, :], pT_new[:, rows], v_new[:, s2, :], start=False, stop=True)
                    mm.then_inc(pv.sem, 1)

                turn_p(0)
                for g in range(PG + 1):
                    if g < PG:
                        turn_p(g + 1)
                    products(g)


def join_heads(nc, c, dram, g, first, tiles, h_hi, h_lo, x1):
    with Phase(nc, f"join{g}") as ph:
        w_raw = ph.sb("w_raw", [P, 2, D_G])
        w_hi = ph.sb("w_hi", [P, KC, D_MODEL], F32R)
        w_lo = ph.sb("w_lo", [P, KC, D_MODEL], F32R)
        o_in = ph.sb("o_in", [P, 2, D_MODEL])
        parts = ph.sb("parts", [P, 3, HEADS, HD + 2])
        o_hi = ph.sb("o_hi", [P, D_MODEL], F32R)
        o_lo = ph.sb("o_lo", [P, D_MODEL], F32R)
        h = ph.sb("h", [P, D_MODEL])
        hg = ph.sb("hg", [P, D_MODEL])
        g_mlp = ph.sb("g_mlp", [P, KC])
        top = ph.sb("top", [P, 2, HEADS])
        e = ph.sb("e", [P, 2, 3, HEADS])
        den = ph.sb("den", [P, 2, HEADS])
        stat = ph.sb("stat", [P, 3])
        minus_half = ph.sb("minus_half", [P, 1])
        to_ps = ph.ps("to", [P, D_MODEL])
        th_ps = ph.ps("th", [P, D_MODEL])
        pr_ps = [ph.ps(f"pr{j}", [P, D_MODEL]) for j in range(2)]

        passed = ph.sem("passed")
        consts = ph.sem("consts")
        x_loaded = ph.sem("x_loaded")
        half_set = ph.sem("half_set")
        w_loaded = ph.sems("w_loaded")
        w_hi_done = ph.sem("w_hi_done")
        w_split = ph.sem("w_split")
        o_loaded = ph.sems("o_loaded")
        parts_loaded = ph.sem("parts_loaded")
        weights = ph.sem("weights")
        exped = ph.sem("exped")
        weighed = ph.sem("weighed")
        merged = ph.sem("merged")
        o_turned = ph.sem("o_turned")
        o_hi_done = ph.sem("o_hi_done")
        o_lo_done = ph.sem("o_lo_done")
        product = ph.sem("product")
        added = ph.sem("added")
        squared = ph.sem("squared")
        mean_done = ph.sem("mean_done")
        rstd_done = ph.sem("rstd_done")
        h_done = ph.sem("h_done")
        h_turned = ph.sem("h_turned")
        hg_done = ph.sem("hg_done")
        h_hi_done = ph.sem("h_hi_done")
        h_lo_done = ph.sem("h_lo_done")
        block = ph.block()

        n_prompt = min(tiles, TILES - first)

        def steps(eng, body):
            body(0)
            with eng.Fori(0, (n_prompt - 2) // 2) as i:
                body(2 * i + 1, 1)
                body(2 * i + 2, 0)
            for t in range(n_prompt - 1, tiles):
                body(t)

        def behind(t):
            return isinstance(t, int) and t == 0

        def ahead(t):
            return not isinstance(t, int) or t + 1 < tiles, not isinstance(t, int) or t + 1 < n_prompt

        @block.sync
        def _(sp):
            def load_o(t, slot):
                rows = ds((first + t) * P, P)
                if isinstance(t, int) and t >= n_prompt:
                    sp.wait_ge(o_turned, t - 1)
                    sp.dma_start(o_in[0:N_SAMPLE, slot, :], dram["att"][SEQ:SEQ + N_SAMPLE, :])\
                        .then_inc(o_loaded[slot], 16)
                    return
                if not (isinstance(t, int) and t < 2):
                    sp.wait_ge(o_turned, t - 1)
                sp.dma_start(o_in[:, slot, 0:D_G], dram["att"][rows, 0:D_G]).then_inc(o_loaded[slot], 16)
                if not (isinstance(t, int) and t == 0):
                    sp.wait_ge(merged, 2 * t)
                sp.dma_start(parts[:, :, :, :].rearrange("p b h d -> p b (h d)"),
                             dram["dil"][:, rows, :].rearrange("b p n -> p b n")).then_inc(parts_loaded, 16)

            def load_w(k):
                sp.dma_start(w_raw[:, k % 2, :], dram["w_o"][k // 2 * P:(k // 2 + 1) * P,
                                                             k % 2 * D_G:(k % 2 + 1) * D_G])\
                    .then_inc(w_loaded[k % 2], 16)

            load_o(0, 0)
            load_w(0)
            load_w(1)
            sp.dma_start(g_mlp[:, :], dram["g_mlp"]).then_inc(consts, 16)
            sp.dma_start(x1[:, 0:tiles, :], dram["x"][first * P:(first + tiles) * P, :]
                         .rearrange("(t p) n -> p t n", p=P)).then_inc(x_loaded, 16)
            for k in range(2, 2 * KC):
                sp.wait_ge(w_split, k - 1)
                load_w(k)
            load_o(1, 1)
            with sp.Fori(0, (n_prompt - 2) // 2) as i:
                load_o(2 * i + 2, 0)
                load_o(2 * i + 3, 1)
            for t in range(n_prompt, tiles):
                load_o(t, t % 2)

        @block.scalar
        def _(act):
            def weigh(t):
                act.wait_ge(weights, 7 * t + 3)
                act.activation(e[:, 1, :, :], e[:, 0, :, :], ACT.Exp).then_inc(exped, 1)

            def hi_o(t):
                act.wait_ge(o_turned, t + 1)
                if not (isinstance(t, int) and t == 0):
                    act.wait_ge(product, t)
                act.activation(o_hi[:, :], to_ps[:, :], ACT.Copy).then_inc(o_hi_done, 1)

            def hi_h(t):
                act.wait_ge(hg_done, 2 * (t + 1))
                act.activation(h_hi[:, :, ds(t * P, P)] if not isinstance(t, int) or t < n_prompt else
                               h_hi[:, :, t * P:t * P + N_SAMPLE],
                               (hg[:, :].rearrange("p (k m) -> p k m", m=P) if not isinstance(t, int) or t < n_prompt
                                else hg[:, :].rearrange("p (k m) -> p k m", m=P)[:, :, 0:N_SAMPLE]),
                               ACT.Copy).then_inc(h_hi_done, 1)

            def body(t, odd=None):
                has, prompt = ahead(t)
                if has:
                    if prompt:
                        weigh(t + 1)
                    hi_o(t + 1)
                act.wait_ge(added, 2 * (t + 1))
                if not behind(t):
                    act.wait_ge(h_turned, t)
                act.activation(h[:, :], x1[:, ds(t, 1), :].rearrange("p a n -> p (a n)"), ACT.Square,
                               accum_out=stat[:, 0:1]).then_inc(squared, 1)
                act.wait_ge(rstd_done, t + 1)
                act.sem_inc(passed, 1)
                act.activation(h[:, :], x1[:, ds(t, 1), :].rearrange("p a n -> p (a n)"), ACT.Copy,
                               scale=stat[:, 2:3]).then_inc(h_done, 1)
                if not behind(t):
                    hi_h(t - 1)

            for k in range(2 * KC):
                act.wait_ge(w_loaded[k % 2], 16 * (k // 2 + 1))
                act.activation(w_hi[:, k // 2, k % 2 * D_G:(k % 2 + 1) * D_G], w_raw[:, k % 2, :], ACT.Copy).then_inc(w_hi_done, 1)
            weigh(0)
            hi_o(0)
            steps(act, body)
            hi_h(tiles - 1)

        @block.gpsimd
        def _(pool):
            pool.memset(minus_half[:, :], -0.5).then_inc(half_set, 1)
            pool.wait_ge(half_set, 1)

            def weigh(t):
                pool.wait_ge(weights, 7 * (t + 1))
                pool.tensor_tensor(parts[:, :, :, 0:HD], parts[:, :, :, 0:HD],
                                   e[:, 0, :, :].unsqueeze(3).to_broadcast([P, 3, HEADS, HD]),
                                   ALU.mult).then_inc(weighed, 1)

            def lo_h(t):
                pool.wait_ge(h_hi_done, t + 1)
                n = N_SAMPLE if isinstance(t, int) and t >= n_prompt else P
                pool.tensor_tensor(h_lo[:, :, ds(t * P, n)], hg[:, :].rearrange("p (k m) -> p k m", m=P)[:, :, 0:n],
                                   h_hi[:, :, ds(t * P, n)].bitcast(F32), ALU.subtract).then_inc(h_lo_done, 1)

            def body(t, odd=None):
                has, prompt = ahead(t)
                if has and prompt:
                    weigh(t + 1)
                pool.wait_ge(mean_done, t + 1)
                pool.tensor_tensor(stat[:, 2:3], stat[:, 1:2], minus_half[:, :], ALU.pow).then_inc(rstd_done, 1)
                if not behind(t):
                    lo_h(t - 1)

            weigh(0)
            steps(pool, body)
            lo_h(tiles - 1)

        @block.vector
        def _(dve):
            m = parts[:, :, :, HD + 1]
            l = parts[:, :, :, HD]

            def merge(t, slot):
                w = 7 * t

                def step(op, k):
                    op.then_inc(weights, 1)
                    if k < 7:
                        dve.wait_ge(weights, w + k)

                dve.wait_ge(parts_loaded, 16 * (t + 1))
                step(dve.tensor_tensor(top[:, 0, :], m[:, 0, :], m[:, 1, :], ALU.max), 1)
                step(dve.tensor_tensor(top[:, 1, :], top[:, 0, :], m[:, 2, :], ALU.max), 2)
                step(dve.tensor_tensor(e[:, 0, :, :], m, top[:, 1:2, :].to_broadcast([P, 3, HEADS]), ALU.subtract), 3)
                dve.wait_ge(exped, t + 1)
                step(dve.tensor_tensor(e[:, 0, :, :], l, e[:, 1, :, :], ALU.mult), 4)
                step(dve.tensor_reduce(den[:, 0, :], e[:, 0, :, :].rearrange("p b h -> p h b"), AX_X, ALU.add), 5)
                step(dve.reciprocal(den[:, 1, :], den[:, 0, :]), 6)
                step(dve.tensor_tensor(e[:, 0, :, :], e[:, 1, :, :],
                                       den[:, 1:2, :].to_broadcast([P, 3, HEADS]), ALU.mult), 7)
                dve.wait_ge(weighed, t + 1)
                dve.wait_ge(o_loaded[slot], 16 * ((t - slot) // 2 + 1) if isinstance(t, int) else half_uses(t))
                out = o_in[:, slot, D_G:D_MODEL].rearrange("p (h d) -> p h d", d=HD)
                dve.tensor_tensor(out, parts[:, 0, :, 0:HD], parts[:, 1, :, 0:HD], ALU.add).then_inc(merged, 1)
                dve.wait_ge(merged, 2 * t + 1)
                dve.tensor_tensor(out, out, parts[:, 2, :, 0:HD], ALU.add).then_inc(merged, 1)

            def lo_o(t):
                dve.wait_ge(o_hi_done, t + 1)
                dve.tensor_tensor(o_lo[:, :], to_ps[:, :], o_hi[:, :].bitcast(F32), ALU.subtract)\
                    .then_inc(o_lo_done, 1)

            def gain(t):
                dve.wait_ge(h_turned, t + 1)
                if not (isinstance(t, int) and t == 0):
                    dve.wait_ge(h_lo_done, t)
                for q in range(2):
                    dve.tensor_tensor(hg[:, q * 512:(q + 1) * 512].rearrange("p (k m) -> p k m", m=P),
                                      th_ps[:, q * 512:(q + 1) * 512].rearrange("p (k m) -> p k m", m=P),
                                      g_mlp[:, 4 * q:4 * q + 4].unsqueeze(2).to_broadcast([P, 4, P]),
                                      ALU.mult).then_inc(hg_done, 1)

            def body(t, odd=None):
                has, prompt = ahead(t)
                slot = t % 2 if isinstance(t, int) else odd
                if has:
                    if prompt:
                        merge(t + 1, 1 - slot)
                    lo_o(t + 1)
                dve.wait_ge(product, t + 1)
                for q in range(2):
                    part = x1[:, ds(t, 1), q * D_G:(q + 1) * D_G].rearrange("p a n -> p (a n)")
                    dve.tensor_tensor(part, pr_ps[slot][:, q * D_G:(q + 1) * D_G], part, ALU.add).then_inc(added, 1)
                dve.wait_ge(squared, t + 1)
                dve.tensor_scalar(stat[:, 1:2], stat[:, 0:1], 1.0 / D_MODEL, EPS, ALU.mult, ALU.add)\
                    .then_inc(mean_done, 1)
                if not behind(t):
                    gain(t - 1)

            for k in range(2 * KC):
                dve.wait_ge(w_hi_done, k + 1)
                half = slice(k % 2 * D_G, (k % 2 + 1) * D_G)
                dve.tensor_tensor(w_lo[:, k // 2, half], w_raw[:, k % 2, :], w_hi[:, k // 2, half].bitcast(F32),
                                  ALU.subtract)\
                    .then_inc(w_split, 1)
            dve.wait_ge(consts, 16)
            dve.wait_ge(x_loaded, 16)

            def half_uses(t):
                return loop_uses[0]

            loop_uses = [None]
            merge(0, 0)
            lo_o(0)
            body(0)
            with dve.Fori(0, (n_prompt - 2) // 2) as i:
                loop_uses[0] = 16 * (i + 2)
                body(2 * i + 1, 1)
                body(2 * i + 2, 0)
            for t in range(n_prompt - 1, tiles):
                body(t)
            gain(tiles - 1)

        @block.tensor
        def _(pe):
            def turn_o(t, slot, prompt=True):
                if prompt:
                    pe.wait_ge(merged, 2 * (t + 1))
                else:
                    pe.wait_ge(o_loaded[slot], 16 * (t // 2 + 1))
                if not behind(t):
                    pe.wait_ge(o_lo_done, t)
                for k in range(KC):
                    mm = pe.transpose(to_ps[:, k * P:(k + 1) * P], o_in[:, slot, k * P:(k + 1) * P],
                                      c["ident"][:, :])
                mm.then_inc(o_turned, 1)

            def turn_h(t):
                pe.wait_ge(h_done, t + 1)
                if not behind(t):
                    pe.wait_ge(hg_done, 2 * t)
                for k in range(KC):
                    mm = pe.transpose(th_ps[:, k * P:(k + 1) * P], h[:, k * P:(k + 1) * P], c["ident"][:, :])
                mm.then_inc(h_turned, 1)

            def body(t, odd=None):
                has, prompt = ahead(t)
                slot = t % 2 if isinstance(t, int) else odd
                pe.wait_ge(o_lo_done, t + 1)
                if not behind(t) and not (isinstance(t, int) and t < 2):
                    pe.wait_ge(added, 2 * (t - 1))
                for q in range(2):
                    out = pr_ps[slot][:, q * D_G:(q + 1) * D_G]
                    for k in range(KC):
                        a = slice(k * P, (k + 1) * P)
                        b = slice(q * D_G, (q + 1) * D_G)
                        pe.matmul(out, o_hi[:, a], w_hi[:, k, b], start=(k == 0), stop=False)
                        pe.matmul(out, o_hi[:, a], w_lo[:, k, b], start=False, stop=False)
                        mm = pe.matmul(out, o_lo[:, a], w_hi[:, k, b], start=False, stop=(k == KC - 1))
                mm.then_inc(product, 1)
                if has:
                    turn_o(t + 1, 1 - slot, prompt)
                if not behind(t):
                    turn_h(t - 1)

            pe.wait_ge(w_split, 2 * KC)
            turn_o(0, 0)
            steps(pe, body)
            turn_h(tiles - 1)


def mlp(nc, c, dram, g, first, tiles, h_hi, h_lo, x1):
    n_prompt = min(tiles, TILES - first)
    chunks = [(4 * P * k, 4 * P, 4) for k in range(n_prompt // 4)]
    if tiles > n_prompt:
        chunks.append((n_prompt * P, N_SAMPLE, 1))
    NCH = len(chunks)
    FB = FBLK // P
    BLOCKS = D_FF // FBLK
    HALF = KC // 2
    PIECES = 4
    with Phase(nc, f"mlp{g}") as ph:
        w_raw = ph.sb("w_raw", [P, 2, 1024])
        w_hi = ph.sb("w_hi", [P, 2, PIECES, 1024], F32R)
        w_lo = ph.sb("w_lo", [P, 2, PIECES, 1024], F32R)
        r = ph.sb("r", [P, FB, 512])
        u = ph.sb("u", [P, FB, 512])
        u_hi = ph.sb("u_hi", [P, 2, FB, 512], F32R)
        u_lo = ph.sb("u_lo", [P, 2, FB, 512], F32R)
        u_ps = [ph.ps(f"u{j}", [P, FB, 512]) for j in range(2)]
        y_ps = [ph.ps(f"y{j}", [P, D_MODEL]) for j in range(2)]
        w_loaded = ph.sems("w_loaded")
        w_hi_done = ph.sem("w_hi_done")
        w_split = ph.sem("w_split")
        up_done = ph.sem("up_done")
        relu_done = ph.sem("relu_done")
        sq_done = ph.sem("sq_done")
        u_hi_done = ph.sem("u_hi_done")
        u_lo_done = ph.sem("u_lo_done")
        y_done = ph.sem("y_done")
        y_added = ph.sem("y_added")
        out_sent = ph.sem("out_sent")
        block = ph.block()

        def blocks(eng, body):
            with eng.Fori(0, BLOCKS // 2 - 1) as i:
                body(2 * i, 0, True)
                body(2 * i + 1, 1, True)
            body(BLOCKS - 2, 0, True)
            body(BLOCKS - 1, 1, False)

        def next_step(b, par, ch):
            if ch + 1 < NCH:
                return par, ch + 1, NCH * b + ch + 1
            return 1 - par, 0, NCH * b + ch + 1

        def u_slot(par, ch):
            return (NCH * par + ch) % 2

        @block.sync
        def _(sp):
            def load(b, q):
                if q < 2:
                    src = dram["w_up"][q * HALF * P:(q + 1) * HALF * P, ds(b * FBLK, FBLK)]\
                        .rearrange("(k p) f -> p k f", p=P)
                    dst = w_raw[:, q % 2, :].rearrange("p (k f) -> p k f", f=FBLK)
                else:
                    src = dram["w_down"][ds(b * FBLK + (q - 2) * P, P), :]
                    dst = w_raw[:, q % 2, :]
                sp.dma_start(dst, src).then_inc(w_loaded[q % 2], 16)

            for q in range(PIECES):
                if q >= 2:
                    sp.wait_ge(w_split, q - 1)
                load(0, q)
            with sp.Fori(0, BLOCKS - 1) as i:
                for q in range(PIECES):
                    sp.wait_ge(w_split, PIECES * (i + 1) + q - 1)
                    load(i + 1, q)
            for t in range(tiles):
                sp.wait_ge(y_added, 2 * (tiles * (BLOCKS - 1) + t + 1))
                sp.dma_start(dram["y"][(first + t) * P:(first + t + 1) * P, :], x1[:, t, :]).then_inc(out_sent, 16)
            sp.wait_ge(out_sent, 16 * tiles)

        @block.scalar
        def _(act):
            def hi_w(b, par):
                for q in range(PIECES):
                    act.wait_ge(w_loaded[q % 2], 16 * (2 * b + q // 2 + 1))
                    act.activation(w_hi[:, par, q, :], w_raw[:, q % 2, :], ACT.Copy).then_inc(w_hi_done, 1)

            def relu(s, par, ch):
                n = chunks[ch][1]
                act.wait_ge(up_done, s + 1)
                if not (isinstance(s, int) and s == 0):
                    act.wait_ge(sq_done, s)
                act.activation(r[:, :, 0:n], u_ps[u_slot(par, ch)][:, :, 0:n], ACT.Relu).then_inc(relu_done, 1)
                act.wait_ge(sq_done, s + 1)
                if not (isinstance(s, int) and s < 2):
                    act.wait_ge(y_done, tile_count(s, par, ch))
                act.activation(u_hi[:, u_slot(par, ch), :, 0:n], u[:, :, 0:n], ACT.Copy).then_inc(u_hi_done, 1)

            def body(b, par, more):
                for ch in range(NCH):
                    if ch == 0 and more:
                        act.wait_ge(y_done, tiles_before(b))
                        hi_w(b + 1, 1 - par)
                    if more or ch + 1 < NCH:
                        np_, nch, s = next_step(b, par, ch)
                        cur[0] = b
                        relu(s, np_, nch)

            cur = [0]

            def tiles_before(b):
                return tiles * b

            def tile_count(s, par, ch):
                b = cur[0]
                k = ch - 2
                nb = b if ch else b + 1
                while k < 0:
                    k += NCH
                    nb = nb - 1
                return tiles * nb + sum(x[2] for x in chunks[:k + 1])

            hi_w(0, 0)
            relu(0, 0, 0)
            cur[0] = 0

            def first_body():
                hi_w(1, 1)
                for ch in range(NCH):
                    np_, nch, s = next_step(0, 0, ch)
                    relu(s, np_, nch)

            first_body()
            body(1, 1, True)
            with act.Fori(1, BLOCKS // 2 - 1) as i:
                body(2 * i, 0, True)
                body(2 * i + 1, 1, True)
            body(BLOCKS - 2, 0, True)
            body(BLOCKS - 1, 1, False)

        @block.gpsimd
        def _(pool):
            def square(s, ch):
                n = chunks[ch][1]
                pool.wait_ge(relu_done, s + 1)
                if not (isinstance(s, int) and s == 0):
                    pool.wait_ge(u_lo_done, s)
                pool.tensor_tensor(u[:, :, 0:n], r[:, :, 0:n], r[:, :, 0:n], ALU.mult).then_inc(sq_done, 1)

            def body(b, par, more):
                for ch in range(NCH):
                    if more or ch + 1 < NCH:
                        _par, nch, s = next_step(b, par, ch)
                        square(s, nch)

            square(0, 0)
            blocks(pool, body)

        @block.vector
        def _(dve):
            def lo_w(b, par):
                for q in range(PIECES):
                    dve.wait_ge(w_hi_done, PIECES * b + q + 1)
                    dve.tensor_tensor(w_lo[:, par, q, :], w_raw[:, q % 2, :], w_hi[:, par, q, :].bitcast(F32),
                                      ALU.subtract).then_inc(w_split, 1)

            def lo_u(s, par, ch):
                n = chunks[ch][1]
                slot = u_slot(par, ch)
                dve.wait_ge(u_hi_done, s + 1)
                dve.tensor_tensor(u_lo[:, slot, :, 0:n], u[:, :, 0:n], u_hi[:, slot, :, 0:n].bitcast(F32),
                                  ALU.subtract).then_inc(u_lo_done, 1)

            def body(b, par, more):
                for ch, (_c0, n, nt) in enumerate(chunks):
                    if ch == 0 and more:
                        lo_w(b + 1, 1 - par)
                    if more or ch + 1 < NCH:
                        np_, nch, s = next_step(b, par, ch)
                        lo_u(s, np_, nch)
                    for m in range(nt):
                        t = 4 * ch + m
                        rows = min(n, P)
                        dve.wait_ge(y_done, tiles * b + t + 1)
                        for q in range(2):
                            part = x1[0:rows, t, q * D_G:(q + 1) * D_G]
                            dve.tensor_tensor(part, y_ps[(tiles * par + t) % 2][0:rows, q * D_G:(q + 1) * D_G], part,
                                              ALU.add).then_inc(y_added, 1)

            lo_w(0, 0)
            lo_u(0, 0, 0)
            blocks(dve, body)

        @block.tensor
        def _(pe):
            def up(s, par, ch):
                c0, n, _nt = chunks[ch]
                slot = u_slot(par, ch)
                if not (isinstance(s, int) and s < 2):
                    pe.wait_ge(relu_done, s - 1)
                for f in range(FB):
                    for k in range(KC):
                        a = slice((k % HALF) * FBLK + f * P, (k % HALF) * FBLK + (f + 1) * P)
                        out = u_ps[slot][:, f, 0:n]
                        hi, lo = w_hi[:, par, k // HALF, a], w_lo[:, par, k // HALF, a]
                        pe.matmul(out, hi, h_hi[:, k, c0:c0 + n], start=(k == 0), stop=False)
                        pe.matmul(out, hi, h_lo[:, k, c0:c0 + n], start=False, stop=False)
                        mm = pe.matmul(out, lo, h_hi[:, k, c0:c0 + n], start=False, stop=(k == KC - 1))
                mm.then_inc(up_done, 1)

            def down(b, par, ch, first_tiles):
                _c0, n, nt = chunks[ch]
                slot = u_slot(par, ch)
                pe.wait_ge(u_lo_done, NCH * b + ch + 1)
                for m in range(nt):
                    t = 4 * ch + m
                    rows = min(n, P)
                    out_ps = y_ps[(tiles * par + t) % 2]
                    if not (first_tiles and t < 2):
                        pe.wait_ge(y_added, 2 * (tiles * b + t - 1))
                    for q in range(2):
                        out = out_ps[0:rows, q * D_G:(q + 1) * D_G]
                        b_ = slice(q * D_G, (q + 1) * D_G)
                        for f in range(FB):
                            a = slice(m * P, m * P + rows)
                            hi, lo = u_hi[:, slot, f, a], u_lo[:, slot, f, a]
                            pe.matmul(out, hi, w_hi[:, par, 2 + f, b_], start=(f == 0), stop=False)
                            pe.matmul(out, hi, w_lo[:, par, 2 + f, b_], start=False, stop=False)
                            mm = pe.matmul(out, lo, w_hi[:, par, 2 + f, b_], start=False, stop=(f == FB - 1))
                    mm.then_inc(y_done, 1)

            def body(b, par, more):
                for ch in range(NCH):
                    if more or ch + 1 < NCH:
                        np_, nch, s = next_step(b, par, ch)
                        if nch == 0:
                            pe.wait_ge(w_split, PIECES * (b + 2))
                        up(s, np_, nch)
                    down(b, par, ch, isinstance(b, int) and b == 0)

            pe.wait_ge(w_split, PIECES)
            up(0, 0, 0)
            body(0, 0, True)
            body(1, 1, True)
            with pe.Fori(1, BLOCKS // 2 - 1) as i:
                body(2 * i, 0, True)
                body(2 * i + 1, 1, True)
            body(BLOCKS - 2, 0, True)
            body(BLOCKS - 1, 1, False)


def finish(nc, c, dram):
    for g, (first, tiles) in enumerate(((0, TILES // 2), (TILES // 2, TILES // 2 + 1))):
        with Phase(nc, f"fin{g}") as ph:
            tokens = min(tiles * P, TILES // 2 * P + N_SAMPLE)
            h_hi = ph.sb("h_hi", [P, KC, tokens], F32R)
            h_lo = ph.sb("h_lo", [P, KC, tokens], F32R)
            x1 = ph.sb("x1", [P, tiles, D_MODEL])
            join_heads(nc, c, dram, g, first, tiles, h_hi, h_lo, x1)
            mlp(nc, c, dram, g, first, tiles, h_hi, h_lo, x1)


def window(nc, c, dram):
    with Phase(nc, "window") as ph:
        moved = ph.sem("moved")
        block = ph.block()

        @block.sync
        def _(sp):
            n = 0
            for new, old, fresh in (("new_win_k", "win_k", "k_b"), ("new_win_v", "win_v", "v_b")):
                for b in range(DEC_BATCH):
                    sp.dma_start(dram[new][b, 0:PAST - DEC_SEQ, :], dram[old][b, DEC_SEQ:PAST, :]).then_inc(moved, 16)
                sp.dma_start(dram[new][:, PAST - DEC_SEQ:PAST, :],
                             dram[fresh][SEQ:SEQ + N_SAMPLE, :].rearrange("(b q) d -> b q d", q=DEC_SEQ))\
                    .then_inc(moved, 16)
                n += DEC_BATCH + 1
            sp.wait_ge(moved, 16 * n)


def build(nc, dram, phases="ABCDWE"):
    with Phase(nc, "all") as ph:
        c = {"ident": ph.sb("ident", [P, P]), "mask": ph.sb("mask", [P, 2 * P]),
             "logf": ph.sb("logf", [P, N_TILES * HEADS])}
        load_constants(nc, c, dram)
        if "A" in phases:
            project(nc, c, dram)
        if "B" in phases:
            attend(nc, c, dram, False)
        if "C" in phases:
            attend(nc, c, dram, True)
        if "D" in phases:
            sample_attend(nc, c, dram, False)
            sample_attend(nc, c, dram, True)
        if "W" in phases:
            window(nc, c, dram)
        if "E" in phases:
            finish(nc, c, dram)


def shape_constants():
    i = np.arange(P)
    f = np.float32
    causal = np.where(i[None, :] <= i[:, None], f(0), f(NEG))
    window = np.where(i[None, :] >= i[:, None], f(0), f(NEG))
    half = 8
    inv = f(500000.0) ** (-np.arange(half, dtype=f) / f(half))
    pos = np.concatenate([np.arange(SEQ), PAST + np.tile(np.arange(DEC_SEQ), DEC_BATCH),
                          np.zeros(ROWS - SEQ - N_SAMPLE, int)]).astype(f)
    ang = (pos[:, None] * inv[None, :]).astype(f).astype(np.float64)
    cos, sin = np.cos(ang).astype(f), np.sin(ang).astype(f)
    row = np.arange(DEC_BATCH // 4 * HEADS * DEC_SEQ)
    q = row % DEC_SEQ
    m = np.arange(P)
    pos = [16 * m + r for r in range(8)]
    pos += [PAST - 512 + 16 * (m // 4) + 8 + 2 * (m % 4) + b for b in range(2)]
    pos = np.concatenate(pos + [PAST + np.arange(DEC_SEQ)])
    back = PAST + q[:, None] - pos[None, :]
    reach = sum(((back >= 0) & (back % d == 0) & (back <= w)).astype(f) for w, d in ((128, 1), (512, 4), (2048, 16)))
    return {
        "reach": reach,
        "unreached": np.where(reach > 0, f(0), f(NEG)),
        "own": (row[:, None] // DEC_SEQ % HEADS == np.arange(HEADS)[None, :]).astype(f),
        "causal_new": np.where(np.arange(DEC_SEQ)[None, :] <= q[:, None], f(0), f(NEG)),
        "after": (i[:, None] > i[None, :]).astype(f),
        "ident": np.eye(P, dtype=f),
        "mask": np.concatenate([window, causal], 1),
        "upto": (i[:, None] <= i[None, :]).astype(f),
        "rope_cos": np.concatenate([cos, cos], 1),
        "rope_sin": np.concatenate([-sin, sin], 1),
    }


def layout(inputs):
    a = {k: np.asarray(v) for k, v in inputs.items()}
    out = {
        "x": np.concatenate([a["x_prompt"].reshape(SEQ, D_MODEL), a["x_sample"].reshape(N_SAMPLE, D_MODEL),
                             np.zeros((ROWS - SEQ - N_SAMPLE, D_MODEL), np.float32)]),
        "g_attn": a["g_attn"][0].reshape(KC, P).T,
        "g_mlp": a["g_mlp"][0].reshape(KC, P).T,
        "cache_k": a["cache_k"][0].reshape(-1, PAGE, D_G),
        "cache_v": a["cache_v"][0].reshape(-1, PAGE, D_G),
        "cache_logf": a["cache_logf"][0],
        "win_k": a["state_win_k"][0].reshape(DEC_BATCH, PAST, D_G),
        "win_v": a["state_win_v"][0].reshape(DEC_BATCH, PAST, D_G),
        "page_table": a["page_table"].reshape(1, -1).astype(np.int32),
    }
    for name in ("w_in", "b_f", "g_qa", "g_ka", "g_qb", "g_kb", "w_o", "w_up", "w_down"):
        out[name] = a[name][0]
    out.update(shape_constants())
    return {k: np.ascontiguousarray(v) for k, v in out.items()}


OUTS = {
    "y": (ROWS, D_MODEL),
    "k_a": (ROWS, D_G), "v_a": (ROWS, D_G), "logf": (ROWS, HEADS), "k_b": (ROWS, D_G), "v_b": (ROWS, D_G),
    "new_win_k": (DEC_BATCH, PAST, D_G), "new_win_v": (DEC_BATCH, PAST, D_G),
}
SCRATCH = {"q_a": (ROWS, D_G), "q_b": (ROWS, D_G), "att": (ROWS, D_MODEL),
           "dil": (3, SEQ, HEADS * (HD + 2)), "x1": (ROWS, D_MODEL)}


def kernel(**inputs):
    import concourse.bacc as bacc
    from concourse.bass_utils import run_bass_kernel_spmd

    nc = bacc.Bacc("TRN2", target_bir_lowering=False, num_devices=1)
    arrays = layout(inputs)
    dram = {n: nc.dram_tensor(f"in_{n}", v.shape, mybir.dt.from_np(v.dtype), kind="ExternalInput").ap()
            for n, v in arrays.items()}
    for n, shape in OUTS.items():
        dram[n] = nc.dram_tensor(f"out_{n}", shape, F32, kind="ExternalOutput").ap()
    for n, shape in SCRATCH.items():
        dram[n] = nc.dram_tensor(f"scratch_{n}", shape, F32).ap()
    build(nc, dram)
    r = run_bass_kernel_spmd(nc, [{f"in_{n}": v for n, v in arrays.items()}], core_ids=[0])
    got = {n: np.asarray(r.results[0][f"out_{n}"]) for n in OUTS}

    def prompt(name, *shape):
        return got[name][:SEQ].reshape(shape)

    def sampled(name, *shape):
        return got[name][SEQ:SEQ + N_SAMPLE].reshape(shape)

    sp = (1, 1, SEQ, HEADS, HD)
    ss = (1, DEC_BATCH, DEC_SEQ, HEADS, HD)
    sw = (1, DEC_BATCH, PAST, HEADS, HD)
    return (prompt("y", 1, SEQ, D_MODEL), sampled("y", DEC_BATCH, DEC_SEQ, D_MODEL),
            prompt("k_a", *sp), prompt("v_a", *sp), prompt("logf", *sp[:4]), prompt("k_b", *sp), prompt("v_b", *sp),
            sampled("k_a", *ss), sampled("v_a", *ss), sampled("logf", *ss[:4]),
            got["new_win_k"].reshape(sw), got["new_win_v"].reshape(sw))
```

```python
from contextlib import ExitStack

import numpy as np

import concourse.bass as bass
from concourse import mybir

F32 = mybir.dt.float32
F32R = mybir.dt.float32r
I32 = mybir.dt.int32
ALU = mybir.AluOpType
ACT = mybir.ActivationFunctionType
AX_X = mybir.AxisListType.X
ds = bass.ds

P = 128
D_MODEL = 1024
SEQ = 2048
DEC_BATCH = 8
DEC_SEQ = 8
PAST = 2048
PAGE = 128
HD = 64
HEADS = 8
D_G = HEADS * HD
D_FF = 4 * D_MODEL
KC = D_MODEL // P
TILES = SEQ // P
N_TILES = TILES + 1
ROWS = N_TILES * P
N_SAMPLE = DEC_BATCH * DEC_SEQ
N_FA = HEADS
EPS = 1e-6
NEG = -1e30
FBLK = 256


class Phase:

    def __init__(self, nc, name):
        self.nc, self.name, self.ctx, self.held = nc, name, ExitStack(), []

    def __enter__(self):
        return self

    def __exit__(self, *said):
        ended = self.ctx.__exit__(*said)
        if self.held and said[0] is None:
            self.nc.clear_and_free_semaphores(self.held)
            self.nc.all_engine_barrier()
        return ended

    def sb(self, name, shape, dt=F32):
        return self.ctx.enter_context(self.nc.sbuf_tensor(f"{self.name}_{name}", shape, dt))

    def ps(self, name, shape, dt=F32):
        return self.ctx.enter_context(self.nc.psum_tensor(f"{self.name}_{name}", shape, dt))

    def sem(self, name):
        self.held.append(self.nc.alloc_semaphore(f"{self.name}_{name}"))
        return self.held[-1]

    def sems(self, name, n=2):
        return [self.sem(f"{name}{i}") for i in range(n)]

    def block(self):
        return self.ctx.enter_context(self.nc.Block())


def load_constants(nc, c, dram):
    with Phase(nc, "const") as ph:
        loaded = ph.sem("loaded")
        block = ph.block()

        @block.sync
        def _(sp):
            pairs = [(c["ident"][:, :], dram["ident"]), (c["mask"][:, :], dram["mask"])]
            for dst, src in pairs:
                sp.dma_start(dst, src).then_inc(loaded, 16)
            sp.wait_ge(loaded, 16 * len(pairs))


PASS_COLS = 2 * D_G
W_COLS = PASS_COLS + N_FA


def project(nc, c, dram):
    w_in = dram["w_in"]
    pieces = [[(0, 0, PASS_COLS)],
              [(0, 3 * D_G, PASS_COLS)],
              [(0, 2 * D_G, D_G), (D_G, 5 * D_G, D_G + N_FA)]]
    dests = [(dram["q_a"], dram["k_a"]), (dram["q_b"], dram["k_b"]), (dram["v_a"], dram["v_b"])]
    PAIRS = TILES // 2

    with Phase(nc, "proj") as ph:
        w_in_slot = ph.sb("w_raw", [P, 2, W_COLS])
        w_hi = ph.sb("w_hi", [P, 2, KC * W_COLS], F32R)
        w_lo = ph.sb("w_lo", [P, 2, KC * W_COLS], F32R)
        x_in = ph.sb("x_in", [P, 2, D_MODEL])
        xg = ph.sb("xg", [P, D_MODEL])
        x_hi = ph.sb("x_hi", [P, 2, D_MODEL], F32R)
        x_lo = ph.sb("x_lo", [P, 2, D_MODEL], F32R)
        z = ph.sb("z", [P, 2, PASS_COLS])
        sq = ph.sb("sq", [P, PASS_COLS])
        junk = ph.sb("junk", [P, D_MODEL])
        w_raw = [w_in_slot[:, 0, :], w_in_slot[:, 1, :], sq[:, :], junk[:, :]]
        W_SLOTS = len(w_raw)
        gains = ph.sb("gains", [P, 2, 2, HD])
        g_attn = ph.sb("g_attn", [P, KC])
        b_f = ph.sb("b_f", [P, N_FA])
        rope = ph.sb("rope", [P, 2, N_TILES, 16])
        turn = ph.sb("turn", [P, 2, 16, 16])
        sums = ph.sb("sums", [P, N_TILES])
        mean = ph.sb("mean", [P, N_TILES])
        rstd = ph.sb("rstd", [P, N_TILES])
        head_sum = ph.sb("head_sum", [P, 16])
        head_mean = ph.sb("head_mean", [P, 16])
        head_rstd = ph.sb("head_rstd", [P, 16])
        minus_half = ph.sb("minus_half", [P, 16])
        fa = ph.sb("fa", [P, N_TILES * N_FA])
        lf_t = ph.sb("lf_t", [P, 5, N_TILES * N_FA])
        t_ps = [ph.ps(f"t{j}", [P, D_MODEL]) for j in range(2)]
        z_ps = [ph.ps(f"z{j}", [P, PASS_COLS]) for j in range(2)]

        consts = ph.sem("consts")
        pool_set = ph.sem("pool_set")
        w_loaded = ph.sems("w_loaded", 4)
        w_hi_done = ph.sem("w_hi_done")
        w_split = ph.sem("w_split")
        x_loaded = ph.sems("x_loaded")
        x_turned = ph.sem("x_turned")
        squared = ph.sem("squared")
        mean_done = ph.sem("mean_done")
        rstd_done = ph.sem("rstd_done")
        xg_done = ph.sem("xg_done")
        hi_done = ph.sem("hi_done")
        lo_done = ph.sem("lo_done")
        product = ph.sem("product")
        z_out = ph.sem("z_out")
        fa_out = ph.sem("fa_out")
        sq_z = ph.sem("sq_z")
        hsum = ph.sem("hsum")
        hmean = ph.sem("hmean")
        hrstd = ph.sem("hrstd")
        z_normed = ph.sem("z_normed")
        z_gained = ph.sem("z_gained")
        turned = ph.sem("turned")
        z_final = ph.sem("z_final")
        z_sent = ph.sems("z_sent")
        lf = ph.sem("lf")
        lf_exp = ph.sem("lf_exp")
        lf_sent = ph.sem("lf_sent")
        block = ph.block()

        def at(p, i, j):
            k = N_TILES * p + j
            return k + 2 * i, k % 2, k // 2 + i

        def w_slot(p, k):
            return k % W_SLOTS if p == 0 else 0

        def w_arrived(eng, p, k):
            if p == 0:
                eng.wait_ge(w_loaded[k % W_SLOTS], 16 * (k // W_SLOTS + 1))
            elif p == 1:
                eng.wait_ge(w_loaded[0], 16 * (KC // W_SLOTS + 1 + k))
            else:
                eng.wait_ge(w_loaded[0], 16 * (KC // W_SLOTS + KC + 2 + 2 * k))

        def w_part(w, p, k):
            return w[:, p % 2, ds(k * W_COLS, W_COLS if p == 2 else PASS_COLS)]

        @block.sync
        def _(sp):
            def load_w(p, k):
                for d0, s0, n in pieces[p]:
                    sp.dma_start(w_raw[w_slot(p, k)][:, d0:d0 + n], w_in[ds(k * P, P), s0:s0 + n])\
                        .then_inc(w_loaded[w_slot(p, k)], 16)

            def load_x(t, p, i, j):
                n, slot, _use = at(p, i, j)
                sp.wait_ge(x_turned, n + 1)
                if p == 0:
                    sp.wait_ge(squared, n + 1)
                elif p == 1:
                    sp.wait_ge(squared, N_TILES + 2)
                sp.dma_start(x_in[:, slot, :], dram["x"][ds(t * P, P), :]).then_inc(x_loaded[slot], 16)

            sp.sem_inc(x_turned, 2)
            sp.sem_inc(squared, 2)
            for slot in range(2):
                sp.sem_inc(z_sent[slot], 32)
            load_x(0, 0, 0, 0)
            for k in range(W_SLOTS):
                load_w(0, k)
            sp.dma_start(g_attn[:, :], dram["g_attn"]).then_inc(consts, 16)
            sp.dma_start(b_f[:, :], dram["b_f"].partition_broadcast(P)).then_inc(consts, 16)
            for n, name in enumerate(("g_qa", "g_ka", "g_qb", "g_kb")):
                sp.dma_start(gains[:, n // 2, n % 2, :],
                             dram[name].partition_broadcast(P)).then_inc(consts, 16)
            for n, name in enumerate(("rope_cos", "rope_sin")):
                sp.dma_start(rope[:, n, :, :],
                             dram[name].rearrange("(t p) d -> p t d", p=P)).then_inc(consts, 16)
            for k in range(W_SLOTS, KC):
                sp.wait_ge(w_split, k - W_SLOTS + 1)
                load_w(0, k)
            load_x(1, 0, 0, 1)
            for p in range(3):
                with sp.Fori(0, PAIRS - 1) as i:
                    for j in range(2):
                        load_x(2 * i + j + 2, p, i, j + 2)
                    if p < 2:
                        sp.wait_ge(w_split, KC * (p + 1) + i)
                        load_w(p + 1, i)
                load_x(TILES, p, PAIRS, 0)
                if p < 2:
                    sp.wait_ge(w_split, KC * (p + 1) + PAIRS - 1)
                    load_w(p + 1, PAIRS - 1)
                if p < 2:
                    load_x(0, p, PAIRS, 1)
                    load_x(1, p, PAIRS, 2)
            sp.wait_ge(lf, 15)
            sp.dma_start(dram["logf"].rearrange("(t p) h -> p t h", p=P),
                         c["logf"][:, :].rearrange("p (t h) -> p t h", h=HEADS)).then_inc(lf_sent, 16)
            sp.wait_ge(lf_sent, 16)

        @block.scalar
        def _(act):
            def hi_w(p, k):
                w_arrived(act, p, k)
                act.activation(w_part(w_hi, p, k), w_raw[w_slot(p, k)][:, 0:W_COLS if p == 2 else PASS_COLS],
                               ACT.Copy).then_inc(w_hi_done, 1)

            def hi_x(p, i, j):
                n, slot, use = at(p, i, j)
                if p == 0:
                    act.wait_ge(x_loaded[slot], 16 * (use + 1))
                    act.wait_ge(squared, n + 2)
                    act.activation(junk[:, :], x_in[:, slot, :], ACT.Square,
                                   accum_out=sums[:, ds(2 * i + j, 1)]).then_inc(squared, 1)
                act.wait_ge(xg_done, 2 * (n + 1))
                act.wait_ge(product, n + 1)
                act.activation(x_hi[:, slot, :], xg[:, :], ACT.Copy).then_inc(hi_done, 1)

            def scale(p, i, j):
                n, slot, use = at(p, i, j)
                if p == 0:
                    act.wait_ge(rstd_done, n + 1)
                act.wait_ge(product, n + 3)
                act.wait_ge(z_sent[slot], 32 * (use + 1))
                for q in range(2):
                    act.activation(z[:, slot, q * D_G:(q + 1) * D_G], z_ps[slot][:, q * D_G:(q + 1) * D_G],
                                   ACT.Copy, scale=rstd[:, ds(2 * i + j, 1)]).then_inc(z_out, 1)
                if p < 2:
                    act.wait_ge(z_out, 4 + 2 * (n + 1))
                    act.wait_ge(hsum, n + 1)
                    for q in range(2):
                        act.activation(sq[:, q * D_G:(q + 1) * D_G], z[:, slot, q * D_G:(q + 1) * D_G],
                                       ACT.Square).then_inc(sq_z, 1)

            def store(p, i, j):
                n, slot, _use = at(p, i, j)
                act.wait_ge(z_final if p < 2 else z_out, n + 1 if p < 2 else 4 + 2 * (n + 1))
                for q in range(2):
                    act.dma_start(dests[p][q][ds((2 * i + j) * P, P), :],
                                 z[:, slot, q * D_G:(q + 1) * D_G]).then_inc(z_sent[slot], 16)

            act.sem_inc(z_out, 4)
            for k in range(KC):
                hi_w(0, k)
            act.wait_ge(w_split, KC)
            hi_x(0, 0, 0)

            def step(p, i, j, last=False):
                if not last:
                    hi_x(p, i, j + 1)
                elif p < 2:
                    hi_next(p)
                if not isinstance(i, int) or 2 * i + j >= 2:
                    store(p, i, j - 2)
                elif p > 0:
                    store(p - 1, PAIRS, j - 1)
                scale(p, i, j)

            def hi_next(p):
                n, slot, _use = at(p, PAIRS, 1)
                act.wait_ge(xg_done, 2 * (n + 1))
                act.wait_ge(product, n + 1)
                act.activation(x_hi[:, slot, :], xg[:, :], ACT.Copy).then_inc(hi_done, 1)

            for p in range(3):
                step(p, 0, 0)
                step(p, 0, 1)
                with act.Fori(0, PAIRS - 1) as i:
                    step(p, i, 2)
                    if p < 2:
                        hi_w(p + 1, i)
                    step(p, i, 3)
                if p < 2:
                    hi_w(p + 1, PAIRS - 1)
                step(p, PAIRS, 0, last=True)
            store(2, PAIRS, -1)
            store(2, PAIRS, 0)
            uses = 3 * N_TILES
            act.wait_ge(z_sent[0], 32 + 32 * ((uses + 1) // 2))
            act.wait_ge(z_sent[1], 32 + 32 * (uses // 2))
            act.wait_ge(lf, 2)
            act.activation(lf_t[:, 1, :], lf_t[:, 0, :], ACT.Exp).then_inc(lf_exp, 1)

        @block.gpsimd
        def _(pool):
            pool.sem_inc(lo_done, 1)
            pool.memset(minus_half[:, :], -0.5).then_inc(pool_set, 1)
            pool.wait_ge(consts, 16 * 8)
            for g in range(2):
                pool.tensor_scalar(gains[:, g, 0, :], gains[:, g, 0, :], HD ** -0.5, None,
                                   ALU.mult).then_inc(pool_set, 1)
            pool.wait_ge(pool_set, 3)

            def lo_x(p, i, j, new_pass=False):
                n, slot, _use = at(p, i, j)
                if p == 0 and not new_pass:
                    pool.wait_ge(mean_done, n + 1)
                    pool.tensor_tensor(rstd[:, ds(2 * i + j, 1)], mean[:, ds(2 * i + j, 1)],
                                       minus_half[:, 0:1], ALU.pow).then_inc(rstd_done, 1)
                pool.wait_ge(hi_done, n + 1)
                pool.tensor_tensor(x_lo[:, slot, :], xg[:, :], x_hi[:, slot, :].bitcast(F32),
                                   ALU.subtract).then_inc(lo_done, 1)

            def norm(p, i, j):
                n, slot, _use = at(p, i, j)
                zs = z[:, slot, :]
                pool.wait_ge(z_out, 4 + 2 * (n + 1))
                pool.wait_ge(hmean, n + 1)
                pool.tensor_tensor(head_rstd[:, :], head_mean[:, :], minus_half[:, :],
                                   ALU.pow).then_inc(hrstd, 1)
                pool.wait_ge(z_normed, n + 1)
                for q in range(2):
                    part = zs[:, q * D_G:(q + 1) * D_G].rearrange("p (h d) -> p h d", d=HD)
                    last = q == 1 and p == 0
                    op = pool.tensor_tensor(part, part, gains[:, p, q:q + 1, :].to_broadcast([P, HEADS, HD]),
                                            ALU.mult)
                    op.then_inc(z_final if last else z_gained, 1)
                if p == 0:
                    return
                m = n - N_TILES
                pool.wait_ge(z_gained, N_TILES + 2 * (m + 1))
                zh = zs.rearrange("p (h d) -> p h d", d=HD)

                def table(a, d0, d1):
                    return rope[:, a, ds(2 * i + j, 1), d0:d1].to_broadcast([P, 16, d1 - d0])

                pool.tensor_tensor(turn[:, 0, :, :], zh[:, :, 0:16], table(0, 0, 16), ALU.mult).then_inc(turned, 1)
                pool.tensor_tensor(turn[:, 1, :, 0:8], zh[:, :, 8:16], table(1, 0, 8), ALU.mult).then_inc(turned, 1)
                pool.tensor_tensor(turn[:, 1, :, 8:16], zh[:, :, 0:8], table(1, 8, 16), ALU.mult)\
                    .then_inc(turned, 1)
                pool.wait_ge(turned, 3 * (m + 1))
                pool.tensor_tensor(zh[:, :, 0:16], turn[:, 0, :, :], turn[:, 1, :, :], ALU.add)\
                    .then_inc(z_final, 1)

            lo_x(0, 0, 0)
            lo_x(0, 0, 1)
            for p in range(3):
                with pool.Fori(0, PAIRS - 1) as i:
                    for j in range(2):
                        lo_x(p, i, j + 2)
                        if p < 2:
                            norm(p, i, j)
                lo_x(p, PAIRS - 1, 2)
                if p < 2:
                    norm(p, PAIRS - 1, 0)
                    for j in (1, 2):
                        lo_x(p, PAIRS - 1, j + 2, new_pass=True)
                        norm(p, PAIRS - 1, j)

        @block.vector
        def _(dve):
            def lo_w(p, k):
                dve.wait_ge(w_hi_done, KC * p + k + 1)
                dve.tensor_tensor(w_part(w_lo, p, k), w_raw[w_slot(p, k)][:, 0:W_COLS if p == 2 else PASS_COLS],
                                  w_part(w_hi, p, k).bitcast(F32), ALU.subtract).then_inc(w_split, 1)

            def gain_x(p, i, j):
                n, slot, _use = at(p, i, j)
                dve.wait_ge(x_turned, n + 3)
                dve.wait_ge(lo_done, n + 1)
                for q in range(2):
                    dve.tensor_tensor(xg[:, q * 512:(q + 1) * 512].rearrange("p (k m) -> p k m", m=P),
                                      t_ps[slot][:, q * 512:(q + 1) * 512].rearrange("p (k m) -> p k m", m=P),
                                      g_attn[:, 4 * q:4 * q + 4].unsqueeze(2).to_broadcast([P, 4, P]),
                                      ALU.mult).then_inc(xg_done, 1)

            def mean_x(p, i, j):
                if p > 0:
                    return
                n, _slot, _use = at(p, i, j)
                dve.wait_ge(squared, n + 3)
                dve.tensor_scalar(mean[:, ds(2 * i + j, 1)], sums[:, ds(2 * i + j, 1)], 1.0 / D_MODEL, EPS,
                                  ALU.mult, ALU.add).then_inc(mean_done, 1)

            def heads(p, i, j):
                n, slot, _use = at(p, i, j)
                if p == 2:
                    dve.wait_ge(product, n + 3)
                    dve.scalar_tensor_tensor(fa[:, ds((2 * i + j) * N_FA, N_FA)], t_ps[slot][:, 0:N_FA],
                                             rstd[:, ds(2 * i + j, 1)], b_f[:, :], ALU.mult, ALU.add)\
                        .then_inc(fa_out, 1)
                    return
                dve.wait_ge(sq_z, 2 * (n + 1))
                dve.tensor_reduce(head_sum[:, :], sq[:, :].rearrange("p (h d) -> p h d", d=HD),
                                  AX_X, ALU.add).then_inc(hsum, 1)
                dve.wait_ge(hsum, n + 2)
                dve.tensor_scalar(head_mean[:, :], head_sum[:, :], 1.0 / HD, EPS, ALU.mult, ALU.add)\
                    .then_inc(hmean, 1)
                dve.wait_ge(hrstd, n + 1)
                zh = z[:, slot, :].rearrange("p (h d) -> p h d", d=HD)
                dve.tensor_tensor(zh, zh, head_rstd[:, :].unsqueeze(2).to_broadcast([P, 16, HD]), ALU.mult)\
                    .then_inc(z_normed, 1)

            dve.sem_inc(fa_out, 2)
            dve.sem_inc(hsum, 1)
            for k in range(KC):
                lo_w(0, k)
            dve.wait_ge(consts, 16 * 8)
            for j in range(2):
                gain_x(0, 0, j)
                mean_x(0, 0, j)

            def step(p, i, j, new_pass=False):
                if p == 2:
                    heads(p, i, j)
                if not (new_pass and p == 2):
                    gain_x(p, i, j + 2)
                if not new_pass:
                    mean_x(p, i, j + 2)
                if p < 2:
                    heads(p, i, j)

            for p in range(3):
                with dve.Fori(0, PAIRS - 1) as i:
                    for j in range(2):
                        step(p, i, j)
                    if p < 2:
                        lo_w(p + 1, i)
                for j in range(3):
                    step(p, PAIRS - 1, j, new_pass=j > 0)
                    if p < 2 and j == 1:
                        lo_w(p + 1, PAIRS - 1)

            step = [0]

            def chain(op):
                op.then_inc(lf, 1)
                step[0] += 1
                dve.wait_ge(lf, step[0])

            t = [lf_t[:, a, :] for a in range(5)]
            dve.wait_ge(fa_out, 2 + N_TILES)
            chain(dve.tensor_scalar(t[2], fa[:, :], -1.0, None, ALU.mult))
            chain(dve.tensor_tensor(t[0], fa[:, :], t[2], ALU.min))
            dve.wait_ge(lf_exp, 1)
            chain(dve.tensor_scalar(t[2], t[1], 2.0, None, ALU.add))
            chain(dve.reciprocal(t[3], t[2]))
            chain(dve.tensor_tensor(t[2], t[1], t[3], ALU.mult))
            chain(dve.tensor_tensor(t[3], t[2], t[2], ALU.mult))
            chain(dve.tensor_scalar(t[4], t[3], 2.0 / 15, None, ALU.mult))
            for k in (13, 11, 9, 7, 5, 3):
                chain(dve.scalar_tensor_tensor(t[4], t[4], 2.0 / k, t[3], ALU.add, ALU.mult))
            chain(dve.scalar_tensor_tensor(t[4], t[4], 2.0, t[2], ALU.add, ALU.mult))
            chain(dve.scalar_tensor_tensor(c["logf"][:, :], fa[:, :], 0.0, t[4], ALU.min, ALU.subtract))

        @block.tensor
        def _(pe):
            def turn_x(p, i, j):
                n, slot, use = at(p, i, j)
                pe.wait_ge(x_loaded[slot], 16 * (use + 1))
                if isinstance(n, int) and n < 2:
                    pass
                elif p == 2:
                    pe.wait_ge(fa_out, n - 2 * N_TILES + 1)
                for k in range(KC):
                    mm = pe.transpose(t_ps[slot][:, k * P:(k + 1) * P], x_in[:, slot, k * P:(k + 1) * P],
                                      c["ident"][:, :])
                mm.then_inc(x_turned, 1)

            def products(p, i, j):
                n, slot, _use = at(p, i, j)
                pe.wait_ge(hi_done, n + 1)
                pe.wait_ge(lo_done, n + 2)
                pe.wait_ge(z_out, 2 * (n + 1))
                halves = [(z_ps[slot][:, q * D_G:(q + 1) * D_G], q * D_G, D_G) for q in range(2)]
                if p == 2:
                    halves.append((t_ps[slot][:, 0:N_FA], PASS_COLS, N_FA))
                for out, w0, cols in halves:
                    for k in range(KC):
                        xs = slice(k * P, (k + 1) * P)
                        ws = slice(k * W_COLS + w0, k * W_COLS + w0 + cols)
                        pe.matmul(out, x_hi[:, slot, xs], w_hi[:, p % 2, ws], start=(k == 0), stop=False)
                        pe.matmul(out, x_hi[:, slot, xs], w_lo[:, p % 2, ws], start=False, stop=False)
                        mm = pe.matmul(out, x_lo[:, slot, xs], w_hi[:, p % 2, ws], start=False,
                                       stop=(k == KC - 1))
                mm.then_inc(product, 1)

            pe.sem_inc(product, 2)
            turn_x(0, 0, 0)
            for p in range(3):
                pe.wait_ge(w_split, KC * (p + 1))
                with pe.Fori(0, PAIRS) as i:
                    for j in range(2):
                        turn_x(p, i, j + 1)
                        products(p, i, j)
                if p < 2:
                    turn_x(p, PAIRS, 1)
                products(p, PAIRS, 0)


PT_BANKS = 3
PT_SLOTS = 4
O_SLOTS = 4
MAX_SLOTS = 8
S_COLS = 2048
HEAD_GROUPS = 2 * TILES // 4


class Count:

    def __init__(self, sem, n):
        self.sem, self.n = sem, n

    def start(self, eng):
        eng.sem_inc(self.sem, 2 * self.n)

    def wait(self, eng, h, k):
        eng.wait_ge(self.sem, self.n * h + 2 * self.n + k + 1)


def last_user(used, k):
    for back in range(1, len(used) + 1):
        if used[(k - back) % len(used)] & used[k]:
            return k - back
    raise ValueError("nothing used it")


def forgetting_steps():
    steps = []
    for i in range(TILES):
        w = (i + 1) * P
        steps.append([dict(q0=i * P, d=1, k0=0, w=w, p=(i % 2) * S_COLS, v=list(range(i + 1)), o=i)])
    return steps


def dilated_units():
    units, base = [], 0
    for d in (1, 4, 16):
        nb = SEQ // d // P
        for r in range(d):
            for n in range(nb):
                at = base + r * nb + n
                q0 = n * P * d + r
                if n:
                    units.append(dict(q0=q0, d=d, k0=q0 - P * d, w=2 * P, v=[at - 1, at], o=at))
                else:
                    units.append(dict(q0=q0, d=d, k0=q0, w=P, v=[at], o=at))
        base += TILES
    return units


def dilated_steps():
    units = dilated_units()
    steps = []
    for w in (P, 2 * P):
        kind = [u for u in units if u["w"] == w]
        steps += [kind[k:k + 512 // w] for k in range(0, len(kind), 512 // w)]
    for s, step in enumerate(steps):
        for k, u in enumerate(step):
            u["p"] = (s % 4) * 512 + k * u["w"]
    return steps


def attend(nc, c, dram, dilated):
    steps = dilated_steps() if dilated else forgetting_steps()
    branches = 3 if dilated else 1
    NS = len(steps)
    row = HD + 2 if dilated else HD
    names = ("q_b", "k_b", "v_b") if dilated else ("q_a", "k_a", "v_a")

    pieces, first_piece = [], []
    for s, step in enumerate(steps):
        width = sum(u["w"] for u in step)
        first_piece.append(len(pieces))
        pieces += [(s, x, min(512, width - x)) for x in range(0, width, 512)]
    NQ = len(pieces)
    n_pieces = [sum(q[0] == s for q in pieces) for s in range(NS)]
    first_piece.append(NQ)

    groups = []
    first_group, last_group = [], []
    for s, step in enumerate(steps):
        blocks = [(u, b) for u in range(len(step)) for b in range(step[u]["w"] // P)]
        first_group.append(len(groups))
        groups += [(s, blocks[k:k + 4]) for k in range(0, len(blocks), 4)]
        last_group.append(len(groups) - 1)
    NG = len(groups)
    copier = [k % 2 for k in range(HEAD_GROUPS)]
    for s in range(NS):
        n = last_group[s] - first_group[s] + 1
        copier += [0 if k < (n + 1) // 2 else 1 for k in range(n)]
    copied_at = [copier[:k].count(copier[k]) for k in range(len(copier))]
    NB = len(copier)
    LOOK = 3 if dilated else 1
    LOOK_EXP = 2 if dilated else 1

    s_used = [{q % 4} for q in range(NQ)]
    p_used = [{x // P for u in step for x in range(u["p"], u["p"] + u["w"], P)} for step in steps]
    m_used = [{s % MAX_SLOTS} for s in range(NS)]
    t_used = [{b % PT_BANKS} for b in range(NB)]
    pT_used = [{g % PT_SLOTS} for g in range(NG)]
    o_used = [{0} for s in range(NS)]

    with Phase(nc, "dil" if dilated else "fox") as ph:
        q_in = ph.sb("q_in", [P, 2, TILES, P])
        k_in = ph.sb("k_in", [P, 2, TILES, P])
        v_in = ph.sb("v_in", [P, 2, branches * TILES, P])
        qT = ph.sb("qT", [P, 2, SEQ])
        kT = ph.sb("kT", [P, 2, SEQ])
        p_sb = ph.sb("p", [P, 2 * S_COLS])
        pT = ph.sb("pT", [P, PT_SLOTS, 4 * P])
        o_sb = ph.sb("o_sb", [P, 2, branches * TILES, row])
        nmax = ph.sb("nmax", [P, MAX_SLOTS, O_SLOTS])
        piece_nmax = ph.sb("piece_nmax", [P, MAX_SLOTS, 4])
        rden = ph.sb("rden", [P, 4])
        s_ps = ph.ps("s", [P, S_COLS])
        t_ps = [ph.ps(f"t{k}", [P, 4 * P]) for k in range(PT_BANKS)]
        o_ps = ph.ps("o", [P, O_SLOTS, P])

        set_up = ph.sem("set_up")
        qk_loaded = ph.sems("qk_loaded")
        v_loaded = ph.sems("v_loaded")
        sums = ph.sem("sums")
        summed = ph.sem("summed")
        decayed = Count(ph.sem("decayed"), 1)
        turned = Count(ph.sem("turned"), NB)
        copied = [Count(ph.sem("copied_act"), copier.count(0)), Count(ph.sem("copied_dve"), copier.count(1))]
        scored = Count(ph.sem("scored"), NQ)
        masked = Count(ph.sem("masked"), NS)
        piece_maxed = Count(ph.sem("piece_maxed"), sum(n for n in n_pieces if n > 1))
        maxed = Count(ph.sem("maxed"), NS)
        exped = Count(ph.sem("exped"), NQ)
        pv = Count(ph.sem("pv"), NG)
        inverted = Count(ph.sem("inverted"), NS)
        posted = Count(ph.sem("posted"), NS)
        o_sent = ph.sems("o_sent")
        moved = ph.sem("moved")
        if not dilated:
            upto = ph.sb("upto", [P, P])
            ones = ph.sb("ones", [P, P])
            before = ph.sb("before", [P, TILES * HEADS])
            neg_c = ph.sb("neg_c", [P, TILES, HEADS])
            c_loaded = ph.sem("c_loaded")
            table = ph.sb("table", [1, DEC_BATCH * PAST // PAGE], I32)
            table_loaded = ph.sem("table_loaded")
            pages_moved = ph.sem("pages_moved")
        n_stores = 6 if dilated else 1
        n_v = n_stores
        block = ph.block()

        def branch_views(tile, hh, cols):
            out = []
            for b, d in enumerate((1, 4, 16) if dilated else (1,)):
                nb = SEQ // d // P
                for r in range(1 if d in (1, 16) else d):
                    t0 = b * TILES + r * nb
                    n = nb if d != 16 else d
                    out.append((tile[:, hh, t0:t0 + n, 0:cols], b, d, r))
            return out

        def tokens(ap, d, r):
            if d == 1:
                return ap.rearrange("(n p) c -> p n c", p=P)
            if d == 16:
                return ap.rearrange("(p r) c -> p r c", r=d)
            return ap.rearrange("(n p r) c -> r p n c", p=P, r=d)[r, :, :, :]

        @block.sync
        def _(sp):
            def load(i, hh):
                h = 2 * i + hh
                cols = ds(h * HD, HD)
                turned.wait(sp, h, -2 * NB + HEAD_GROUPS - 1)
                for name, tile in ((names[0], q_in), (names[1], k_in)):
                    sp.dma_start(tile[:, hh, :, 0:HD], dram[name][0:SEQ, cols].rearrange("(n p) c -> p n c", p=P))\
                        .then_inc(qk_loaded[hh], 16)
                pv.wait(sp, h, -NG - 1)
                for dst, _b, d, r in branch_views(v_in, hh, HD):
                    sp.dma_start(dst, tokens(dram[names[2]][0:SEQ, cols], d, r)).then_inc(v_loaded[hh], 16)

            def store(i, hh):
                h = 2 * i + hh
                posted.wait(sp, h, NS - 1)
                for src, b, d, r in branch_views(o_sb, hh, row):
                    to = dram["dil"][b, :, ds(h * row, row)] if dilated else dram["att"][0:SEQ, ds(h * HD, HD)]
                    sp.dma_start(tokens(to, d, r), src).then_inc(o_sent[hh], 16)

            for hh in range(2):
                sp.sem_inc(o_sent[hh], 16 * n_stores)
            if not dilated:
                sp.dma_start(upto[:, :], dram["upto"]).then_inc(c_loaded, 16)
            assert DEC_BATCH == HEADS
            new, old, fresh = ("new_win_v", "win_v", "v_b") if dilated else ("new_win_k", "win_k", "k_b")

            def move_window(i, hh):
                b = ds(2 * i + hh, 1)
                sp.dma_start(dram[new][b, 0:PAST - DEC_SEQ, :].rearrange("b t d -> (b t) d"),
                             dram[old][b, DEC_SEQ:PAST, :].rearrange("b t d -> (b t) d")).then_inc(moved, 16)

            load(0, 0)
            load(0, 1)
            with sp.Fori(0, HEADS // 2 - 1) as i:
                for hh in range(2):
                    store(i, hh)
                    load(i + 1, hh)
                    move_window(i, hh)
            for hh in range(2):
                move_window(HEADS // 2 - 1, hh)
            sp.dma_start(dram[new][:, PAST - DEC_SEQ:PAST, :],
                         dram[fresh][SEQ:SEQ + N_SAMPLE, :].rearrange("(b q) d -> b q d", q=DEC_SEQ))\
                .then_inc(moved, 16)
            for hh in range(2):
                store(HEADS // 2 - 1, hh)
            sp.wait_ge(moved, 16 * (HEADS + 1))
            for hh in range(2):
                sp.wait_ge(o_sent[hh], 16 * n_stores * (HEADS // 2 + 1))

        @block.gpsimd
        def _(pool):
            pool.memset(q_in[:, :, :, HD:P], 0.0).then_inc(set_up, 1)
            pool.memset(k_in[:, :, :, HD:P], 0.0).then_inc(set_up, 1)
            pool.memset(v_in[:, :, :, HD:P], 0.0).then_inc(set_up, 1)
            pool.wait_ge(set_up, 3)
            pool.memset(v_in[:, :, :, HD:HD + 1], 1.0).then_inc(set_up, 1)
            if not dilated:
                pool.memset(q_in[:, :, :, HD:HD + 1], 1.0).then_inc(set_up, 1)
                pool.memset(ones[:, :], 1.0).then_inc(set_up, 1)
                pool.dma_start(table[:, :], dram["page_table"]).then_inc(table_loaded, 16)
                pool.wait_ge(table_loaded, 16)
                with pool.Fori(0, DEC_BATCH * PAST // PAGE) as n:
                    page = pool.value_load(table[0:1, ds(n, 1)], min_val=0,
                                           max_val=dram["cache_logf"].shape[0] - 1)
                    pool.dma_start(dram["lf_pages"][ds(n, 1), :],
                                   dram["cache_logf"][ds(page, 1), :, :].rearrange("a p h -> a (p h)"))\
                        .then_inc(pages_moved, 16)
                pool.wait_ge(pages_moved, 16 * DEC_BATCH * PAST // PAGE)
        SET_UP = 4 if dilated else 6

        def copy_group(eng, i, hh, b):
            h = 2 * i + hh
            turned.wait(eng, h, b)
            bank = t_ps[b % PT_BANKS]
            if b < HEAD_GROUPS:
                to = (qT if b < HEAD_GROUPS // 2 else kT)[:, hh, b % (HEAD_GROUPS // 2) * 512:][:, 0:512]
                n = 4 * P
                scored.wait(eng, h, -NQ - 1)
            else:
                g = b - HEAD_GROUPS
                n = len(groups[g][1]) * P
                pv.wait(eng, h, last_user(pT_used, g))
                to = pT[:, g % PT_SLOTS, 0:n]
            if copier[b] == 0:
                op = nc.scalar.activation(to, bank[:, 0:n], ACT.Copy)
            else:
                op = nc.vector.tensor_copy(to, bank[:, 0:n])
            op.then_inc(copied[copier[b]].sem, 1)

        @block.scalar
        def _(act):
            def exps(i, hh, s):
                h = 2 * i + hh
                maxed.wait(act, h, s)
                turned.wait(act, h, turned_at(last_user(p_used, s)))
                for q in range(first_piece[s], first_piece[s + 1]):
                    for k, u in enumerate(steps[s]):
                        x = pieces[q][1] if len(steps[s]) == 1 else 0
                        n = min(u["w"], pieces[q][2])
                        a = (q % 4) * 512 + k * u["w"]
                        op = act.activation(p_sb[:, u["p"] + x:u["p"] + x + n], s_ps[:, a:a + n], ACT.Exp,
                                            bias=nmax[:, s % MAX_SLOTS, k:k + 1])
                    op.then_inc(exped.sem, 1)

            def turned_at(s):
                return HEAD_GROUPS + last_group[s] if s >= 0 else HEAD_GROUPS + last_group[s + NS] - NB

            exped.start(act)
            copied[0].start(act)
            with act.Fori(0, HEADS // 2) as i:
                for hh in range(2):
                    for b in range(HEAD_GROUPS):
                        if copier[b] == 0:
                            copy_group(act, i, hh, b)
                    for s in range(LOOK_EXP):
                        exps(i, hh, s)
                    for s in range(NS):
                        for g in range(first_group[s], last_group[s] + 1):
                            if copier[HEAD_GROUPS + g] == 0:
                                copy_group(act, i, hh, HEAD_GROUPS + g)
                        if s + LOOK_EXP < NS:
                            exps(i, hh, s + LOOK_EXP)

        @block.vector
        def _(dve):
            def maxima(i, hh, s):
                h = 2 * i + hh
                step = steps[s]
                n, w = len(step), step[0]["w"]
                posted.wait(dve, h, last_user(m_used, s))
                for b, q in enumerate(range(first_piece[s], first_piece[s + 1])):
                    _s, x, cols = pieces[q]
                    s0 = (q % 4) * 512
                    scored.wait(dve, h, q)
                    if q + 1 == first_piece[s + 1]:
                        if dilated:
                            part = s_ps[:, s0:s0 + n * w].rearrange("p (n w) -> p n w", w=w)
                            mask = c["mask"][:, 2 * P - w:2 * P].unsqueeze(1).to_broadcast([P, n, w])
                        else:
                            part = s_ps[:, s0 + cols - P:s0 + cols]
                            mask = c["mask"][:, P:2 * P]
                        dve.tensor_tensor(part, part, mask, ALU.add).then_inc(masked.sem, 1)
                        masked.wait(dve, h, s)
                    if n_pieces[s] == 1:
                        dve.tensor_reduce(nmax[:, s % MAX_SLOTS, 0:n],
                                          s_ps[:, s0:s0 + cols].rearrange("p (n w) -> p n w", n=n),
                                          AX_X, ALU.max, negate=True).then_inc(maxed.sem, 1)
                    else:
                        dve.tensor_reduce(piece_nmax[:, s % MAX_SLOTS, b:b + 1], s_ps[:, s0:s0 + cols], AX_X, ALU.max,
                                          negate=True).then_inc(piece_maxed.sem, 1)
                if n_pieces[s] > 1:
                    piece_maxed.wait(dve, h, sum(m for m in n_pieces[:s + 1] if m > 1) - 1)
                    dve.tensor_reduce(nmax[:, s % MAX_SLOTS, 0:1], piece_nmax[:, s % MAX_SLOTS, 0:n_pieces[s]], AX_X, ALU.min)\
                        .then_inc(maxed.sem, 1)

            def outputs(i, hh, s):
                h = 2 * i + hh
                step = steps[s]
                pv.wait(dve, h, last_group[s])
                if s == 0:
                    dve.wait_ge(o_sent[hh], 16 * n_stores * (i + 1))
                if dilated:
                    for k, u in enumerate(step):
                        slot = k
                        dve.tensor_scalar(o_sb[:, hh, u["o"], HD + 1:HD + 2], nmax[:, s % MAX_SLOTS, k:k + 1], -1.0, None,
                                          ALU.mult)
                        op = dve.tensor_copy(o_sb[:, hh, u["o"], 0:HD + 1], o_ps[:, slot, 0:HD + 1])
                    op.then_inc(posted.sem, 1)
                    return
                slot = 0
                dve.reciprocal(rden[:, slot:slot + 1], o_ps[:, slot, HD:HD + 1]).then_inc(inverted.sem, 1)
                inverted.wait(dve, h, s)
                dve.tensor_scalar(o_sb[:, hh, s, :], o_ps[:, slot, 0:HD], rden[:, slot:slot + 1], None, ALU.mult)\
                    .then_inc(posted.sem, 1)

            for e in (masked, maxed, posted, inverted, decayed, copied[1]) + (() if dilated else (piece_maxed,)):
                e.start(dve)
            if not dilated:
                step = [0]
                lf = c["logf"]
                dve.memset(before[:, 0:HEADS], 0.0).then_inc(sums, 1)
                for t in range(1, TILES):
                    dve.wait_ge(sums, t)
                    dve.tensor_tensor(before[:, t * HEADS:(t + 1) * HEADS], before[:, (t - 1) * HEADS:t * HEADS],
                                      lf[:, (t - 1) * HEADS:t * HEADS], ALU.add).then_inc(sums, 1)
                dve.wait_ge(summed, 1)
                dve.tensor_scalar(neg_c[:, :, :].rearrange("p t h -> p (t h)"), s_ps[:, 0:TILES * HEADS], -1.0, None,
                                  ALU.mult).then_inc(sums, 1)
            dve.wait_ge(set_up, SET_UP)
            with dve.Fori(0, HEADS // 2) as i:
                for hh in range(2):
                    if not dilated:
                        h = 2 * i + hh
                        dve.wait_ge(sums, TILES + 1)
                        turned.wait(dve, h, -2 * NB + HEAD_GROUPS - 1)
                        dve.tensor_copy(k_in[:, hh, :, HD:HD + 1], neg_c[:, :, ds(h, 1)]).then_inc(decayed.sem, 1)
                    for b in range(HEAD_GROUPS):
                        if copier[b] == 1:
                            copy_group(dve, i, hh, b)
                    for s in range(LOOK):
                        maxima(i, hh, s)
                    for s in range(NS):
                        if s + LOOK < NS:
                            maxima(i, hh, s + LOOK)
                        if s > 0:
                            outputs(i, hh, s - 1)
                        for g in range(first_group[s], last_group[s] + 1):
                            if copier[HEAD_GROUPS + g] == 1:
                                copy_group(dve, i, hh, HEAD_GROUPS + g)
                    outputs(i, hh, NS - 1)

        @block.tensor
        def _(pe):
            def bank_free(h, b):
                k = last_user(t_used, b)
                who = copier[k % NB]
                n = copied[who].n
                copied[who].wait(pe, h, copied_at[k % NB] - (n if k < 0 else 0))

            def is_copied(h, b):
                copied[copier[b]].wait(pe, h, copied_at[b])

            def turn_head(i, hh):
                h = 2 * i + hh
                pe.wait_ge(qk_loaded[hh], 32 * (i + 1))
                if not dilated:
                    decayed.wait(pe, h, 0)
                for b in range(HEAD_GROUPS):
                    bank_free(h, b)
                    src = q_in if b < HEAD_GROUPS // 2 else k_in
                    for k in range(4):
                        mm = pe.transpose(t_ps[b % PT_BANKS][:, k * P:(k + 1) * P],
                                          src[:, hh, b % (HEAD_GROUPS // 2) * 4 + k, :], c["ident"][:, :])
                    mm.then_inc(turned.sem, 1)

            def scores(i, hh, s):
                h = 2 * i + hh
                for q in range(first_piece[s], first_piece[s + 1]):
                    exped.wait(pe, h, last_user(s_used, q))
                    _s, x, cols = pieces[q]
                    for k, u in enumerate(steps[s]):
                        q0, d = u["q0"], u["d"]
                        n = min(u["w"], cols)
                        to = (q % 4) * 512 + k * u["w"]
                        a = u["k0"] + (x * d if len(steps[s]) == 1 else 0)
                        mm = pe.matmul(s_ps[:, to:to + n], qT[:, hh, q0:q0 + (P - 1) * d + 1:d],
                                       kT[:, hh, a:a + (n - 1) * d + 1:d], start=True, stop=True)
                    mm.then_inc(scored.sem, 1)

            def turn_group(i, hh, g):
                h = 2 * i + hh
                s, blocks = groups[g]
                b = HEAD_GROUPS + g
                exped.wait(pe, h, first_piece[s] + g - first_group[s])
                bank_free(h, b)
                for k, (u, blk) in enumerate(blocks):
                    p0 = steps[s][u]["p"] + blk * P
                    mm = pe.transpose(t_ps[b % PT_BANKS][:, k * P:(k + 1) * P], p_sb[:, p0:p0 + P], c["ident"][:, :])
                mm.then_inc(turned.sem, 1)

            def products(i, hh, g):
                h = 2 * i + hh
                s, blocks = groups[g]
                is_copied(h, HEAD_GROUPS + g)
                if g == first_group[s]:
                    posted.wait(pe, h, last_user(o_used, s))
                for k, (u, blk) in enumerate(blocks):
                    unit = steps[s][u]
                    mm = pe.matmul(o_ps[:, u, :], pT[:, g % PT_SLOTS, k * P:(k + 1) * P],
                                   v_in[:, hh, unit["v"][blk], :], start=(blk == 0), stop=(blk == unit["w"] // P - 1))
                mm.then_inc(pv.sem, 1)

            for e in (turned, scored, pv):
                e.start(pe)
            if not dilated:
                pe.wait_ge(c_loaded, 16)
                pe.wait_ge(set_up, SET_UP)
                pe.wait_ge(sums, TILES)
                pe.matmul(s_ps[:, 0:TILES * HEADS], upto[:, :], c["logf"][:, 0:TILES * HEADS], start=True, stop=False)
                pe.matmul(s_ps[:, 0:TILES * HEADS], ones[:, :], before[:, :], start=False, stop=True)\
                    .then_inc(summed, 1)
                pe.wait_ge(sums, TILES + 1)
            pe.wait_ge(set_up, SET_UP)
            with pe.Fori(0, HEADS // 2) as i:
                for hh in range(2):
                    turn_head(i, hh)
                    for b in range(HEAD_GROUPS - 3, HEAD_GROUPS):
                        is_copied(2 * i + hh, b)
                    for s in range(LOOK):
                        scores(i, hh, s)
                    pe.wait_ge(v_loaded[hh], 16 * n_v * (i + 1))
                    for s in range(NS):
                        if s + LOOK < NS:
                            scores(i, hh, s + LOOK)
                        for g in range(first_group[s], last_group[s] + 1):
                            turn_group(i, hh, g)
                            if g > 0:
                                products(i, hh, g - 1)
                    products(i, hh, NG - 1)


GROUPS_KV = 2 * HEADS * DEC_SEQ


def sample_attend(nc, c, dram, dilated):
    NT = 10 if dilated else PAST // PAGE
    sizes = [4, 4, 2] if dilated else [4] * (NT // 4)
    loads = [1, 1, 1] if dilated else [4] * (NT // 4)
    starts = [sum(sizes[:g]) for g in range(len(sizes))]
    NG = len(sizes)
    W = NT * P
    PAIRS = DEC_BATCH // 2
    SEQROWS = HEADS * DEC_SEQ
    names = ("q_b", "k_b", "v_b") if dilated else ("q_a", "k_a", "v_a")
    NX = 2 * NT
    copier = [x % 2 for x in range(NX)]
    p_groups = [list(range(k, min(k + 4, NT))) for k in range(0, NT, 4)]
    PG = len(p_groups)

    with Phase(nc, "sdil" if dilated else "sfox") as ph:
        k_in = ph.sb("k_in", [P, 2, NT, D_G])
        v_in = ph.sb("v_in", [P, 2, NT, D_G])
        kT = ph.sb("kT", [P, 2, 4, 4 * P])
        p_sb = ph.sb("p", [P, W + DEC_SEQ])
        pT = ph.sb("pT", [P, 2, 4 * P])
        pT_new = ph.sb("pT_new", [DEC_SEQ, P])
        new_in = ph.sb("new_in", [2 * DEC_SEQ, 2, D_G])
        v_new = ph.sb("v_new", [DEC_SEQ, 2, D_G])
        q_bd = ph.sb("q_bd", [P, 2, 4, SEQROWS])
        k_new = ph.sb("k_new", [P, 4, 2 * DEC_SEQ])
        own = ph.sb("own", [P, HEADS])
        causal = ph.sb("causal", [P, DEC_SEQ])
        stat = ph.sb("stat", [P, 8])
        o_all = ph.sb("o_all", [P, HEADS, HD])
        o_own = ph.sb("o_own", [P, HD])
        o_sb = ph.sb("o_sb", [P, HD])
        s_ps = ph.ps("s", [P, 2048])
        t_ps = [ph.ps(f"t{k}", [P, 4 * P]) for k in range(2)]
        m_ps = ph.ps("m", [P, 512])
        o_ps = ph.ps("o", [P, D_G])
        if dilated:
            reach = ph.sb("reach", [P, W + DEC_SEQ])
            unreached = ph.sb("unreached", [P, W + DEC_SEQ])
        else:
            table = ph.sb("table", [1, DEC_BATCH * NT], I32)
            lf_pages = ph.sb("lf_pages", [P, PAGE, HEADS])
            lf_in = ph.sb("lf_in", [P, HEADS, DEC_BATCH, NT])
            lf_back = ph.sb("lf_back", [P, HEADS, DEC_BATCH, NT])
            lf_x = ph.sb("lf_x", [P, 2, NT, P])
            lf_new = ph.sb("lf_new", [DEC_SEQ, 2, HEADS])
            lf_newx = ph.sb("lf_newx", [DEC_SEQ, 2, SEQROWS])
            after = ph.sb("after", [P, P])
            upto = ph.sb("upto", [P, P])
            ones = ph.sb("ones", [P, P])
            table_loaded = ph.sem("table_loaded")
            lf_loaded = ph.sem("lf_loaded")
            lf_turned = ph.sem("lf_turned")
            lf_copied = ph.sem("lf_copied")
            lfn_loaded = ph.sem("lfn_loaded")
            backed = ph.sem("backed")
            lf_set = Count(ph.sem("lf_set"), 5)

        passed = ph.sem("passed")
        consts = ph.sem("consts")
        zeroed = ph.sem("zeroed")
        new_loaded = ph.sem("new_loaded")
        vn_loaded = ph.sem("vn_loaded")
        k_loaded = [ph.sem(f"k_loaded{g}") for g in range(2 * NG)]
        v_loaded = [ph.sem(f"v_loaded{g}") for g in range(2 * NG)]
        new_turned = Count(ph.sem("new_turned"), 1)
        q_spread = Count(ph.sem("q_spread"), 1)
        turned = Count(ph.sem("turned"), NX)
        copied = [Count(ph.sem("copied_act"), NX // 2), Count(ph.sem("copied_dve"), NX // 2)]
        scored = Count(ph.sem("scored"), 2 * NG + 1)
        masked = Count(ph.sem("masked"), 2)
        maxed = Count(ph.sem("maxed"), 3)
        exped = Count(ph.sem("exped"), 1)
        weighed = Count(ph.sem("weighed"), 1)
        p_turned = Count(ph.sem("p_turned"), PG + 1)
        p_copied = Count(ph.sem("p_copied"), PG + 1)
        pv = Count(ph.sem("pv"), PG + 1)
        out = Count(ph.sem("out"), 4)
        o_sent = ph.sem("o_sent")
        block = ph.block()
        PT_ALL = 2 * NG

        def load_kv(eng, i, s2, g, kv):
            tile, src = ((k_in, "win_k"), (v_in, "win_v"))[kv] if dilated else \
                        ((k_in, "cache_k"), (v_in, "cache_v"))[kv]
            sem = (k_loaded, v_loaded)[kv][s2 * NG + g]
            if kv == 0:
                turned.wait(eng, i, s2 * NT + starts[g] + sizes[g] - 1 - NX)
            else:
                pv.wait(eng, i, g - PG - 1)
            eng.sem_inc(passed, 1)
            if dilated:
                win = dram[src][ds(2 * i + s2, 1), :, :]
                if g < 2:
                    view = win.rearrange("a (m r) d -> (a m) r d", r=16)[:, 4 * g:4 * g + 4, :]
                    eng.dma_start(tile[:, s2, 4 * g:4 * g + 4, :], view).then_inc(sem, 16)
                else:
                    view = win.rearrange("a (m r) d -> (a m) r d", r=16)[96:128, 8:16, :]
                    eng.dma_start(tile[:, s2, 8:10, :], view.rearrange("m (b t) d -> m b (t d)", t=2))\
                        .then_inc(sem, 16)
                return
            for t in range(starts[g], starts[g] + sizes[g]):
                page = eng.value_load(table[0:1, ds((2 * i + s2) * NT + t, 1)], min_val=0,
                                     max_val=dram[src].shape[0] - 1)
                eng.dma_start(tile[:, s2, t, :], dram[src][ds(page, 1), :, :].rearrange("a p d -> (a p) d"))\
                    .then_inc(sem, 16)

        @block.sync
        def _(sp):
            pairs = [(own[:, :], dram["own"]), (causal[:, :], dram["causal_new"])]
            if dilated:
                pairs += [(reach[:, :], dram["reach"]), (unreached[:, :], dram["unreached"])]
            else:
                pairs += [(after[:, :], dram["after"]), (upto[:, :], dram["upto"])]
                sp.dma_start(table[:, :], dram["page_table"]).then_inc(table_loaded, 16)
                sp.wait_ge(table_loaded, 16)
                sp.dma_start(lf_pages[:, :, :], dram["lf_pages"].rearrange("n (p h) -> n p h", h=HEADS))\
                    .then_inc(lf_loaded, 16)
            for dst, src in pairs:
                sp.dma_start(dst, src).then_inc(consts, 16)

            def load_new(i):
                rows = ds(SEQ + i * 2 * DEC_SEQ, 2 * DEC_SEQ)
                new_turned.wait(sp, i, -1)
                for n in range(2):
                    sp.dma_start(new_in[:, n, :], dram[names[n]][rows, :]).then_inc(new_loaded, 16)
                if not dilated:
                    lf_set.wait(sp, i, -1)
                    sp.dma_start(lf_new[:, :, :], dram["logf"][rows, :].rearrange("(s q) h -> q s h", q=DEC_SEQ))\
                        .then_inc(lfn_loaded, 16)

            def load_new_v(i):
                rows = ds(SEQ + i * 2 * DEC_SEQ, 2 * DEC_SEQ)
                pv.wait(sp, i, -1)
                sp.dma_start(v_new[:, :, :], dram[names[2]][rows, :].rearrange("(s q) d -> q s d", q=DEC_SEQ))\
                    .then_inc(vn_loaded, 16)

            with sp.Fori(0, PAIRS) as i:
                load_new(i)
                for s2 in range(2):
                    for g in range(NG):
                        load_kv(sp, i, s2, g, 0)
                load_new_v(i)
                if dilated:
                    for g in range(NG):
                        for s2 in range(2):
                            load_kv(sp, i, s2, g, 1)

        @block.gpsimd
        def _(pool):
            pool.memset(q_bd[:, :, :, :], 0.0).then_inc(zeroed, 1)
            if not dilated:
                pool.memset(ones[:, :], 1.0).then_inc(zeroed, 1)
            if dilated:
                return
            pool.wait_ge(table_loaded, 16)

            pool.wait_ge(k_loaded[NG + 1], 16 * loads[1])
            with pool.Fori(0, PAIRS) as i:
                for g in range(NG):
                    for s2 in range(2):
                        load_kv(pool, i, s2, g, 1)

        def copy_tile(eng, i, x):
            turned.wait(eng, i, x)
            s2, t = divmod(x, NT)
            g = t // 4
            scored.wait(eng, i, s2 * NG + g - 2 if s2 * NG + g >= 2 else s2 * NG + g - 3)
            k = t - starts[g]
            to = kT[:, (s2 * NG + g) % 2, :, k * P:(k + 1) * P]
            src = t_ps[x % 2][:, :].rearrange("p (j m) -> p j m", m=P)
            if copier[x] == 0:
                nc.scalar.activation(to, src, ACT.Copy).then_inc(copied[0].sem, 1)
            else:
                nc.vector.tensor_copy(to, src).then_inc(copied[1].sem, 1)

        @block.scalar
        def _(act):
            act.sem_inc(o_sent, 32)
            copied[0].start(act)
            exped.start(act)
            p_copied.start(act)
            with act.Fori(0, PAIRS) as i:
                for x in range(0, NX, 2):
                    copy_tile(act, i, x)
                maxed.wait(act, i, 2)
                p_turned.wait(act, i, -1)
                out.wait(act, i, -1)
                act.activation(p_sb[:, 0:W], s_ps[:, 0:W], ACT.Exp, bias=stat[:, 2:3], accum_out=stat[:, 3:4])
                act.activation(p_sb[:, W:W + DEC_SEQ], m_ps[:, 0:DEC_SEQ], ACT.Exp, bias=stat[:, 2:3],
                               accum_out=stat[:, 4:5]).then_inc(exped.sem, 1)
                for g in range(PG + 1):
                    p_turned.wait(act, i, g)
                    pv.wait(act, i, g - 2 if g >= 2 else g - PG - 1)
                    if g < PG:
                        n = len(p_groups[g]) * P
                        op = act.activation(pT[:, g % 2, 0:n], t_ps[g % 2][:, 0:n], ACT.Copy)
                    else:
                        op = act.activation(pT_new[:, :], t_ps[g % 2][0:DEC_SEQ, 0:P], ACT.Copy)
                    op.then_inc(p_copied.sem, 1)
                out.wait(act, i, 3)
                for s2 in range(2):
                    rows = ds(i * 2 * DEC_SEQ + SEQ + s2 * DEC_SEQ, DEC_SEQ)
                    col = D_G if dilated else 0
                    act.dma_start(dram["att"][rows, col:col + D_G].rearrange("q (h d) -> h q d", h=HEADS),
                                  o_sb[s2 * SEQROWS:(s2 + 1) * SEQROWS, :]).then_inc(o_sent, 16)
            act.wait_ge(o_sent, 32 + 16 * 2 * PAIRS)

        @block.vector
        def _(dve):
            for e in (copied[1], masked, maxed, weighed, q_spread, out) + (() if dilated else (lf_set,)):
                e.start(dve)
            dve.wait_ge(consts, 64)
            dve.wait_ge(zeroed, 1)
            if not dilated:
                for k in range(2):
                    dve.wait_ge(lf_turned, k + 1)
                    dve.tensor_copy(lf_in[:, 4 * k:4 * k + 4, :, :],
                                    t_ps[k][:, :].rearrange("p (h b t) -> p h b t", h=4, b=DEC_BATCH))\
                        .then_inc(lf_copied, 1)
                dve.wait_ge(lf_copied, 2)
                dve.memset(lf_back[:, :, :, NT - 1], 0.0).then_inc(backed, 1)
                for n, t in enumerate(reversed(range(NT - 1))):
                    dve.wait_ge(backed, n + 1)
                    dve.tensor_tensor(lf_back[:, :, :, t], lf_back[:, :, :, t + 1], lf_in[:, :, :, t + 1], ALU.add)\
                        .then_inc(backed, 1)
                dve.wait_ge(backed, NT)

            def spread_lf(i, n):
                if n < 4:
                    k, s2 = divmod(n, 2)
                    dst = lf_x[:, k, :, s2 * SEQROWS:(s2 + 1) * SEQROWS].rearrange("p t (h q) -> p t h q", q=DEC_SEQ)
                    src = (lf_in, lf_back)[k][:, :, ds(2 * i + s2, 1), :].rearrange("p h a t -> p t (a h)")
                    dve.tensor_copy(dst, src.unsqueeze(3).to_broadcast([P, NT, HEADS, DEC_SEQ]))\
                        .then_inc(lf_set.sem, 1)
                else:
                    dve.wait_ge(lfn_loaded, 16 * (i + 1))
                    dve.sem_inc(passed, 1)
                    dve.tensor_scalar(lf_newx[:, :, :].rearrange("p s (h q) -> p s h q", q=DEC_SEQ),
                                      lf_new[:, :, :].unsqueeze(3).to_broadcast([DEC_SEQ, 2, HEADS, DEC_SEQ]),
                                      -1.0, None, ALU.mult).then_inc(lf_set.sem, 1)

            with dve.Fori(0, PAIRS) as i:
                new_turned.wait(dve, i, 0)
                scored.wait(dve, i, -1)
                turned_new = m_ps[:, 0:2 * 4 * 2 * DEC_SEQ].rearrange("p (n j s q) -> p n j s q", n=2, j=4, s=2)
                for hp in range(2):
                    rows = slice(hp * HD, (hp + 1) * HD)
                    for j in range(4):
                        a = (2 * j + hp) * DEC_SEQ
                        dve.tensor_copy(q_bd[rows, :, j, a:a + DEC_SEQ], turned_new[rows, 0, j, :, :])
                dve.tensor_copy(k_new[:, :, :].rearrange("p j (s q) -> p j s q", s=2), turned_new[:, 1, :, :, :])\
                    .then_inc(q_spread.sem, 1)
                for x in range(1, NX, 2):
                    copy_tile(dve, i, x)
                    if not dilated and x % 4 == 1 and x < 20:
                        spread_lf(i, x // 4)
                scored.wait(dve, i, PT_ALL)
                if dilated:
                    dve.tensor_tensor(s_ps[:, 0:W], s_ps[:, 0:W], unreached[:, 0:W], ALU.add).then_inc(masked.sem, 1)
                    dve.tensor_tensor(m_ps[:, 0:DEC_SEQ], m_ps[:, 0:DEC_SEQ], unreached[:, W:W + DEC_SEQ], ALU.add)\
                        .then_inc(masked.sem, 1)
                else:
                    dve.tensor_tensor(m_ps[:, 0:DEC_SEQ], m_ps[:, 0:DEC_SEQ], causal[:, :], ALU.add)\
                        .then_inc(masked.sem, 2)
                masked.wait(dve, i, 1)
                out.wait(dve, i, -1)
                dve.tensor_reduce(stat[:, 0:1], s_ps[:, 0:W], AX_X, ALU.max, negate=True).then_inc(maxed.sem, 1)
                dve.tensor_reduce(stat[:, 1:2], m_ps[:, 0:DEC_SEQ], AX_X, ALU.max, negate=True).then_inc(maxed.sem, 1)
                maxed.wait(dve, i, 1)
                dve.tensor_tensor(stat[:, 2:3], stat[:, 0:1], stat[:, 1:2], ALU.min).then_inc(maxed.sem, 1)
                exped.wait(dve, i, 0)
                if dilated:
                    dve.scalar_tensor_tensor(p_sb[:, :], p_sb[:, :], 1.0, reach[:, :], ALU.mult, ALU.mult,
                                             accum_out=stat[:, 5:6]).then_inc(weighed.sem, 1)
                else:
                    dve.tensor_tensor(stat[:, 5:6], stat[:, 3:4], stat[:, 4:5], ALU.add).then_inc(weighed.sem, 1)
                weighed.wait(dve, i, 0)
                dve.reciprocal(stat[:, 6:7], stat[:, 5:6]).then_inc(out.sem, 1)
                pv.wait(dve, i, PG)
                dve.tensor_tensor(o_all[:, :, :], o_ps[:, :].rearrange("p (h d) -> p h d", d=HD),
                                  own[:, :].unsqueeze(2).to_broadcast([P, HEADS, HD]), ALU.mult).then_inc(out.sem, 1)
                out.wait(dve, i, 1)
                dve.tensor_reduce(o_own[:, :], o_all[:, :, :].rearrange("p h d -> p d h"), AX_X, ALU.add)\
                    .then_inc(out.sem, 1)
                out.wait(dve, i, 2)
                dve.wait_ge(o_sent, 16 * 2 * i + 32)
                dve.tensor_scalar(o_sb[:, :], o_own[:, :], stat[:, 6:7], None, ALU.mult).then_inc(out.sem, 1)

        @block.tensor
        def _(pe):
            for e in (new_turned, turned, scored, p_turned, pv):
                e.start(pe)
            pe.wait_ge(consts, 64)
            pe.wait_ge(zeroed, 1 if dilated else 2)
            if not dilated:
                pe.wait_ge(lf_loaded, 16)
                for k in range(2):
                    for h in range(4):
                        mm = pe.transpose(t_ps[k][:, h * P:(h + 1) * P], lf_pages[:, :, 4 * k + h], c["ident"][:, :])
                    mm.then_inc(lf_turned, 1)
                pe.wait_ge(lf_copied, 2)

            def is_copied(i, x):
                copied[copier[x % NX]].wait(pe, i, (x % NX) // 2 - (NX // 2 if x < 0 else 0))

            def turn_tile(i, x):
                s2, t = divmod(x, NT)
                g = t // 4
                if t == starts[g]:
                    pe.wait_ge(k_loaded[s2 * NG + g], 16 * loads[g] * (i + 1))
                if x < 2:
                    p_copied.wait(pe, i, -1)
                else:
                    is_copied(i, x - 2)
                for j in range(4):
                    mm = pe.transpose(t_ps[x % 2][:, j * P:(j + 1) * P], k_in[:, s2, t, j * P:(j + 1) * P],
                                      c["ident"][:, :])
                mm.then_inc(turned.sem, 1)

            def scores(i, gg):
                s2, g = divmod(gg, NG)
                last = s2 * NT + starts[g] + sizes[g] - 1
                is_copied(i, last)
                is_copied(i, last - 1)
                if gg == 0:
                    exped.wait(pe, i, -1)
                n = sizes[g] * P
                rows = slice(s2 * SEQROWS, (s2 + 1) * SEQROWS)
                for j in range(4):
                    mm = pe.matmul(s_ps[rows, starts[g] * P:starts[g] * P + n], q_bd[:, s2, j, :],
                                   kT[:, gg % 2, j, 0:n], start=(j == 0), stop=(j == 3 and dilated))
                mm.then_inc(scored.sem, 1)

            with pe.Fori(0, PAIRS) as i:
                pe.wait_ge(new_loaded, 32 * (i + 1))
                exped.wait(pe, i, -1)
                pe.sem_inc(passed, 1)
                for n in range(2):
                    for j in range(4):
                        a = (n * 4 + j) * 2 * DEC_SEQ
                        mm = pe.transpose(m_ps[:, a:a + 2 * DEC_SEQ], new_in[:, n, j * P:(j + 1) * P],
                                          c["ident"][0:2 * DEC_SEQ, 0:2 * DEC_SEQ])
                mm.then_inc(new_turned.sem, 1)
                q_spread.wait(pe, i, 0)
                done = 0
                for x in range(NX):
                    turn_tile(i, x)
                    while done < 2 * NG and x >= min(NX - 1, (done // NG) * NT + starts[done % NG] + sizes[done % NG] + 1):
                        scores(i, done)
                        done += 1
                while done < 2 * NG:
                    scores(i, done)
                    done += 1
                for s2 in range(2):
                    rows = slice(s2 * SEQROWS, (s2 + 1) * SEQROWS)
                    for j in range(4):
                        mm = pe.matmul(m_ps[rows, 0:DEC_SEQ], q_bd[:, s2, j, :],
                                       k_new[:, j, s2 * DEC_SEQ:(s2 + 1) * DEC_SEQ], start=(j == 0),
                                       stop=(j == 3 and dilated))
                    if not dilated:
                        if s2 == 0:
                            lf_set.wait(pe, i, 4)
                        mm = pe.matmul(m_ps[rows, 0:DEC_SEQ], lf_newx[:, s2, :], upto[0:DEC_SEQ, 0:DEC_SEQ],
                                       start=False, stop=True)
                if not dilated:
                    for t in range(NT):
                        pe.matmul(s_ps[:, t * P:(t + 1) * P], lf_x[:, 0, t, :], after[:, :], start=False, stop=False)
                        mm = pe.matmul(s_ps[:, t * P:(t + 1) * P], lf_x[:, 1, t, :], ones[:, :], start=False,
                                       stop=(t % 4 == 3))
                mm.then_inc(scored.sem, 1)

                def turn_p(g):
                    if g < 2:
                        is_copied(i, NX - 2 + g)
                        if g == 0:
                            weighed.wait(pe, i, 0)
                    else:
                        p_copied.wait(pe, i, g - 2)
                    if g < PG:
                        for k, t in enumerate(p_groups[g]):
                            mm = pe.transpose(t_ps[g % 2][:, k * P:(k + 1) * P], p_sb[:, t * P:(t + 1) * P],
                                              c["ident"][:, :])
                    else:
                        mm = pe.transpose(t_ps[g % 2][0:DEC_SEQ, 0:P], p_sb[:, W:W + DEC_SEQ], c["ident"][:, :])
                    mm.then_inc(p_turned.sem, 1)

                def products(g):
                    p_copied.wait(pe, i, g)
                    if g == 0:
                        out.wait(pe, i, 1 - 4)
                    if g == PG:
                        pe.wait_ge(vn_loaded, 16 * (i + 1))
                    for s2 in range(2):
                        rows = slice(s2 * SEQROWS, (s2 + 1) * SEQROWS)
                        if g < PG:
                            pe.wait_ge(v_loaded[s2 * NG + g], 16 * loads[g] * (i + 1))
                            for k, t in enumerate(p_groups[g]):
                                mm = pe.matmul(o_ps[rows, :], pT[:, g % 2, k * P + s2 * SEQROWS:k * P + (s2 + 1) * SEQROWS],
                                               v_in[:, s2, t, :], start=(t == 0), stop=False)
                        else:
                            mm = pe.matmul(o_ps[rows, :], pT_new[:, rows], v_new[:, s2, :], start=False, stop=True)
                    mm.then_inc(pv.sem, 1)

                turn_p(0)
                for g in range(PG + 1):
                    if g < PG:
                        turn_p(g + 1)
                    products(g)


def join_heads(nc, c, dram, g, first, tiles, h_hi, h_lo, x1):
    with Phase(nc, f"join{g}") as ph:
        w_hi = ph.sb("w_hi", [P, KC, D_MODEL], F32R)
        w_lo = ph.sb("w_lo", [P, KC, D_MODEL], F32R)
        o_in = ph.sb("o_in", [P, 2, D_MODEL])
        parts = ph.sb("parts", [P, 3, HEADS, HD + 2])
        o_hi = ph.sb("o_hi", [P, D_MODEL], F32R)
        o_lo = ph.sb("o_lo", [P, D_MODEL], F32R)
        h = ph.sb("h", [P, D_MODEL])
        hg = ph.sb("hg", [P, D_MODEL])
        w_raw = [(h, hg)[k // 2][:, k % 2 * D_G:(k % 2 + 1) * D_G] for k in range(4)]
        g_mlp = ph.sb("g_mlp", [P, KC])
        top = ph.sb("top", [P, 2, HEADS])
        e = ph.sb("e", [P, 2, 3, HEADS])
        den = ph.sb("den", [P, 2, HEADS])
        stat = ph.sb("stat", [P, 3])
        minus_half = ph.sb("minus_half", [P, 1])
        to_ps = ph.ps("to", [P, D_MODEL])
        th_ps = ph.ps("th", [P, D_MODEL])
        pr_ps = [ph.ps(f"pr{j}", [P, D_MODEL]) for j in range(2)]

        passed = ph.sem("passed")
        consts = ph.sem("consts")
        x_loaded = ph.sems("x_loaded")
        half_set = ph.sem("half_set")
        w_loaded = ph.sems("w_loaded", 4)
        w_hi_done = ph.sem("w_hi_done")
        w_split = ph.sem("w_split")
        o_loaded = ph.sems("o_loaded")
        parts_loaded = ph.sem("parts_loaded")
        weights = ph.sem("weights")
        exped = ph.sem("exped")
        weighed = ph.sem("weighed")
        merged = ph.sem("merged")
        o_turned = ph.sem("o_turned")
        o_hi_done = ph.sem("o_hi_done")
        o_lo_done = ph.sem("o_lo_done")
        product = ph.sem("product")
        added = ph.sem("added")
        squared = ph.sem("squared")
        mean_done = ph.sem("mean_done")
        rstd_done = ph.sem("rstd_done")
        h_done = ph.sem("h_done")
        h_turned = ph.sem("h_turned")
        hg_done = ph.sem("hg_done")
        h_hi_done = ph.sem("h_hi_done")
        h_lo_done = ph.sem("h_lo_done")
        block = ph.block()

        n_prompt = min(tiles, TILES - first)

        LOOPS = (n_prompt - 3) // 2

        def steps(eng, body):
            body(0)
            with eng.Fori(0, LOOPS) as i:
                body(2 * i + 1, 1)
                body(2 * i + 2, 0)
            for t in range(2 * LOOPS + 1, tiles):
                body(t)

        def behind(t):
            return isinstance(t, int) and t == 0

        def ahead(t):
            return not isinstance(t, int) or t + 1 < tiles, not isinstance(t, int) or t + 1 < n_prompt

        def merges(t):
            return not isinstance(t, int) or t + 2 < n_prompt

        @block.sync
        def _(sp):
            def load_o(t, slot):
                rows = ds((first + t) * P, P)
                if isinstance(t, int) and t >= n_prompt:
                    sp.wait_ge(o_turned, t - 1)
                    sp.dma_start(o_in[0:N_SAMPLE, slot, :], dram["att"][SEQ:SEQ + N_SAMPLE, :])\
                        .then_inc(o_loaded[slot], 16)
                    return
                if not (isinstance(t, int) and t < 2):
                    sp.wait_ge(o_turned, t - 1)
                sp.dma_start(o_in[:, slot, 0:D_G], dram["att"][rows, 0:D_G]).then_inc(o_loaded[slot], 16)
                if not (isinstance(t, int) and t == 0):
                    sp.wait_ge(merged, 2 * t)
                sp.dma_start(parts[:, :, :, :].rearrange("p b h d -> p b (h d)"),
                             dram["dil"][:, rows, :].rearrange("b p n -> p b n")).then_inc(parts_loaded, 16)

            def load_w(k):
                sp.dma_start(w_raw[k % 4], dram["w_o"][k // 2 * P:(k // 2 + 1) * P,
                                                             k % 2 * D_G:(k % 2 + 1) * D_G])\
                    .then_inc(w_loaded[k % 4], 16)

            load_o(0, 0)
            for k in range(4):
                load_w(k)
            sp.dma_start(g_mlp[:, :], dram["g_mlp"]).then_inc(consts, 16)
            for k in range(4, 2 * KC):
                sp.wait_ge(w_split, k - 3)
                if k == KC + 4:
                    load_o(1, 1)
                load_w(k)
            for n, (a, b) in enumerate(((0, 1), (1, tiles))):
                sp.dma_start(x1[:, a:b, :], dram["x"][(first + a) * P:(first + b) * P, :]
                             .rearrange("(t p) n -> p t n", p=P)).then_inc(x_loaded[n], 16)
            with sp.Fori(0, (n_prompt - 2) // 2) as i:
                load_o(2 * i + 2, 0)
                load_o(2 * i + 3, 1)
            for t in range(n_prompt, tiles):
                load_o(t, t % 2)

        @block.scalar
        def _(act):
            def weigh(t):
                act.wait_ge(weights, 7 * t + 3)
                act.activation(e[:, 1, :, :], e[:, 0, :, :], ACT.Exp).then_inc(exped, 1)

            def hi_o(t):
                act.wait_ge(o_turned, t + 1)
                for q in range(2):
                    if not (isinstance(t, int) and t == 0):
                        act.wait_ge(product, 2 * t + q - 1)
                    half = slice(q * D_G, (q + 1) * D_G)
                    act.activation(o_hi[:, half], to_ps[:, half], ACT.Copy).then_inc(o_hi_done, 1)

            def hi_h(t):
                act.wait_ge(hg_done, 2 * (t + 1))
                act.activation(h_hi[:, :, ds(t * P, P)] if not isinstance(t, int) or t < n_prompt else
                               h_hi[:, :, t * P:t * P + N_SAMPLE],
                               (hg[:, :].rearrange("p (k m) -> p k m", m=P) if not isinstance(t, int) or t < n_prompt
                                else hg[:, :].rearrange("p (k m) -> p k m", m=P)[:, :, 0:N_SAMPLE]),
                               ACT.Copy).then_inc(h_hi_done, 1)

            def body(t, odd=None):
                if merges(t):
                    weigh(t + 2)
                if ahead(t)[0]:
                    hi_o(t + 1)
                act.wait_ge(added, 2 * (t + 1))
                if not behind(t):
                    act.wait_ge(h_turned, t)
                act.activation(h[:, :], x1[:, ds(t, 1), :].rearrange("p a n -> p (a n)"), ACT.Square,
                               accum_out=stat[:, 0:1]).then_inc(squared, 1)
                act.wait_ge(rstd_done, t + 1)
                act.sem_inc(passed, 1)
                act.activation(h[:, :], x1[:, ds(t, 1), :].rearrange("p a n -> p (a n)"), ACT.Copy,
                               scale=stat[:, 2:3]).then_inc(h_done, 1)
                if not behind(t):
                    hi_h(t - 1)

            weigh(0)
            for k in range(2 * KC):
                if k == KC:
                    hi_o(0)
                act.wait_ge(w_loaded[k % 4], 16 * (k // 4 + 1))
                act.activation(w_hi[:, k // 2, k % 2 * D_G:(k % 2 + 1) * D_G], w_raw[k % 4], ACT.Copy).then_inc(w_hi_done, 1)
            weigh(1)
            steps(act, body)
            hi_h(tiles - 1)

        @block.gpsimd
        def _(pool):
            pool.memset(minus_half[:, :], -0.5).then_inc(half_set, 1)
            pool.wait_ge(half_set, 1)

            def weigh(t):
                pool.wait_ge(weights, 7 * (t + 1))
                pool.tensor_tensor(parts[:, :, :, 0:HD], parts[:, :, :, 0:HD],
                                   e[:, 0, :, :].unsqueeze(3).to_broadcast([P, 3, HEADS, HD]),
                                   ALU.mult).then_inc(weighed, 1)

            def lo_h(t):
                pool.wait_ge(h_hi_done, t + 1)
                n = N_SAMPLE if isinstance(t, int) and t >= n_prompt else P
                pool.tensor_tensor(h_lo[:, :, ds(t * P, n)], hg[:, :].rearrange("p (k m) -> p k m", m=P)[:, :, 0:n],
                                   h_hi[:, :, ds(t * P, n)].bitcast(F32), ALU.subtract).then_inc(h_lo_done, 1)

            def body(t, odd=None):
                if merges(t):
                    weigh(t + 2)
                pool.wait_ge(mean_done, t + 1)
                pool.tensor_tensor(stat[:, 2:3], stat[:, 1:2], minus_half[:, :], ALU.pow).then_inc(rstd_done, 1)
                if not behind(t):
                    lo_h(t - 1)

            weigh(0)
            weigh(1)
            steps(pool, body)
            lo_h(tiles - 1)

        @block.vector
        def _(dve):
            m = parts[:, :, :, HD + 1]
            l = parts[:, :, :, HD]

            def branch_weights(t):
                w = 7 * t

                def step(op, k):
                    op.then_inc(weights, 1)
                    if k < 7:
                        dve.wait_ge(weights, w + k)

                dve.wait_ge(parts_loaded, 16 * (t + 1))
                step(dve.tensor_tensor(top[:, 0, :], m[:, 0, :], m[:, 1, :], ALU.max), 1)
                step(dve.tensor_tensor(top[:, 1, :], top[:, 0, :], m[:, 2, :], ALU.max), 2)
                step(dve.tensor_tensor(e[:, 0, :, :], m, top[:, 1:2, :].to_broadcast([P, 3, HEADS]), ALU.subtract), 3)
                dve.wait_ge(exped, t + 1)
                step(dve.tensor_tensor(e[:, 0, :, :], l, e[:, 1, :, :], ALU.mult), 4)
                step(dve.tensor_reduce(den[:, 0, :], e[:, 0, :, :].rearrange("p b h -> p h b"), AX_X, ALU.add), 5)
                step(dve.reciprocal(den[:, 1, :], den[:, 0, :]), 6)
                step(dve.tensor_tensor(e[:, 0, :, :], e[:, 1, :, :],
                                       den[:, 1:2, :].to_broadcast([P, 3, HEADS]), ALU.mult), 7)

            def branch_sum(t, slot, uses):
                dve.wait_ge(weighed, t + 1)
                dve.wait_ge(o_loaded[slot], 16 * uses)
                out = o_in[:, slot, D_G:D_MODEL].rearrange("p (h d) -> p h d", d=HD)
                dve.tensor_tensor(out, parts[:, 0, :, 0:HD], parts[:, 1, :, 0:HD], ALU.add).then_inc(merged, 1)
                dve.wait_ge(merged, 2 * t + 1)
                dve.tensor_tensor(out, out, parts[:, 2, :, 0:HD], ALU.add).then_inc(merged, 1)

            def lo_o(t):
                for q in range(2):
                    dve.wait_ge(o_hi_done, 2 * t + q + 1)
                    half = slice(q * D_G, (q + 1) * D_G)
                    dve.tensor_tensor(o_lo[:, half], to_ps[:, half], o_hi[:, half].bitcast(F32), ALU.subtract)\
                        .then_inc(o_lo_done, 1)

            def gain(t):
                dve.wait_ge(h_turned, t + 1)
                if not (isinstance(t, int) and t == 0):
                    dve.wait_ge(h_lo_done, t)
                for q in range(2):
                    dve.tensor_tensor(hg[:, q * 512:(q + 1) * 512].rearrange("p (k m) -> p k m", m=P),
                                      th_ps[:, q * 512:(q + 1) * 512].rearrange("p (k m) -> p k m", m=P),
                                      g_mlp[:, 4 * q:4 * q + 4].unsqueeze(2).to_broadcast([P, 4, P]),
                                      ALU.mult).then_inc(hg_done, 1)

            def body(t, odd=None, uses=None):
                slot = t % 2 if isinstance(t, int) else odd
                if merges(t):
                    branch_weights(t + 2)
                if ahead(t)[0]:
                    lo_o(t + 1)
                dve.wait_ge(product, 2 * (t + 1))
                if isinstance(t, int) and t <= 0:
                    dve.wait_ge(x_loaded[0], 16)
                for q in range(2):
                    part = x1[:, ds(t, 1), q * D_G:(q + 1) * D_G].rearrange("p a n -> p (a n)")
                    dve.tensor_tensor(part, pr_ps[slot][:, q * D_G:(q + 1) * D_G], part, ALU.add).then_inc(added, 1)
                if merges(t):
                    branch_sum(t + 2, slot, t // 2 + 2 if isinstance(t, int) else uses)
                dve.wait_ge(squared, t + 1)
                dve.tensor_scalar(stat[:, 1:2], stat[:, 0:1], 1.0 / D_MODEL, EPS, ALU.mult, ALU.add)\
                    .then_inc(mean_done, 1)
                if not behind(t):
                    gain(t - 1)

            branch_weights(0)
            for k in range(2 * KC):
                if k == KC:
                    branch_sum(0, 0, 1)
                    lo_o(0)
                dve.wait_ge(w_hi_done, k + 1)
                half = slice(k % 2 * D_G, (k % 2 + 1) * D_G)
                dve.tensor_tensor(w_lo[:, k // 2, half], w_raw[k % 4], w_hi[:, k // 2, half].bitcast(F32),
                                  ALU.subtract)\
                    .then_inc(w_split, 1)
            branch_weights(1)
            branch_sum(1, 1, 1)
            dve.wait_ge(consts, 16)
            body(0)
            dve.wait_ge(x_loaded[1], 16)
            with dve.Fori(0, LOOPS) as i:
                body(2 * i + 1, 1, i + 2)
                body(2 * i + 2, 0, i + 3)
            for t in range(2 * LOOPS + 1, tiles):
                body(t)
            gain(tiles - 1)

        @block.tensor
        def _(pe):
            def turn_o(t, slot, prompt=True):
                if prompt:
                    pe.wait_ge(merged, 2 * (t + 1))
                else:
                    pe.wait_ge(o_loaded[slot], 16 * (t // 2 + 1))
                if not behind(t):
                    pe.wait_ge(o_lo_done, 2 * t)
                for k in range(KC):
                    mm = pe.transpose(to_ps[:, k * P:(k + 1) * P], o_in[:, slot, k * P:(k + 1) * P],
                                      c["ident"][:, :])
                mm.then_inc(o_turned, 1)

            def turn_h(t):
                pe.wait_ge(h_done, t + 1)
                if not behind(t):
                    pe.wait_ge(hg_done, 2 * t)
                for k in range(KC):
                    mm = pe.transpose(th_ps[:, k * P:(k + 1) * P], h[:, k * P:(k + 1) * P], c["ident"][:, :])
                mm.then_inc(h_turned, 1)

            def body(t, odd=None):
                has, prompt = ahead(t)
                slot = t % 2 if isinstance(t, int) else odd
                for half in range(2):
                    pe.wait_ge(o_lo_done, 2 * t + half + 1)
                    if behind(t):
                        pe.wait_ge(w_split, (half + 1) * KC)
                    if half == 0 and not behind(t) and not (isinstance(t, int) and t < 2):
                        pe.wait_ge(added, 2 * (t - 1))
                    for k in range(half * KC // 2, (half + 1) * KC // 2):
                        a = slice(k * P, (k + 1) * P)
                        for q in range(2):
                            b = slice(q * D_G, (q + 1) * D_G)
                            out = pr_ps[slot][:, b]
                            pe.matmul(out, o_hi[:, a], w_hi[:, k, b], start=(k == 0), stop=False)
                            pe.matmul(out, o_hi[:, a], w_lo[:, k, b], start=False, stop=False)
                            mm = pe.matmul(out, o_lo[:, a], w_hi[:, k, b], start=False, stop=(k == KC - 1))
                    mm.then_inc(product, 1)
                    if half == 0 and has:
                        turn_o(t + 1, 1 - slot, prompt)
                if not behind(t):
                    turn_h(t - 1)

            turn_o(0, 0)
            steps(pe, body)
            turn_h(tiles - 1)


def mlp(nc, c, dram, g, first, tiles, h_hi, h_lo, x1):
    tokens = min(tiles * P, (TILES - first) * P + N_SAMPLE)
    NCH = -(-tokens // 512)
    per = -(-tiles // NCH)
    chunks = [(t, min(per, tiles - t), t * P, min(per * P, tokens - t * P)) for t in range(0, tiles, per)]
    FB = FBLK // P
    BLOCKS = D_FF // FBLK
    HALF = KC // 2
    PIECES = 4
    with Phase(nc, f"mlp{g}") as ph:
        w_raw = ph.sb("w_raw", [P, 2, 1024])
        w_hi = ph.sb("w_hi", [P, 2, PIECES, 1024], F32R)
        w_lo = ph.sb("w_lo", [P, 2, PIECES, 1024], F32R)
        r = ph.sb("r", [P, FB, 512])
        u = ph.sb("u", [P, FB, 512])
        u_hi = ph.sb("u_hi", [P, 2, FB, 512], F32R)
        u_lo = ph.sb("u_lo", [P, 2, FB, 512], F32R)
        u_ps = [ph.ps(f"u{j}", [P, FB, 512]) for j in range(2)]
        y_ps = [ph.ps(f"y{j}", [P, D_MODEL]) for j in range(2)]
        w_loaded = ph.sems("w_loaded")
        w_hi_done = ph.sem("w_hi_done")
        w_split = ph.sem("w_split")
        up_done = ph.sem("up_done")
        relu_done = ph.sem("relu_done")
        sq_done = ph.sem("sq_done")
        u_hi_done = ph.sem("u_hi_done")
        u_lo_done = ph.sem("u_lo_done")
        y_done = ph.sem("y_done")
        y_added = ph.sem("y_added")
        out_sent = ph.sem("out_sent")
        block = ph.block()

        def blocks(eng, body):
            with eng.Fori(0, BLOCKS // 2 - 1) as i:
                body(2 * i, 0, True)
                body(2 * i + 1, 1, True)
            body(BLOCKS - 2, 0, True)
            body(BLOCKS - 1, 1, False)

        def next_step(b, par, ch):
            if ch + 1 < NCH:
                return par, ch + 1, NCH * b + ch + 1
            return 1 - par, 0, NCH * b + ch + 1

        def u_slot(par, ch):
            return (NCH * par + ch) % 2

        @block.sync
        def _(sp):
            def load(b, q):
                if q < 2:
                    src = dram["w_up"][q * HALF * P:(q + 1) * HALF * P, ds(b * FBLK, FBLK)]\
                        .rearrange("(k p) f -> p k f", p=P)
                    dst = w_raw[:, q % 2, :].rearrange("p (k f) -> p k f", f=FBLK)
                else:
                    src = dram["w_down"][ds(b * FBLK + (q - 2) * P, P), :]
                    dst = w_raw[:, q % 2, :]
                sp.dma_start(dst, src).then_inc(w_loaded[q % 2], 16)

            for q in range(PIECES):
                if q >= 2:
                    sp.wait_ge(w_split, q - 1)
                load(0, q)
            with sp.Fori(0, BLOCKS - 1) as i:
                for q in range(PIECES):
                    sp.wait_ge(w_split, PIECES * (i + 1) + q - 1)
                    load(i + 1, q)
            for t in range(tiles):
                sp.wait_ge(y_added, 2 * (tiles * (BLOCKS - 1) + t + 1))
                sp.dma_start(dram["y"][(first + t) * P:(first + t + 1) * P, :], x1[:, t, :]).then_inc(out_sent, 16)
            sp.wait_ge(out_sent, 16 * tiles)

        @block.scalar
        def _(act):
            def hi_w(b, par):
                for q in range(PIECES):
                    act.wait_ge(w_loaded[q % 2], 16 * (2 * b + q // 2 + 1))
                    act.activation(w_hi[:, par, q, :], w_raw[:, q % 2, :], ACT.Copy).then_inc(w_hi_done, 1)

            def relu(s, par, ch):
                n = chunks[ch][3]
                act.wait_ge(up_done, s + 1)
                if not (isinstance(s, int) and s == 0):
                    act.wait_ge(sq_done, s)
                act.activation(r[:, :, 0:n], u_ps[u_slot(par, ch)][:, :, 0:n], ACT.Relu).then_inc(relu_done, 1)
                act.wait_ge(sq_done, s + 1)
                if not (isinstance(s, int) and s < 2):
                    act.wait_ge(y_done, tile_count(s, par, ch))
                act.activation(u_hi[:, u_slot(par, ch), :, 0:n], u[:, :, 0:n], ACT.Copy).then_inc(u_hi_done, 1)

            def body(b, par, more):
                for ch in range(NCH):
                    if ch == 0 and more:
                        act.wait_ge(y_done, tiles_before(b))
                        hi_w(b + 1, 1 - par)
                    if more or ch + 1 < NCH:
                        np_, nch, s = next_step(b, par, ch)
                        cur[0] = b
                        relu(s, np_, nch)

            cur = [0]

            def tiles_before(b):
                return tiles * b

            def tile_count(s, par, ch):
                b = cur[0]
                k = ch - 2
                nb = b if ch else b + 1
                while k < 0:
                    k += NCH
                    nb = nb - 1
                return tiles * nb + sum(x[1] for x in chunks[:k + 1])

            hi_w(0, 0)
            relu(0, 0, 0)
            cur[0] = 0

            def first_body():
                hi_w(1, 1)
                for ch in range(NCH):
                    np_, nch, s = next_step(0, 0, ch)
                    relu(s, np_, nch)

            first_body()
            body(1, 1, True)
            with act.Fori(1, BLOCKS // 2 - 1) as i:
                body(2 * i, 0, True)
                body(2 * i + 1, 1, True)
            body(BLOCKS - 2, 0, True)
            body(BLOCKS - 1, 1, False)

        @block.gpsimd
        def _(pool):
            def square(s, ch):
                n = chunks[ch][3]
                pool.wait_ge(relu_done, s + 1)
                if not (isinstance(s, int) and s == 0):
                    pool.wait_ge(u_lo_done, s)
                pool.tensor_tensor(u[:, :, 0:n], r[:, :, 0:n], r[:, :, 0:n], ALU.mult).then_inc(sq_done, 1)

            def body(b, par, more):
                for ch in range(NCH):
                    if more or ch + 1 < NCH:
                        _par, nch, s = next_step(b, par, ch)
                        square(s, nch)

            square(0, 0)
            blocks(pool, body)

        @block.vector
        def _(dve):
            def lo_w(b, par):
                for q in range(PIECES):
                    dve.wait_ge(w_hi_done, PIECES * b + q + 1)
                    dve.tensor_tensor(w_lo[:, par, q, :], w_raw[:, q % 2, :], w_hi[:, par, q, :].bitcast(F32),
                                      ALU.subtract).then_inc(w_split, 1)

            def lo_u(s, par, ch):
                n = chunks[ch][3]
                slot = u_slot(par, ch)
                dve.wait_ge(u_hi_done, s + 1)
                dve.tensor_tensor(u_lo[:, slot, :, 0:n], u[:, :, 0:n], u_hi[:, slot, :, 0:n].bitcast(F32),
                                  ALU.subtract).then_inc(u_lo_done, 1)

            def body(b, par, more):
                for ch, (t0, nt, _c0, n) in enumerate(chunks):
                    if ch == 0 and more:
                        lo_w(b + 1, 1 - par)
                    for m in range(nt):
                        if m == 2 and (more or ch + 1 < NCH):
                            np_, nch, s = next_step(b, par, ch)
                            lo_u(s, np_, nch)
                        t = t0 + m
                        rows = min(n - m * P, P)
                        dve.wait_ge(y_done, tiles * b + t + 1)
                        for q in range(2):
                            part = x1[0:rows, t, q * D_G:(q + 1) * D_G]
                            dve.tensor_tensor(part, y_ps[(tiles * par + t) % 2][0:rows, q * D_G:(q + 1) * D_G], part,
                                              ALU.add).then_inc(y_added, 1)

            lo_w(0, 0)
            lo_u(0, 0, 0)
            blocks(dve, body)

        @block.tensor
        def _(pe):
            def up(s, par, ch):
                _t0, _nt, c0, n = chunks[ch]
                slot = u_slot(par, ch)
                if not (isinstance(s, int) and s < 2):
                    pe.wait_ge(relu_done, s - 1)
                for f in range(FB):
                    for k in range(KC):
                        a = slice((k % HALF) * FBLK + f * P, (k % HALF) * FBLK + (f + 1) * P)
                        out = u_ps[slot][:, f, 0:n]
                        hi, lo = w_hi[:, par, k // HALF, a], w_lo[:, par, k // HALF, a]
                        pe.matmul(out, hi, h_hi[:, k, c0:c0 + n], start=(k == 0), stop=False)
                        pe.matmul(out, hi, h_lo[:, k, c0:c0 + n], start=False, stop=False)
                        mm = pe.matmul(out, lo, h_hi[:, k, c0:c0 + n], start=False, stop=(k == KC - 1))
                mm.then_inc(up_done, 1)

            def down(b, par, ch, first_tiles):
                t0, nt, _c0, n = chunks[ch]
                slot = u_slot(par, ch)
                pe.wait_ge(u_lo_done, NCH * b + ch + 1)
                for m in range(nt):
                    t = t0 + m
                    rows = min(n - m * P, P)
                    out_ps = y_ps[(tiles * par + t) % 2]
                    if not (first_tiles and t < 2):
                        pe.wait_ge(y_added, 2 * (tiles * b + t - 1))
                    for q in range(2):
                        out = out_ps[0:rows, q * D_G:(q + 1) * D_G]
                        b_ = slice(q * D_G, (q + 1) * D_G)
                        for f in range(FB):
                            a = slice(m * P, m * P + rows)
                            hi, lo = u_hi[:, slot, f, a], u_lo[:, slot, f, a]
                            pe.matmul(out, hi, w_hi[:, par, 2 + f, b_], start=(f == 0), stop=False)
                            pe.matmul(out, hi, w_lo[:, par, 2 + f, b_], start=False, stop=False)
                            mm = pe.matmul(out, lo, w_hi[:, par, 2 + f, b_], start=False, stop=(f == FB - 1))
                    mm.then_inc(y_done, 1)

            def body(b, par, more):
                for ch in range(NCH):
                    if more or ch + 1 < NCH:
                        np_, nch, s = next_step(b, par, ch)
                        if nch == 0:
                            pe.wait_ge(w_split, PIECES * (b + 2))
                        up(s, np_, nch)
                    down(b, par, ch, isinstance(b, int) and b == 0)

            pe.wait_ge(w_split, PIECES // 2)
            up(0, 0, 0)
            pe.wait_ge(w_split, PIECES)
            body(0, 0, True)
            body(1, 1, True)
            with pe.Fori(1, BLOCKS // 2 - 1) as i:
                body(2 * i, 0, True)
                body(2 * i + 1, 1, True)
            body(BLOCKS - 2, 0, True)
            body(BLOCKS - 1, 1, False)


def finish(nc, c, dram):
    for g, (first, tiles) in enumerate(((0, TILES // 2), (TILES // 2, TILES // 2 + 1))):
        with Phase(nc, f"fin{g}") as ph:
            tokens = min(tiles * P, TILES // 2 * P + N_SAMPLE)
            h_hi = ph.sb("h_hi", [P, KC, tokens], F32R)
            h_lo = ph.sb("h_lo", [P, KC, tokens], F32R)
            x1 = ph.sb("x1", [P, tiles, D_MODEL])
            join_heads(nc, c, dram, g, first, tiles, h_hi, h_lo, x1)
            mlp(nc, c, dram, g, first, tiles, h_hi, h_lo, x1)


def build(nc, dram, phases="ABCDWE"):
    with Phase(nc, "all") as ph:
        c = {"ident": ph.sb("ident", [P, P]), "mask": ph.sb("mask", [P, 2 * P]),
             "logf": ph.sb("logf", [P, N_TILES * HEADS])}
        load_constants(nc, c, dram)
        if "A" in phases:
            project(nc, c, dram)
        if "B" in phases:
            attend(nc, c, dram, False)
        if "C" in phases:
            attend(nc, c, dram, True)
        if "D" in phases:
            sample_attend(nc, c, dram, False)
            sample_attend(nc, c, dram, True)
        if "E" in phases:
            finish(nc, c, dram)


def shape_constants():
    i = np.arange(P)
    f = np.float32
    causal = np.where(i[None, :] <= i[:, None], f(0), f(NEG))
    window = np.where(i[None, :] >= i[:, None], f(0), f(NEG))
    half = 8
    inv = f(500000.0) ** (-np.arange(half, dtype=f) / f(half))
    pos = np.concatenate([np.arange(SEQ), PAST + np.tile(np.arange(DEC_SEQ), DEC_BATCH),
                          np.zeros(ROWS - SEQ - N_SAMPLE, int)]).astype(f)
    ang = (pos[:, None] * inv[None, :]).astype(f).astype(np.float64)
    cos, sin = np.cos(ang).astype(f), np.sin(ang).astype(f)
    row = np.arange(DEC_BATCH // 4 * HEADS * DEC_SEQ)
    q = row % DEC_SEQ
    m = np.arange(P)
    pos = [16 * m + r for r in range(8)]
    pos += [PAST - 512 + 16 * (m // 4) + 8 + 2 * (m % 4) + b for b in range(2)]
    pos = np.concatenate(pos + [PAST + np.arange(DEC_SEQ)])
    back = PAST + q[:, None] - pos[None, :]
    reach = sum(((back >= 0) & (back % d == 0) & (back <= w)).astype(f) for w, d in ((128, 1), (512, 4), (2048, 16)))
    return {
        "reach": reach,
        "unreached": np.where(reach > 0, f(0), f(NEG)),
        "own": (row[:, None] // DEC_SEQ % HEADS == np.arange(HEADS)[None, :]).astype(f),
        "causal_new": np.where(np.arange(DEC_SEQ)[None, :] <= q[:, None], f(0), f(NEG)),
        "after": (i[:, None] > i[None, :]).astype(f),
        "ident": np.eye(P, dtype=f),
        "mask": np.concatenate([window, causal], 1),
        "upto": (i[:, None] <= i[None, :]).astype(f),
        "rope_cos": np.concatenate([cos, cos], 1),
        "rope_sin": np.concatenate([-sin, sin], 1),
    }


def layout(inputs):
    a = {k: np.asarray(v) for k, v in inputs.items()}
    out = {
        "x": np.concatenate([a["x_prompt"].reshape(SEQ, D_MODEL), a["x_sample"].reshape(N_SAMPLE, D_MODEL),
                             np.zeros((ROWS - SEQ - N_SAMPLE, D_MODEL), np.float32)]),
        "g_attn": a["g_attn"][0].reshape(KC, P).T,
        "g_mlp": a["g_mlp"][0].reshape(KC, P).T,
        "cache_k": a["cache_k"][0].reshape(-1, PAGE, D_G),
        "cache_v": a["cache_v"][0].reshape(-1, PAGE, D_G),
        "cache_logf": a["cache_logf"][0],
        "win_k": a["state_win_k"][0].reshape(DEC_BATCH, PAST, D_G),
        "win_v": a["state_win_v"][0].reshape(DEC_BATCH, PAST, D_G),
        "page_table": a["page_table"].reshape(1, -1).astype(np.int32),
    }
    for name in ("w_in", "b_f", "g_qa", "g_ka", "g_qb", "g_kb", "w_o", "w_up", "w_down"):
        out[name] = a[name][0]
    out.update(shape_constants())
    return {k: np.ascontiguousarray(v) for k, v in out.items()}


OUTS = {
    "y": (ROWS, D_MODEL),
    "k_a": (ROWS, D_G), "v_a": (ROWS, D_G), "logf": (ROWS, HEADS), "k_b": (ROWS, D_G), "v_b": (ROWS, D_G),
    "new_win_k": (DEC_BATCH, PAST, D_G), "new_win_v": (DEC_BATCH, PAST, D_G),
}
SCRATCH = {"q_a": (ROWS, D_G), "q_b": (ROWS, D_G), "att": (ROWS, D_MODEL),
           "dil": (3, SEQ, HEADS * (HD + 2)), "x1": (ROWS, D_MODEL),
           "lf_pages": (DEC_BATCH * PAST // PAGE, PAGE * HEADS)}


def kernel(**inputs):
    import concourse.bacc as bacc
    from concourse.bass_utils import run_bass_kernel_spmd

    nc = bacc.Bacc("TRN2", target_bir_lowering=False, num_devices=1)
    arrays = layout(inputs)
    dram = {n: nc.dram_tensor(f"in_{n}", v.shape, mybir.dt.from_np(v.dtype), kind="ExternalInput").ap()
            for n, v in arrays.items()}
    for n, shape in OUTS.items():
        dram[n] = nc.dram_tensor(f"out_{n}", shape, F32, kind="ExternalOutput").ap()
    for n, shape in SCRATCH.items():
        dram[n] = nc.dram_tensor(f"scratch_{n}", shape, F32).ap()
    build(nc, dram)
    r = run_bass_kernel_spmd(nc, [{f"in_{n}": v for n, v in arrays.items()}], core_ids=[0])
    got = {n: np.asarray(r.results[0][f"out_{n}"]) for n in OUTS}

    def prompt(name, *shape):
        return got[name][:SEQ].reshape(shape)

    def sampled(name, *shape):
        return got[name][SEQ:SEQ + N_SAMPLE].reshape(shape)

    sp = (1, 1, SEQ, HEADS, HD)
    ss = (1, DEC_BATCH, DEC_SEQ, HEADS, HD)
    sw = (1, DEC_BATCH, PAST, HEADS, HD)
    return (prompt("y", 1, SEQ, D_MODEL), sampled("y", DEC_BATCH, DEC_SEQ, D_MODEL),
            prompt("k_a", *sp), prompt("v_a", *sp), prompt("logf", *sp[:4]), prompt("k_b", *sp), prompt("v_b", *sp),
            sampled("k_a", *ss), sampled("v_a", *ss), sampled("logf", *ss[:4]),
            got["new_win_k"].reshape(sw), got["new_win_v"].reshape(sw))
```
